# Optimizing a Trainium2 kernel written in Bass

```python
import math
import jax, jax.numpy as jnp
from jax import lax
import numpy as np

D_MODEL = 1024
BATCH = 1
SEQ = 256
DEPTH = 1

N_META = 16
CONV_CH = D_MODEL
CONV_WIDTH = 31
RET_HEADS = 4
RET_DK = 256
RET_DV = 512
RET_CHUNK = 128
ROPE_BASE = 10000.0
COLS_CONV = 2 * CONV_CH
COLS_Q = RET_HEADS * RET_DK
COLS_K = RET_HEADS * RET_DK
COLS_V = RET_HEADS * RET_DV
COLS_G = RET_HEADS * RET_DV
COLS_GATE = 2 * D_MODEL
PROJ_COLS = COLS_CONV + COLS_Q + COLS_K + COLS_V + COLS_G + COLS_GATE
N_EXPERTS = 32
TOP_K = 4
D_EXPERT = D_MODEL
SWIGLU_LIMIT = 7.0
SWIGLU_ALPHA = 1.702
EXPERT_BLOCK = 128
EPS = 1e-5

kernel_name = "hybrid_conv_retention_moe_block"

def rmsnorm(x, w):
    x32 = x.astype(jnp.float32)
    y = x32 * lax.rsqrt(jnp.mean(x32 * x32, axis=-1, keepdims=True) + EPS)
    return (y * w.astype(jnp.float32)).astype(x.dtype)

def layernorm(x, w, b):
    x32 = x.astype(jnp.float32)
    mu = jnp.mean(x32, axis=-1, keepdims=True)
    xc = x32 - mu
    y = xc * lax.rsqrt(jnp.mean(xc * xc, axis=-1, keepdims=True) + EPS)
    return (y * w.astype(jnp.float32) + b.astype(jnp.float32)).astype(x.dtype)

def rotary(x, positions):
    d = x.shape[-1]
    inv_freq = ROPE_BASE ** (-jnp.arange(0, d, 2, dtype=jnp.float32) / d)
    ang = positions.astype(jnp.float32)[:, None] * inv_freq[None, :]
    cos = jnp.cos(ang)[None, :, None, :]
    sin = jnp.sin(ang)[None, :, None, :]
    x32 = x.astype(jnp.float32)
    x1, x2 = x32[..., : d // 2], x32[..., d // 2:]
    return jnp.concatenate([x1 * cos - x2 * sin, x2 * cos + x1 * sin], axis=-1)

def causal_depthwise_conv(u, w, b):
    out = lax.conv_general_dilated(
        u, w[:, None, :].astype(u.dtype), window_strides=(1,),
        padding=[(CONV_WIDTH - 1, 0)],
        dimension_numbers=("NWC", "WIO", "NWC"),
        feature_group_count=u.shape[-1])
    return out + b

def chunkwise_retention(q, k, v):
    Bsz, L, H, _ = q.shape
    C = RET_CHUNK
    pad = C - N_META
    padf = lambda t: jnp.pad(t.astype(jnp.float32), ((0, 0), (pad, 0), (0, 0), (0, 0)))
    q, k, v = padf(q), padf(k), padf(v)
    Lp = L + pad
    nC = Lp // C
    q = q.reshape(Bsz, nC, C, H, RET_DK)
    k = k.reshape(Bsz, nC, C, H, RET_DK)
    v = v.reshape(Bsz, nC, C, H, RET_DV)

    log_gamma = jnp.log1p(-jnp.exp2(-5.0 - jnp.arange(H, dtype=jnp.float32)))
    idx = jnp.arange(C, dtype=jnp.float32)
    diff = idx[:, None] - idx[None, :]
    decay_in = jnp.where(diff[None] >= 0,
                         jnp.exp(log_gamma[:, None, None] * jnp.maximum(diff, 0.0)[None]), 0.0)
    zeta = jnp.exp(log_gamma[None, :] * (C - 1 - idx)[:, None])
    xi = jnp.exp(log_gamma[None, :] * (idx + 1.0)[:, None])
    chunk_decay = jnp.exp(log_gamma * C)

    scores = jnp.einsum("bnihd,bnjhd->bnhij", q, k) * decay_in[None, None]
    inner = jnp.einsum("bnhij,bnjhe->bnihe", scores, v)

    kz = k * zeta[None, None, :, :, None]
    def step(R, inp):
        qc, kc, vc = inp
        cross = jnp.einsum("bihd,bhde->bihe", qc, R)
        R = R * chunk_decay[None, :, None, None] + jnp.einsum("bjhd,bjhe->bhde", kc, vc)
        return R, cross
    R0 = jnp.zeros((Bsz, H, RET_DK, RET_DV), jnp.float32)
    _, cross = lax.scan(step, R0, (q.transpose(1, 0, 2, 3, 4),
                                   kz.transpose(1, 0, 2, 3, 4),
                                   v.transpose(1, 0, 2, 3, 4)))
    cross = cross.transpose(1, 0, 2, 3, 4) * xi[None, None, :, :, None]
    y = (inner + cross).reshape(Bsz, Lp, H, RET_DV)
    return y[:, pad:]

def token_mixer(h, w_in, dw_w, dw_b, ln_w, ln_b, w_conv_out, b_conv_out, gn_w, w_ret_out, w_mix_out):
    Bsz, L, _ = h.shape
    z = h @ w_in
    splits = np.cumsum([COLS_CONV, COLS_Q, COLS_K, COLS_V, COLS_G]).tolist()
    z_conv, z_q, z_k, z_v, z_g, z_gate = jnp.split(z, splits, axis=-1)

    a, b = jnp.split(z_conv, 2, axis=-1)
    u = a * jax.nn.sigmoid(b)
    u = causal_depthwise_conv(u, dw_w, dw_b)
    u = jax.nn.silu(layernorm(u, ln_w, ln_b))
    y_conv = u @ w_conv_out + b_conv_out

    pos = jnp.arange(L)
    q = rotary(z_q.reshape(Bsz, L, RET_HEADS, RET_DK), pos) * (RET_DK ** -0.5)
    k = rotary(z_k.reshape(Bsz, L, RET_HEADS, RET_DK), pos)
    v = z_v.reshape(Bsz, L, RET_HEADS, RET_DV)
    y = chunkwise_retention(q, k, v)
    mu = jnp.mean(y, axis=-1, keepdims=True)
    yc = y - mu
    y = yc * lax.rsqrt(jnp.mean(yc * yc, axis=-1, keepdims=True) + EPS)
    y = y.reshape(Bsz, L, RET_HEADS * RET_DV) * gn_w.astype(jnp.float32)
    y_ret = (jax.nn.silu(z_g.astype(jnp.float32)) * y).astype(h.dtype) @ w_ret_out

    g_a, g_b = jnp.split(z_gate, 2, axis=-1)
    merged = jax.nn.sigmoid(g_a) * y_conv + jax.nn.sigmoid(g_b) * y_ret
    return merged @ w_mix_out

def moe_ffn(xn, w_router, b_router, w_gate_up, b_gate_up, w_down, b_down):
    Bsz, L, D = xn.shape
    T = Bsz * L
    xt = xn.reshape(T, D)
    logits = (xt @ w_router + b_router).astype(jnp.float32)
    top_v, top_i = lax.top_k(logits, TOP_K)
    gates = jax.nn.softmax(top_v, axis=-1)

    A = T * TOP_K
    e_flat = top_i.reshape(A)
    tok_flat = jnp.arange(A, dtype=jnp.int32) // TOP_K
    w_flat = gates.reshape(A)
    order = jnp.argsort(e_flat)
    e_sorted = e_flat[order]
    counts = jnp.bincount(e_flat, length=N_EXPERTS)
    starts = jnp.cumsum(counts) - counts
    pcounts = (counts + EXPERT_BLOCK - 1) // EXPERT_BLOCK * EXPERT_BLOCK
    pends = jnp.cumsum(pcounts)
    pstarts = pends - pcounts
    dest = pstarts[e_sorted] + (jnp.arange(A) - starts[e_sorted])
    n_blocks = -(-A // EXPERT_BLOCK) + N_EXPERTS
    P = n_blocks * EXPERT_BLOCK
    row_tok = jnp.full((P,), T, jnp.int32).at[dest].set(tok_flat[order])
    row_w = jnp.zeros((P,), jnp.float32).at[dest].set(w_flat[order])
    block_e = jnp.minimum(jnp.searchsorted(pends, jnp.arange(n_blocks) * EXPERT_BLOCK, side="right"),
                          N_EXPERTS - 1)
    x_pad = jnp.concatenate([xt, jnp.zeros((1, D), xt.dtype)], axis=0)
    xs = x_pad[row_tok].reshape(n_blocks, EXPERT_BLOCK, D)

    def expert_block(args):
        xb, e = args
        hgu = xb @ w_gate_up[e] + b_gate_up[e]
        h_gate, h_up = jnp.split(hgu, 2, axis=-1)
        h_gate = jnp.minimum(h_gate, SWIGLU_LIMIT)
        h_up = jnp.clip(h_up, -SWIGLU_LIMIT, SWIGLU_LIMIT)
        act = h_gate * jax.nn.sigmoid(SWIGLU_ALPHA * h_gate) * (h_up + 1.0)
        return act @ w_down[e] + b_down[e]

    ys = lax.map(expert_block, (xs, block_e)).reshape(P, D)
    out = jax.ops.segment_sum(ys * row_w[:, None], row_tok, num_segments=T + 1)[:T]
    return out.reshape(Bsz, L, D).astype(xn.dtype)

def setup_inputs(seed: int = 0) -> dict:
    key = jax.random.key(seed)
    ks = jax.random.split(key, 24)
    f32 = jnp.float32
    nrm = lambda k, shape, scale: jax.random.normal(k, shape, f32) * scale
    gain = lambda k, shape: 1.0 + 0.02 * jax.random.normal(k, shape, f32)
    return {
        "x": jax.random.normal(ks[0], (BATCH, SEQ, D_MODEL), f32),
        "meta_tokens": nrm(ks[1], (N_META, D_MODEL), 1.0),
        "norm_mix_w": gain(ks[2], (DEPTH, D_MODEL)),
        "w_in": nrm(ks[3], (DEPTH, D_MODEL, PROJ_COLS), D_MODEL ** -0.5),
        "conv_dw_w": nrm(ks[4], (DEPTH, CONV_WIDTH, CONV_CH), CONV_WIDTH ** -0.5),
        "conv_dw_b": nrm(ks[5], (DEPTH, CONV_CH), 0.02),
        "conv_ln_w": gain(ks[6], (DEPTH, CONV_CH)),
        "conv_ln_b": nrm(ks[7], (DEPTH, CONV_CH), 0.02),
        "w_conv_out": nrm(ks[8], (DEPTH, CONV_CH, D_MODEL), CONV_CH ** -0.5),
        "b_conv_out": nrm(ks[9], (DEPTH, D_MODEL), 0.02),
        "ret_gn_w": gain(ks[10], (DEPTH, RET_HEADS * RET_DV)),
        "w_ret_out": nrm(ks[11], (DEPTH, RET_HEADS * RET_DV, D_MODEL), (RET_HEADS * RET_DV) ** -0.5),
        "w_mix_out": nrm(ks[12], (DEPTH, D_MODEL, D_MODEL), D_MODEL ** -0.5),
        "norm_ffn_w": gain(ks[13], (DEPTH, D_MODEL)),
        "w_router": nrm(ks[14], (DEPTH, D_MODEL, N_EXPERTS), D_MODEL ** -0.5),
        "b_router": nrm(ks[15], (DEPTH, N_EXPERTS), 0.01),
        "w_gate_up": nrm(ks[16], (DEPTH, N_EXPERTS, D_MODEL, 2 * D_EXPERT), D_MODEL ** -0.5),
        "b_gate_up": nrm(ks[17], (DEPTH, N_EXPERTS, 2 * D_EXPERT), 0.02),
        "w_down": nrm(ks[18], (DEPTH, N_EXPERTS, D_EXPERT, D_MODEL), D_EXPERT ** -0.5),
        "b_down": nrm(ks[19], (DEPTH, N_EXPERTS, D_MODEL), 0.02),
        "norm_final_w": gain(ks[20], (D_MODEL,)),
    }

def reference(x, meta_tokens, norm_mix_w, w_in, conv_dw_w, conv_dw_b, conv_ln_w, conv_ln_b,
              w_conv_out, b_conv_out, ret_gn_w, w_ret_out, w_mix_out, norm_ffn_w,
              w_router, b_router, w_gate_up, b_gate_up, w_down, b_down, norm_final_w):
    Bsz = x.shape[0]
    meta = jnp.broadcast_to(meta_tokens[None].astype(x.dtype), (Bsz, N_META, x.shape[-1]))
    h = jnp.concatenate([meta, x], axis=1)
    for layer in range(DEPTH):
        h = h + token_mixer(rmsnorm(h, norm_mix_w[layer]), w_in[layer], conv_dw_w[layer],
                            conv_dw_b[layer], conv_ln_w[layer], conv_ln_b[layer],
                            w_conv_out[layer], b_conv_out[layer], ret_gn_w[layer],
                            w_ret_out[layer], w_mix_out[layer])
        h = h + moe_ffn(rmsnorm(h, norm_ffn_w[layer]), w_router[layer], b_router[layer],
                        w_gate_up[layer], b_gate_up[layer], w_down[layer], b_down[layer])
    out = rmsnorm(h, norm_final_w)
    return out[:, N_META:]


_drawn_inputs = setup_inputs


def setup_inputs(seed=0):
    import zlib

    import numpy as np

    out = dict(_drawn_inputs(seed))
    spreads = {}
    factors = {'b_gate_up': 5.497, 'b_down': 6.367, 'norm_final_w': 2.958}
    for name, (base, spread) in spreads.items():
        noise = np.random.default_rng([zlib.crc32(name.encode()), seed]).standard_normal(out[name].shape)
        drawn = base * np.exp(spread * noise) if base else spread * noise
        out[name] = __import__('jax').numpy.asarray(drawn.astype(out[name].dtype))
    for name, factor in factors.items():
        out[name] = (out[name] * factor).astype(out[name].dtype)
    return out
```

```python
from contextlib import ExitStack

import concourse.bass as bass
from concourse import mybir

F32 = mybir.dt.float32
I32 = mybir.dt.int32
U32 = mybir.dt.uint32
R32 = mybir.dt.float32r
BF16 = mybir.dt.bfloat16
ALU = mybir.AluOpType
ACT = mybir.ActivationFunctionType
AX_X = mybir.AxisListType.X

P = 128
D = 1024
KC = D // P
META = 16
REAL = 256
TT = REAL // P
TALL = META + REAL
TAPS = 31
PADL = TAPS - 1 - META
HEADS = 4
DK = 256
DV = 512
VC = DV // P
UNIT = 256
NE = 32
TOPK = 4
SLOTS = 64
MAXB = 48
STEPS = D // UNIT
HALVES = 6
HW = KC * UNIT // 2
HS = 4
PARTS = 3
EPS = 1e-5
LIMIT = 7.0
ALPHA = 1.702

TAP0, LNW, LNB, BCO, GNW = 0, 256, 264, 272, 280
NPAR = 296


class Chain:

    def __init__(self, eng, sem):
        self.eng, self.sem, self.base, self.n = eng, sem, 0, 0

    def did(self, ins):
        ins.then_inc(self.sem, 1)
        self.n += 1

    def wait(self, back=0):
        self.eng.wait_ge(self.sem, self.base + (self.n - back))

    def enter(self, i, per):
        self.start, self.per = self.base + self.n, per
        self.base, self.n = i * per + self.start, 0

    def leave(self, trips):
        assert self.n == self.per, (self.n, self.per)
        self.base, self.n = self.start + trips * self.per, 0


def build_block(nc, a, out):
    with ExitStack() as ctx:
        def sb(name, shape, dt=F32):
            return ctx.enter_context(nc.sbuf_tensor(name, shape, dt))

        def sem(name):
            return ctx.enter_context(nc.semaphore(name))

        pb = ctx.enter_context(nc.psum_tensor("pb", [P, 8, 512], F32))

        ring = sb("ring", [P, 6, KC, UNIT])
        xnT = sb("xnT", [P, KC, TALL])
        hx = sb("hx", [P, TT, D])
        cv = sb("cv", [P, KC, REAL])
        rT = sb("rT", [P, 4 * VC + VC, REAL])
        yret = sb("yret", [P, KC, REAL])
        scratch = sb("scratch", [P, 11840])
        whi = sb("whi", [P, HS, HW], R32)
        wlo = sb("wlo", [P, HS, HW], R32)
        xhi, xlo = (sb(n, [P, KC, SLOTS], R32) for n in ("xhi", "xlo"))
        ahi, alo = (sb(n, [P, 2, SLOTS], R32) for n in ("ahi", "alo"))
        yhi, ylo = (sb(n, [SLOTS, D], R32) for n in ("yhi", "ylo"))
        ghi, glo = (sb(n, [SLOTS, REAL], R32) for n in ("ghi", "glo"))
        bias3 = sb("bias3", [P, 3 * D], BF16)
        pick_e = sb("pick_e", [P, SLOTS], BF16)
        eid = sb("eid", [P, SLOTS])
        par = sb("par", [P, NPAR])
        ident = sb("ident", [P, P])
        ones = sb("ones", [P, P])
        before = sb("before", [P, P])
        iota_s = sb("iota_s", [P, SLOTS])
        iota_e = sb("iota_e", [P, NE])
        iota_b = sb("iota_b", [P, MAXB])
        mhalf = sb("mhalf", [P, 1])
        epsc = sb("epsc", [P, 1])
        stat = sb("stat", [P, 24])
        wt = sb("wt", [P, 32, 2])
        topi = sb("topi", [P, TT, 8], U32)
        onehot = sb("onehot", [P, TT, SLOTS], BF16)
        table = sb("table", [1, MAXB + 1], I32)
        nblocks = sb("nblocks", [1, 2], I32)
        tabf = sb("tabf", [P, MAXB])
        bst = sb("bst", [P, TT, 6])
        bmv = sb("bmv", [P, TT, 4])

        flat = scratch[:, :]
        at = [0]

        def tmp(*shape):
            n = 1
            for s in shape:
                n *= s
            v = flat[:, at[0]:at[0] + n]
            at[0] += n
            assert at[0] <= 11840
            if len(shape) == 2:
                v = v.rearrange("p (a b) -> p a b", a=shape[0])
            return v

        decay = tmp(HEADS, TALL)
        cos = tmp(TALL)
        sin = tmp(TALL)
        early = at[0]
        qraw, kraw = tmp(2, REAL), tmp(2, TALL)
        qrot, krot = tmp(2, REAL), tmp(2, TALL)
        rc, rs = tmp(2, TALL), tmp(2, TALL)
        vT = tmp(VC, TALL)
        vsb = tmp(2, DV)
        vM = tmp(DV)
        sA, sB, sM = tmp(REAL), tmp(P), tmp(REAL)
        at[0] = max(at[0], early + 6 * D + 384)
        yn = tmp(TT, DV)
        sg = tmp(VC, REAL)
        upad = tmp(2, PADL + TALL)
        cacc = tmp(2, REAL)
        sigb = tmp(2, TALL)
        dflat = flat[:, early:]
        hm = dflat[:, 0:D]
        xn = dflat[:, D:4 * D].rearrange("p (a b) -> p a b", a=3)
        wmb = dflat[:, 4 * D:5 * D]
        prow = dflat[:, 5 * D:5 * D + 384].rearrange("p (a b) -> p a b", a=3)
        junk1 = dflat[:, 5 * D + 384:6 * D + 384]
        sq = flat[:, 0:KC * REAL].rearrange("p (a b) -> p a b", a=KC)

        sga = rT[:, 0:KC, :]
        sgb = rT[:, KC:2 * KC, :]
        rflat = rT[:, :, :].rearrange("p a b -> p (a b)")
        lnv, sigma = rflat[:, 4096:4096 + REAL], rflat[:, 4096 + REAL:4096 + 2 * REAL]
        brows = rflat[0:3 * NE, 0:3 * D]
        gatehot = flat[:, 0:TT * SLOTS].rearrange("p (a b) -> p a b", a=TT)
        hg = flat[0:SLOTS, 256:256 + UNIT]
        hu = flat[0:SLOTS, 512:512 + UNIT]
        sig = flat[0:SLOTS, 768:768 + UNIT]
        act = flat[0:SLOTS, 1024:1024 + UNIT]
        pick = flat[:, 2048:3072]
        at[0] = 3072
        wr = tmp(KC, NE)
        brb, nblk, pend = tmp(NE), tmp(NE), tmp(NE)
        lg, mask, gdense, slot = (tmp(TT, NE) for _ in range(4))
        top, topf, gate4 = tmp(TT, 8), tmp(TT, TOPK), tmp(TT, TOPK)
        assert at[0] <= 4096
        xres = flat[:, 4096:4096 + TT * D].rearrange("p (a b) -> p a b", a=TT)
        x3 = flat[:, 8192:8192 + PARTS * TT * D // 2].bitcast(BF16).rearrange("p (q a b) -> p q a b", q=PARTS, a=TT)
        junk2 = rflat[:, 4096:5120]
        xn2 = yret[:, :, :].rearrange("p a b -> p (a b)").rearrange("p (a b) -> p a b", a=TT)
        xflat = xnT[:, :, :].rearrange("p a b -> p (a b)")[:, 0:KC * REAL]
        xn2T = xflat.rearrange("p (a b) -> p a b", a=KC)
        osb = xflat.rearrange("p (a b) -> p a b", a=TT)
        nwb = cv[:, :, :].rearrange("p a b -> p (a b)").rearrange("p (a b) -> p a b", a=2)

        x_in, meta_in, wmb_in = sem("x_in"), sem("meta_in"), sem("wmb_in")
        eid_in, par_in, bias_in, tab_in, rout_in, nwb_in = (sem(n) for n in ("eid_in", "par_in", "bias_in", "tab_in", "rout_in", "nwb_in"))
        landed = [sem(f"landed{s}") for s in range(6)]
        e_in = [sem(f"e_in{s}") for s in range(6)]
        consts = sem("consts")
        masked = sem("masked")
        cols = sem("cols")
        colse = sem("colse")
        a_full, b_full = sem("a_full"), sem("b_full")
        a_free, b_free = sem("a_free"), sem("b_free")
        sq_done, vr_done, pow_done, xn_done = (sem(n) for n in ("sq_done", "vr_done", "pow_done", "xn_done"))
        sig_done = sem("sig_done")
        conv_step = sem("conv_step")
        rope_done, pool_step = sem("rope_done"), sem("pool_step")
        vt_done, v_done = sem("vt_done"), sem("v_done")
        sc_done, s_done, y_done = sem("sc_done"), sem("s_done"), sem("y_done")
        gn_step, gv_done, gp_done, yn_done = sem("gn_step"), sem("gv_done"), sem("gp_done"), sem("yn_done")
        yt_done, rt_done = sem("yt_done"), sem("rt_done")
        xc_done, lsq_done, lnv_done, lnp_done, lnx_done, ln_done = (
            sem(n) for n in ("xc_done", "lsq_done", "lnv_done", "lnp_done", "lnx_done", "ln_done"))
        yr_done, sga_done, sgb_done, gb_done, vm_done, merged = (
            sem(n) for n in ("yr_done", "sga_done", "sgb_done", "gb_done", "vm_done", "merged"))
        h2_done, x2t, x2e, lgt, route = sem("h2_done"), sem("x2t"), sem("x2e"), sem("lgt"), sem("route")
        shift_done, wt_done, route_step = sem("shift_done"), sem("wt_done"), sem("route_step")
        exp_done, rank_done, table_done = sem("exp_done"), sem("rank_done"), sem("table_done")
        w_used = sem("w_used")
        hi_done = sem("hi_done")
        lo_v, lo_p = sem("lo_v"), sem("lo_p")
        lgt_read = sem("lgt_read")
        min_rdy, clip_rdy, sig_rdy, prod_rdy, act_rdy = (
            sem(n) for n in ("min_rdy", "clip_rdy", "sig_rdy", "prod_rdy", "act_rdy"))
        turned, ahi_rdy, alo_rdy = sem("turned"), sem("ahi_rdy"), sem("alo_rdy")
        yhi_rdy, ylo_rdy, ght_done, ghi_rdy, glo_rdy = (
            sem(n) for n in ("yhi_rdy", "ylo_rdy", "ght_done", "ghi_rdy", "glo_rdy"))
        hot_rdy, gathered, xhi_rdy, xlo_rdy = sem("hot_rdy"), sem("gathered"), sem("xhi_rdy"), sem("xlo_rdy")
        gh_rdy, sel_rdy, slot_step = sem("gh_rdy"), sem("sel_rdy"), sem("slot_step")
        zeroed, x3_rdy, xr_rdy, b3_step = sem("zeroed"), sem("x3_rdy"), sem("xr_rdy"), sem("b3_step")
        acc_done, fin, out_rdy, out_in = sem("acc_done"), sem("fin"), sem("out_rdy"), sem("out_in")

        w_in = a["w_in"][0].rearrange("(k p) n -> p k n", p=P)
        w_co = a["w_conv_out"][0].rearrange("(k p) n -> p k n", p=P)
        w_ro = a["w_ret_out"][0].rearrange("(k p) n -> p k n", p=P)
        w_mo = a["w_mix_out"][0].rearrange("(k p) n -> p k n", p=P)
        w_gu = a["w_gate_up"][0]
        w_dn = a["w_down"][0]


        def gate_src(e, q, up):
            c0 = (D if up else 0) + q * UNIT
            return w_gu[bass.ds(e, 1), :, c0:c0 + UNIT].rearrange("o (k p) n -> p (o k) n", p=P)

        def down_src(e, q):
            return w_dn[bass.ds(e, 1), q * UNIT:(q + 1) * UNIT, :].rearrange("o (k p) n -> p (o k) n", p=P)

        def lo_count(b, k):
            q, h = divmod(k, HALVES)
            return 16 * b + (4 * q + h + 1) if h < 4 else 8 * b + (2 * q + h - 3)

        UC = D // UNIT
        U_A, U_B = 0, UC
        U_Q, U_K, U_V, U_G, U_GA, U_GB = 2 * UC, 3 * UC, 4 * UC, 6 * UC, 8 * UC, 9 * UC

        def raw_half(k):
            return ring[:, k // 2 % 6, :, :].rearrange("p a b -> p (a b)")[:, k % 2 * HW:(k % 2 + 1) * HW]

        block = ctx.enter_context(nc.Block())


        @block.sync
        def _(sp):
            def load(s, src, u):
                cols_ = slice(u * UNIT, u * UNIT + UNIT) if isinstance(u, int) else bass.ds(u * UNIT, UNIT)
                sp.dma_start(ring[:, s, :, :], src[:, :, cols_]).then_inc(landed[s], 16)

            xr = a["x"][0].rearrange("(t p) n -> p t n", p=P)
            sp.dma_start(hm[0:META, :], a["meta_tokens"]).then_inc(meta_in, 16)
            sp.dma_start(hx[:, 0, :], xr[:, 0, :]).then_inc(x_in, 16)
            sp.dma_start(wmb, a["norm_mix_w"][0:1, :].to_broadcast([P, D])).then_inc(wmb_in, 16)
            sp.dma_start(hx[:, 1, :], xr[:, 1, :]).then_inc(x_in, 16)
            load(0, w_in, U_A)
            load(1, w_in, U_B)
            load(2, w_in, U_Q)
            load(3, w_in, U_K)
            load(4, w_in, U_V)
            load(5, w_in, U_V + 1)
            with sp.Fori(1, 4) as i:
                sp.wait_ge(a_full, 2 * i)
                load(0, w_in, i + U_A)
                sp.wait_ge(b_full, 2 * i)
                load(1, w_in, i + U_B)
            sp.wait_ge(a_full, 8)
            load(0, w_in, U_G)
            sp.wait_ge(b_full, 8)
            load(1, w_in, U_G + 1)
            with sp.Fori(1, HEADS) as h:
                sp.wait_ge(a_full, 6 * h + 4)
                load(2, w_in, h + U_Q)
                sp.wait_ge(b_full, 6 * h + 4)
                load(3, w_in, h + U_K)
                sp.wait_ge(a_full, 6 * h + 6)
                load(4, w_in, 2 * h + U_V)
                sp.wait_ge(b_full, 6 * h + 6)
                load(5, w_in, 2 * h + (U_V + 1))
                sp.wait_ge(a_full, 6 * h + 8)
                load(0, w_in, 2 * h + U_G)
                sp.wait_ge(b_full, 6 * h + 8)
                load(1, w_in, 2 * h + (U_G + 1))
            sp.wait_ge(a_full, 30)
            load(4, w_ro[:, 0:KC, :], 0)
            sp.wait_ge(b_full, 30)
            load(5, w_ro[:, KC:2 * KC, :], 0)
            sp.wait_ge(a_full, 28)
            load(2, w_in, U_GA)
            load(3, w_in, U_GB)
            with sp.Fori(1, UC) as r:
                sp.wait_ge(a_full, 2 * r + 32)
                load(4, w_ro[:, 0:KC, :], r)
                load(5, w_ro[:, KC:2 * KC, :], r)
            sp.wait_ge(a_full, 32)
            load(0, w_co, 0)
            sp.wait_ge(b_full, 32)
            load(1, w_co, 1)
            for g in range(UC):
                if g:
                    sp.wait_ge(a_full, 2 * (20 + g))
                    load(2, w_in, U_GA + g)
                    sp.wait_ge(b_full, 2 * (18 + g))
                    load(3, w_in, U_GB + g)
            sp.wait_ge(a_full, 48)
            sp.wait_ge(b_full, 44)
            for n in range(UC):
                load(2 + n, w_mo, n)
            sp.wait_ge(a_full, 50)
            load(0, w_co, 2)
            sp.wait_ge(b_full, 46)
            load(1, w_co, 3)
            sp.wait_ge(a_full, 52)
            sp.wait_ge(b_full, 48)
            sp.dma_start(wr, a["w_router"][0].rearrange("(k p) n -> p k n", p=P)).then_inc(rout_in, 16)
            sp.dma_start(brb, a["b_router"][0:1, :].to_broadcast([P, NE])).then_inc(rout_in, 16)
            sp.dma_start(nwb[:, 0, :], a["norm_ffn_w"][0:1, :].to_broadcast([P, D])).then_inc(nwb_in, 16)
            sp.dma_start(nwb[:, 1, :], a["norm_final_w"].rearrange("(o n) -> o n", o=1)[0:1, :]
                         .to_broadcast([P, D])).then_inc(nwb_in, 16)

            def unit(e_prev, e, j):
                q, kind = divmod(j, 3)
                dst = ring[:, j % 6, :, :]
                if kind == 2:
                    dst = dst.rearrange("p a b -> p (a b)").rearrange("p (a b) -> p a b", a=2)
                src = gate_src(e, q, kind) if kind < 2 else down_src(e if q else e_prev, q - 1 if q else STEPS - 1)
                sp.dma_start(dst, src).then_inc(e_in[j % 6], 16)

            def slot_free(b, j):
                sp.wait_ge(lo_p if j % 3 == 2 else lo_v, lo_count(b, 2 * (j - 6) + 1))

            for j in range(6):
                if j == 2:
                    sp.wait_ge(a_full, 54)
                    sp.wait_ge(b_full, 50)
                unit(0, 0, j)
            sp.wait_ge(table_done, 4)
            nb = sp.value_load(nblocks[0:1, 0:1], min_val=NE, max_val=MAXB - 1)
            before_last = sp.value_load(nblocks[0:1, 1:2], min_val=NE - 1, max_val=MAXB - 2)
            with sp.Fori(0, before_last) as b:
                e0 = sp.value_load(table[0:1, bass.ds(b + 1, 1)], min_val=0, max_val=NE - 1)
                e1 = sp.value_load(table[0:1, bass.ds(b + 2, 1)], min_val=0, max_val=NE - 1)
                for j in range(6, 18):
                    slot_free(b, j)
                    unit(e0, e0 if j < 12 else e1, j % 12)
            el = sp.value_load(table[0:1, bass.ds(nb, 1)], min_val=0, max_val=NE - 1)
            for j in range(6, 12):
                slot_free(before_last, j)
                unit(el, el, j)
            slot_free(before_last, 14)
            unit(el, el, 2)
            outr = out[0].rearrange("(t p) n -> p t n", p=P)
            for t in range(TT):
                sp.wait_ge(out_rdy, t + 1)
                sp.dma_start(outr[:, t, :], osb[:, t, :]).then_inc(out_in, 16)
            sp.wait_ge(out_in, 16 * TT)

        @block.gpsimd
        def _(pool):
            pool.memset(ident[:, :], 0.0).then_inc(consts, 1)
            pool.memset(ones[:, :], 1.0).then_inc(consts, 1)
            pool.memset(before[:, :], 1.0).then_inc(consts, 1)
            pool.memset(mhalf[:, :], -0.5).then_inc(consts, 1)
            pool.wait_ge(consts, 3)
            pool.affine_select(out=ident[:, :], in_=ident[:, :], compare_op=ALU.not_equal, fill=1.0,
                               base=0, pattern=[[-1, P]], channel_multiplier=1).then_inc(masked, 1)
            pool.affine_select(out=before[:, :], in_=before[:, :], compare_op=ALU.is_gt, fill=0.0,
                               base=0, pattern=[[1, P]], channel_multiplier=-1).then_inc(masked, 1)
            pool.iota(iota_s[:, :], [[1, SLOTS]], base=0, channel_multiplier=0,
                      allow_small_or_imprecise_dtypes=True).then_inc(consts, 1)
            pool.iota(iota_e[:, :], [[1, NE]], base=0, channel_multiplier=0,
                      allow_small_or_imprecise_dtypes=True).then_inc(consts, 1)
            pool.iota(iota_b[:, :], [[1, MAXB]], base=0, channel_multiplier=0,
                      allow_small_or_imprecise_dtypes=True).then_inc(consts, 1)
            pool.memset(upad[:, :, 0:PADL], 0.0).then_inc(consts, 1)
            pool.memset(sg[:, :, :], 0.0).then_inc(consts, 1)
            pool.memset(yn[:, :, :], 0.0).then_inc(yn_done, 1)
            pool.memset(stat[:, 18:20], 0.0).then_inc(rope_done, 1)

            def rsqrt(o, v, n):
                return pool.tensor_tensor(o, v, mhalf[0:v.shape[0], 0:1].to_broadcast([v.shape[0], n]), ALU.pow)

            pool.wait_ge(consts, 4)
            for t in range(3):
                rows = META if t == 2 else P
                pool.wait_ge(vr_done, t + 1)
                rsqrt(stat[0:rows, 6 + t:7 + t], stat[0:rows, 3 + t:4 + t], 1).then_inc(pow_done, 1)

            pool.wait_ge(bias_in, 16 * 6)
            b3 = Chain(pool, b3_step)

            def do(ins):
                b3.did(ins)
                b3.wait()

            last = slice(2 * NE, 3 * NE)
            do(pool.tensor_copy(bias3[0:3 * NE, :], brows))
            do(pool.tensor_tensor(brows, brows, bias3[0:3 * NE, :], ALU.subtract))
            do(pool.tensor_copy(bias3[NE:2 * NE, :], brows[NE:2 * NE, :]))
            do(pool.tensor_copy(bias3[last, :], brows[last, :]))
            do(pool.tensor_tensor(brows[last, :], brows[last, :], bias3[last, :], ALU.subtract))
            do(pool.tensor_copy(bias3[last, :], brows[last, :]))

            pool.wait_ge(tab_in, 48)
            step = Chain(pool, pool_step)
            with pool.Fori(0, HEADS) as h:
                step.enter(h, 6)
                for which, (raw, rot, n) in enumerate(((qraw, qrot, REAL), (kraw, krot, TALL))):
                    t0 = TALL - n
                    c_ = cos[:, t0:TALL].rearrange("p (o n) -> p o n", o=1).to_broadcast([P, 2, n])
                    pool.wait_ge((a_free, b_free)[which], 6 * h + 12)
                    if which:
                        step.wait()
                        pool.wait_ge(rope_done, 2 * h + 2)
                    else:
                        pool.wait_ge(rope_done, 2 * h + 1)
                    step.did(pool.tensor_tensor(rc[:, :, 0:n], raw[:, :, :], c_, ALU.mult))
                    step.did(pool.tensor_tensor(rs[:, 0, 0:n], raw[:, 1, :], sin[:, t0:TALL], ALU.mult))
                    step.did(pool.tensor_tensor(rs[:, 1, 0:n], raw[:, 0, :], sin[:, t0:TALL], ALU.mult))
                    step.wait()
                    pool.tensor_tensor(rot[:, 0, :], rc[:, 0, 0:n], rs[:, 0, 0:n], ALU.subtract)
                    pool.tensor_tensor(rot[:, 1, :], rc[:, 1, 0:n], rs[:, 1, 0:n], ALU.add).then_inc(rope_done, 1)
                pool.wait_ge(gv_done, h + 1)
                rsqrt(stat[:, 18:20], stat[:, 16:18], 2).then_inc(gp_done, 1)
            step.leave(HEADS)
            pool.wait_ge(lnv_done, 2)
            rsqrt(sigma[:, :], lnv[:, :], REAL).then_inc(lnp_done, 1)
            for t in range(TT):
                pool.wait_ge(vr_done, 4 + t)
                rsqrt(stat[:, 6 + t:7 + t], stat[:, 3 + t:4 + t], 1).then_inc(pow_done, 1)
            pool.wait_ge(table_done, 4)
            nb = pool.value_load(nblocks[0:1, 0:1], min_val=NE, max_val=MAXB - 1)

            def low(b, k):
                pool.wait_ge(hi_done, 24 * b + (k + 1))
                pool.tensor_tensor(wlo[:, k % HS, :], raw_half(k), whi[:, k % HS, :].bitcast(F32),
                                   ALU.subtract).then_inc(lo_p, 1)

            with pool.Fori(0, nb) as b:
                for k in range(STEPS * HALVES):
                    if k % HALVES > 3:
                        low(b, k)
            for c in range(2):
                pool.wait_ge(hi_done, 24 * nb + (c + 1))
                pool.tensor_tensor(wlo[:, c, :], raw_half(4 + c), whi[:, c, :].bitcast(F32), ALU.subtract).then_inc(lo_p, 1)
            for t in range(TT):
                pool.wait_ge(vr_done, 6 + t)
                rsqrt(stat[:, 6 + t:7 + t], stat[:, 3 + t:4 + t], 1).then_inc(pow_done, 1)

        @block.tensor
        def _(pe):
            def copyT(o, i, n):
                return pe.transpose(o, i, ident[0:n, 0:n])

            pe.wait_ge(masked, 2)
            pe.wait_ge(par_in, 16 * 7)
            for r, n in enumerate((P, P, NPAR - 2 * P)):
                copyT(pb[:, 0, r * P:r * P + n], prow[0:n, r, :], n).then_inc(cols, 1)
            for t in (0, 1, 2):
                pe.wait_ge(xn_done, t + 1)
                n = META if t == 2 else P
                for k in range(KC):
                    o = pb[:, 1, k * META:(k + 1) * META] if t == 2 else pb[:, 4 + 2 * t + k // 4, (k % 4) * P:(k % 4 + 1) * P]
                    ins = copyT(o, xn[0:n, t, k * P:(k + 1) * P], n)
                ins.then_inc(cols, 1)
            pe.wait_ge(colse, 3)

            def project(s, use, fill, bank, t0, free, full, rhs=None):
                pe.wait_ge(landed[s], 16 * use)
                pe.wait_ge(free, 2 * fill)
                for j in range(2):
                    for k in range(KC):
                        mv = xnT[:, k, t0:TALL] if rhs is None else rhs[:, k, :]
                        ins = pe.matmul(pb[:, bank + j, 0:TALL - t0], ring[:, s, k, j * P:(j + 1) * P], mv,
                                        start=(k == 0), stop=(k == KC - 1))
                    ins.then_inc(full, 1)

            with pe.Fori(0, 4) as i:
                project(0, i + 1, i + 1, 0, 0, a_free, a_full)
                project(1, i + 1, i + 1, 2, 0, b_free, b_full)

            def turn_y(h1):
                pe.wait_ge(yn_done, 2 * h1 - 1)
                for c in range(VC):
                    for t in range(TT):
                        ins = copyT(pb[:, 4 + 3 * (c // 2), (c % 2) * REAL + t * P:(c % 2) * REAL + (t + 1) * P],
                                    yn[:, t, c * P:(c + 1) * P], P)
                    ins.then_inc(yt_done, 1)

            with pe.Fori(0, HEADS) as h:
                project(2, h + 1, 3 * h + 5, 0, META, a_free, a_full)
                project(3, h + 1, 3 * h + 5, 2, 0, b_free, b_full)
                project(4, h + 1, 3 * h + 6, 0, 0, a_free, a_full)
                turn_y(h + 1)
                project(5, h + 1, 3 * h + 6, 2, 0, b_free, b_full)
                project(0, h + 5, 3 * h + 7, 0, META, a_free, a_full)
                pe.wait_ge(a_free, 6 * h + 14)
                pe.wait_ge(b_free, 6 * h + 14)
                pe.wait_ge(rt_done, 4 * h + 4)
                for bank, t0, n in ((4, META, P), (5, META + P, P), (6, 0, META)):
                    for c in range(VC):
                        ins = copyT(pb[0:n, bank, c * P:(c + 1) * P], vT[:, c, t0:t0 + n], P)
                    ins.then_inc(vt_done, 1)
                pe.wait_ge(rope_done, 2 * h + 3)
                for c in range(2):
                    ins = pe.matmul(pb[:, 7, 0:REAL], krot[:, c, META:META + P], qrot[:, c, :],
                                    start=(c == 0), stop=(c == 1))
                ins.then_inc(sc_done, 1)
                for c in range(2):
                    ins = pe.matmul(pb[0:META, 7, REAL:2 * REAL], krot[:, c, 0:META], qrot[:, c, :],
                                    start=(c == 0), stop=(c == 1))
                ins.then_inc(sc_done, 1)
                project(1, h + 5, 3 * h + 7, 2, META, b_free, b_full)
                pe.wait_ge(v_done, 3 * h + 3)
                for c in range(2):
                    ins = pe.matmul(pb[:, 4, 0:P], krot[:, c, META + P:TALL], qrot[:, c, P:REAL],
                                    start=(c == 0), stop=(c == 1))
                ins.then_inc(sc_done, 1)
                pe.wait_ge(s_done, 3 * h + 2)
                pe.matmul(pb[:, 5, :], sM[0:META, 0:P], vM[0:META, :], start=True, stop=False)
                pe.matmul(pb[:, 5, :], sA[:, 0:P], vsb[:, 0, :], start=False, stop=True).then_inc(y_done, 1)
                pe.matmul(pb[:, 6, :], sM[0:META, P:REAL], vM[0:META, :], start=True, stop=False)
                pe.matmul(pb[:, 6, :], sA[:, P:REAL], vsb[:, 0, :], start=False, stop=False)
                pe.wait_ge(s_done, 3 * h + 3)
                pe.matmul(pb[:, 6, :], sB[:, 0:P], vsb[:, 1, :], start=False, stop=True).then_inc(y_done, 1)

            def channel_sum(src, fill):
                pe.wait_ge(b_free, 2 * fill)
                for k in range(KC):
                    ins = pe.matmul(pb[:, 2, 0:REAL], ones[:, :], src[:, k, :], start=(k == 0), stop=(k == KC - 1))
                    if k in (0, KC - 1):
                        ins.then_inc(b_full, 1)

            pe.wait_ge(conv_step, 4 * 62)
            channel_sum(cv, 17)
            turn_y(HEADS + 1)
            pe.wait_ge(rt_done, 4 * (HEADS + 1))
            with pe.Fori(0, UC) as r:
                pe.wait_ge(landed[4], 16 * (r + 5))
                pe.wait_ge(landed[5], 16 * (r + 5))
                pe.wait_ge(a_free, 2 * (r + 17))
                for j in range(2):
                    for k in range(2 * KC):
                        ins = pe.matmul(pb[:, j, 0:REAL], ring[:, 4 + k // KC, k % KC, j * P:(j + 1) * P],
                                        rT[:, VC + k, :], start=(k == 0), stop=(k == 2 * KC - 1))
                    ins.then_inc(a_full, 1)
            pe.wait_ge(lsq_done, 1)
            channel_sum(sq, 18)
            with pe.Fori(0, UC) as g:
                project(2, g + 5, g + 21, 0, META, a_free, a_full)
                project(3, g + 5, g + 19, 2, META, b_free, b_full)
            pe.wait_ge(ln_done, KC)
            with pe.Fori(0, 2) as i:
                project(0, i + 9, i + 25, 0, META, a_free, a_full, cv)
                project(1, i + 9, i + 23, 2, META, b_free, b_full, cv)
            pe.wait_ge(merged, KC)
            pe.wait_ge(a_free, 2 * 27)
            pe.wait_ge(b_free, 2 * 25)
            for n in range(UC):
                pe.wait_ge(landed[2 + n], 16 * 9)
                for t in range(TT):
                    for k in range(KC):
                        ins = pe.matmul(pb[:, n, t * UNIT:(t + 1) * UNIT], yret[:, k, t * P:(t + 1) * P],
                                        ring[:, 2 + n, k, :], start=(k == 0), stop=(k == KC - 1))
                ins.then_inc((a_full, b_full)[n // 2], 1)
            for t in range(TT):
                pe.wait_ge(xn_done, 4 + t)
                for k in range(KC):
                    ins = copyT(pb[:, 4 + 2 * t + k // 4, (k % 4) * P:(k % 4 + 1) * P], xn2[:, t, k * P:(k + 1) * P], P)
                ins.then_inc(x2t, 1)
            pe.wait_ge(rout_in, 32)
            for t in range(TT):
                pe.wait_ge(x2e, t + 1)
                for k in range(KC):
                    ins = pe.matmul(pb[:, 4 + t, 0:NE], xn2T[:, k, t * P:(t + 1) * P], wr[:, k, :],
                                    start=(k == 0), stop=(k == KC - 1))
                ins.then_inc(lgt, 1)
            pe.wait_ge(h2_done, 4)
            for t in range(TT):
                for c in range(2):
                    pe.matmul(pb[:, 2 * t + c, :], ident[:, :], hx[:, t, c * 512:(c + 1) * 512],
                              start=True, stop=False, skip_group_check=True)
            pe.wait_ge(route, 2)
            pe.wait_ge(lgt_read, 2)
            pe.matmul(pb[:, 6, 0:NE], before[:, :], mask[:, 0, :], start=True, stop=True).then_inc(w_used, 1)
            pe.matmul(pb[:, 6, NE:2 * NE], before[:, :], mask[:, 1, :], start=True, stop=False).then_inc(w_used, 1)
            pe.matmul(pb[:, 6, NE:2 * NE], ones[:, :], mask[:, 0, :], start=False, stop=True).then_inc(w_used, 1)
            pe.matmul(pb[:, 6, 2 * NE:3 * NE], ones[:, :], mask[:, 0, :], start=True, stop=False).then_inc(w_used, 1)
            pe.matmul(pb[:, 6, 2 * NE:3 * NE], ones[:, :], mask[:, 1, :], start=False, stop=True).then_inc(rank_done, 1)

            def gather():
                for k in range(KC):
                    for n in range(PARTS * TT):
                        ins = pe.matmul(pb[:, 7, k * SLOTS:(k + 1) * SLOTS], x3[:, n % PARTS, n // PARTS, k * P:(k + 1) * P],
                                        onehot[:, n // PARTS, :], start=(n == 0), stop=(n == PARTS * TT - 1))
                ins.then_inc(gathered, 1)

            def split_product(pairs, stop):
                ins = None
                for m, (x, y) in enumerate(((0, 0), (0, 1), (1, 0))):
                    for o, st, mv in pairs:
                        ins = pe.matmul(o, st[x], mv[y], start=False, stop=(stop and m == 2), skip_group_check=True)
                return ins

            def low_ready(b, k):
                pe.wait_ge(lo_v if k % HALVES < 4 else lo_p, lo_count(b, k))

            def hidden(b, k, stop):
                up = k % HALVES // 2
                low_ready(b, k)
                for r in range(KC // 2):
                    c = k % 2 * (KC // 2) + r
                    mv = [w[:, k % HS, r * UNIT:(r + 1) * UNIT] for w in (whi, wlo)]
                    ins = split_product([(pb[0:SLOTS, 4, up * UNIT:(up + 1) * UNIT], (xhi[:, c, :], xlo[:, c, :]), mv)],
                                        stop and r == KC // 2 - 1)
                ins.then_inc(w_used, 1)

            def down(k, stop):
                st = (ahi[:, k % 2, :], alo[:, k % 2, :])
                split_product([(pb[0:SLOTS, 5 + c, :], st, [w[:, k % HS, c * 512:(c + 1) * 512] for w in (whi, wlo)])
                               for c in range(2)], stop).then_inc(w_used, 1)

            def turn_act(n):
                pe.wait_ge(act_rdy, n + 1)
                for c in range(2):
                    ins = pe.matmul(pb[:, 7, c * SLOTS:(c + 1) * SLOTS], act[:, c * P:(c + 1) * P],
                                    ident[0:SLOTS, 0:SLOTS], start=True, stop=True)
                ins.then_inc(turned, 1)

            def turn_gates():
                for t in range(TT):
                    ins = pe.matmul(pb[0:SLOTS, 7, t * P:(t + 1) * P], gatehot[:, t, :], ident[:, :],
                                    start=True, stop=True)
                ins.then_inc(ght_done, 1)

            def scatter(stop):
                for t in range(TT):
                    st = (ghi[:, t * P:(t + 1) * P], glo[:, t * P:(t + 1) * P])
                    ins = split_product([(pb[:, 2 * t + c, :], st, (yhi[:, c * 512:(c + 1) * 512], ylo[:, c * 512:(c + 1) * 512]))
                                         for c in range(2)], stop)
                return ins

            pe.wait_ge(x3_rdy, PARTS)
            pe.wait_ge(hot_rdy, 2)
            gather()
            pe.wait_ge(b3_step, 6)
            pe.wait_ge(zeroed, 1)
            pe.wait_ge(gh_rdy, 1)
            pe.wait_ge(xlo_rdy, 1)
            turn_gates()
            pe.wait_ge(table_done, 4)
            nb = pe.value_load(nblocks[0:1, 0:1], min_val=NE, max_val=MAXB - 1)
            with pe.Fori(0, nb) as b:
                for q in range(STEPS):
                    k = q * HALVES
                    if q == 0:
                        pe.wait_ge(xlo_rdy, b + 1)
                        pe.wait_ge(sel_rdy, b + 1)
                    pe.wait_ge(clip_rdy, 4 * b + (q + 1))
                    pe.matmul(pb[0:SLOTS, 4, :], pick_e[:, :],
                              bias3[:, 0:2 * D].rearrange("p (u n) -> p u n", u=2)[:, :, q * UNIT:(q + 1) * UNIT],
                              start=True, stop=False, skip_group_check=True)
                    hidden(b, k, False)
                    hidden(b, k + 1, True)
                    if q == 0:
                        pe.wait_ge(glo_rdy, b + 1)
                    turn_act(4 * b + (q + 1))
                    hidden(b, k + 2, False)
                    hidden(b, k + 3, True)
                    if q == 3:
                        pe.wait_ge(hot_rdy, 2 * b + 4)
                        pe.wait_ge(alo_rdy, 4 * b + (q + 1))
                        gather()
                        pe.wait_ge(glo_rdy, b + 1)
                        pe.wait_ge(ylo_rdy, b + 1)
                        scatter(False)
                    pe.wait_ge(alo_rdy, 4 * b + (q + 1))
                    if q == 1:
                        pe.wait_ge(ylo_rdy, b + 1)
                        for c in range(2):
                            pe.matmul(pb[0:SLOTS, 5 + c, :], pick_e[:, :], bias3[:, 2 * D + c * 512:2 * D + (c + 1) * 512],
                                      start=True, stop=False, skip_group_check=True)
                    low_ready(b, k + 4)
                    down(k + 4, False)
                    low_ready(b, k + 5)
                    down(k + 5, q == 0)
                    if q == 3:
                        pe.wait_ge(gh_rdy, 2 * b + 3)
                        pe.wait_ge(xlo_rdy, b + 2)
                        turn_gates()
            pe.wait_ge(glo_rdy, nb + 1)
            turn_act(4 * nb + 1)
            pe.wait_ge(alo_rdy, 4 * nb + 1)
            pe.wait_ge(lo_p, 8 * nb + 1)
            down(4, False)
            pe.wait_ge(lo_p, 8 * nb + 2)
            down(5, True)
            pe.wait_ge(ylo_rdy, nb + 1)
            scatter(True).then_inc(acc_done, 1)

        @block.scalar
        def _(sc):
            rows = {0: a["conv_dw_w"][0].rearrange("w (c p) -> (w c) p", p=P)}
            sc.dma_start(prow[:, 0, :], rows[0][0:P, :]).then_inc(par_in, 16)
            sc.dma_start(prow[0:TAPS * KC - P, 1, :], rows[0][P:TAPS * KC, :]).then_inc(par_in, 16)
            for name, r0, n in (("conv_dw_b", TAPS * KC, KC), ("conv_ln_w", LNW, KC), ("conv_ln_b", LNB, KC),
                                ("b_conv_out", BCO, KC), ("ret_gn_w", GNW, 4 * VC)):
                sc.dma_start(prow[r0 % P:r0 % P + n, r0 // P, :],
                             a[name][0].rearrange("(c p) -> c p", p=P)).then_inc(par_in, 16)
            for q in range(3):
                sc.dma_start(brows[q * NE:(q + 1) * NE, 0:2 * D], a["b_gate_up"][0]).then_inc(bias_in, 16)
                sc.dma_start(brows[q * NE:(q + 1) * NE, 2 * D:3 * D], a["b_down"][0]).then_inc(bias_in, 16)
            sc.dma_start(eid[:, :], a["eid"]).then_inc(eid_in, 16)
            sc.dma_start(decay[:, :, :], a["decay"]).then_inc(tab_in, 16)
            sc.dma_start(cos, a["cos"]).then_inc(tab_in, 16)
            sc.dma_start(sin, a["sin"]).then_inc(tab_in, 16)

            for t in range(3):
                rows_ = META if t == 2 else P
                if t == 2:
                    sc.wait_ge(meta_in, 16)
                else:
                    sc.wait_ge(x_in, 32)
                if t:
                    sc.wait_ge(sq_done, t)
                sc.activation(junk1[0:rows_, :], hm[0:META, :] if t == 2 else hx[:, t, :], ACT.Square,
                              accum_out=stat[0:rows_, t:t + 1]).then_inc(sq_done, 1)
            sc.wait_ge(cols, 3)
            sc.activation(par[:, 0:P], pb[:, 0, 0:P], ACT.Copy).then_inc(a_free, 1)
            sc.activation(par[:, P:NPAR], pb[:, 0, P:NPAR], ACT.Copy).then_inc(a_free, 1)
            for t in range(3):
                sc.wait_ge(cols, 4 + t)
                if t < 2:
                    src = pb[:, 4 + 2 * t:6 + 2 * t, :].rearrange("p b (k n) -> p (b k) n", n=P)
                    dst = xnT[:, :, META + t * P:META + (t + 1) * P]
                else:
                    src = pb[:, 1, 0:KC * META].rearrange("p (k n) -> p k n", n=META)
                    dst = xnT[:, :, 0:META]
                sc.activation(dst, src, ACT.Copy).then_inc(colse, 1)

            with sc.Fori(0, 4) as i:
                for j in range(2):
                    sc.wait_ge(b_full, 2 * i + (1 + j))
                    if j == 0:
                        sc.wait_ge(a_free, 2 * i + 2)
                    sc.activation(sigb[:, j, :], pb[:, 2 + j, 0:TALL], ACT.Sigmoid).then_inc(b_free, 1)

            with sc.Fori(0, HEADS) as h:
                sc.wait_ge(rope_done, 2 * h + 1)
                for j in range(2):
                    sc.wait_ge(a_full, 6 * h + (9 + j))
                    sc.activation(qraw[:, j, :], pb[:, j, 0:REAL], ACT.Copy).then_inc(a_free, 1)
                for j in range(2):
                    sc.wait_ge(b_full, 6 * h + (9 + j))
                    sc.activation(kraw[:, j, :], pb[:, 2 + j, 0:TALL], ACT.Copy).then_inc(b_free, 1)
                for j in range(VC):
                    sc.wait_ge((a_full, b_full)[j // 2], 6 * h + (11 + j % 2))
                    sc.activation(vT[:, j, :], pb[:, j, 0:TALL], ACT.Copy).then_inc((a_free, b_free)[j // 2], 1)
                sc.wait_ge(rt_done, 4 * h + 4)
                for j in range(2):
                    sc.wait_ge(a_full, 6 * h + (13 + j))
                    sc.activation(sg[:, j, :], pb[:, j, 0:REAL], ACT.Silu).then_inc(a_free, 1)
                sc.wait_ge(vt_done, 3 * h + 1)
                sc.activation(vsb[:, 0, :], pb[:, 4, :], ACT.Copy).then_inc(v_done, 1)
                sc.wait_ge(vt_done, 3 * h + 2)
                sc.activation(vsb[:, 1, :], pb[:, 5, :], ACT.Copy).then_inc(v_done, 1)
                sc.wait_ge(vt_done, 3 * h + 3)
                sc.activation(vM[0:META, :], pb[0:META, 6, :], ACT.Copy).then_inc(v_done, 1)
                for j in range(2):
                    sc.wait_ge(b_full, 6 * h + (13 + j))
                    sc.activation(sg[:, 2 + j, :], pb[:, 2 + j, 0:REAL], ACT.Silu).then_inc(b_free, 1)

            sc.wait_ge(xc_done, 2)
            sc.activation(sq, cv[:, :, :], ACT.Square).then_inc(lsq_done, 1)
            with sc.Fori(0, UC) as r:
                for j in range(2):
                    sc.wait_ge(a_full, 2 * r + (33 + j))
                    sc.activation(yret[:, bass.ds(2 * r + j, 1), :], pb[:, j:j + 1, 0:REAL], ACT.Copy).then_inc(a_free, 1)
            sc.wait_ge(lnx_done, 1)
            for k in range(KC):
                sc.activation(cv[:, k, :], cv[:, k, :], ACT.Silu, scale=par[:, LNW + k:LNW + k + 1],
                              bias=par[:, LNB + k:LNB + k + 1]).then_inc(ln_done, 1)
            with sc.Fori(0, UC) as g:
                for j in range(2):
                    sc.wait_ge(a_full, 2 * g + (41 + j))
                    sc.activation(sga[:, bass.ds(2 * g + j, 1), :], pb[:, j:j + 1, 0:REAL], ACT.Sigmoid).then_inc(a_free, 1)
                for j in range(2):
                    sc.wait_ge(b_full, 2 * g + (37 + j))
                    sc.activation(sgb[:, bass.ds(2 * g + j, 1), :], pb[:, 2 + j:3 + j, 0:REAL], ACT.Sigmoid).then_inc(b_free, 1)

            sc.wait_ge(h2_done, 4)
            for t in range(TT):
                if t:
                    sc.wait_ge(sq_done, 3 + t)
                sc.activation(junk2, hx[:, t, :], ACT.Square, accum_out=stat[:, t:t + 1]).then_inc(sq_done, 1)
            for t in range(TT):
                sc.wait_ge(x2t, t + 1)
                sc.activation(xn2T[:, :, t * P:(t + 1) * P],
                              pb[:, 4 + 2 * t:6 + 2 * t, :].rearrange("p b (k n) -> p (b k) n", n=P),
                              ACT.Copy).then_inc(x2e, 1)
            sc.activation(x3[:, 0, :, :], xn2[:, :, :], ACT.Copy).then_inc(x3_rdy, 1)
            for t in range(TT):
                sc.wait_ge(shift_done, t + 1)
                sc.activation(gate4[:, t, :], gate4[:, t, :], ACT.Exp, accum_out=stat[:, 10 + t:11 + t]).then_inc(exp_done, 1)
            for q in range(1, PARTS):
                sc.wait_ge(xr_rdy, q)
                sc.activation(x3[:, q, :, :], xres[:, :, :], ACT.Copy).then_inc(x3_rdy, 1)

            def tokens(n):
                sc.wait_ge(gathered, n)
                sc.activation(xhi[:, :, :], pb[:, 7, :].rearrange("p (k n) -> p k n", n=SLOTS), ACT.Copy).then_inc(xhi_rdy, 1)

            tokens(1)
            sc.wait_ge(table_done, 4)
            nb = sc.value_load(nblocks[0:1, 0:1], min_val=NE, max_val=MAXB - 1)

            def high(b, k):
                if k % 2 == 0:
                    sc.wait_ge(e_in[k // 2 % 6], 32 * b + 16 * (1 + k // 12))
                sc.wait_ge(w_used, 24 * b + (k + 1))
                sc.activation(whi[:, k % HS, :], raw_half(k), ACT.Copy).then_inc(hi_done, 1)

            def sigmoid(n):
                sc.wait_ge(min_rdy, n)
                sc.activation(sig, hg, ACT.Sigmoid, scale=ALPHA).then_inc(sig_rdy, 1)

            def act_high(n):
                sc.wait_ge(turned, n)
                sc.activation(ahi[:, :, :], pb[:, 7, 0:2 * SLOTS].rearrange("p (k n) -> p k n", n=SLOTS),
                              ACT.Copy).then_inc(ahi_rdy, 1)

            def gates_high(n):
                sc.wait_ge(ght_done, n)
                sc.activation(ghi[:, :], pb[0:SLOTS, 7, 0:REAL], ACT.Copy).then_inc(ghi_rdy, 1)

            def out_high(b):
                sc.wait_ge(w_used, 24 * b + (HS + 6))
                sc.activation(yhi[:, :], pb[0:SLOTS, 5:7, :].rearrange("p a b -> p (a b)"), ACT.Copy).then_inc(yhi_rdy, 1)

            with sc.Fori(0, nb) as b:
                for q in range(STEPS):
                    k = q * HALVES
                    high(b, k)
                    sigmoid(4 * b + (q + 1))
                    high(b, k + 1)
                    if q == 0:
                        gates_high(b + 1)
                    high(b, k + 2)
                    if q == 1:
                        out_high(b)
                    high(b, k + 3)
                    high(b, k + 4)
                    act_high(4 * b + (q + 1))
                    high(b, k + 5)
                    if q == 3:
                        tokens(b + 2)
            sigmoid(4 * nb + 1)
            gates_high(nb + 1)
            act_high(4 * nb + 1)
            sc.wait_ge(e_in[2], 32 * nb + 16)
            for k in (4, 5):
                sc.wait_ge(w_used, 24 * nb + (k - 3))
                sc.activation(whi[:, k % HS, :], raw_half(k), ACT.Copy).then_inc(hi_done, 1)
            sc.wait_ge(w_used, 24 * nb + (HS + 2))
            sc.activation(yhi[:, :], pb[0:SLOTS, 5:7, :].rearrange("p a b -> p (a b)"), ACT.Copy).then_inc(yhi_rdy, 1)
            sc.wait_ge(acc_done, 1)
            for t in range(TT):
                if t:
                    sc.wait_ge(sq_done, 5 + t)
                sc.activation(junk2, pb[:, 2 * t:2 * t + 2, :].rearrange("p a b -> p (a b)"), ACT.Square,
                              accum_out=stat[:, t:t + 1]).then_inc(sq_done, 1)

        @block.vector
        def _(dve):
            def variance(t, rows, n):
                dve.wait_ge(sq_done, n)
                dve.tensor_scalar(stat[0:rows, 3 + t:4 + t], stat[0:rows, t:t + 1], 1.0 / D, EPS, ALU.mult,
                                  ALU.add).then_inc(vr_done, 1)

            dve.memset(bias3[3 * NE:P, :], 0.0).then_inc(zeroed, 1)
            for c in (22, 23):
                dve.memset(stat[:, c:c + 1], 0.0).then_inc(b_free, 1)
            dve.wait_ge(wmb_in, 16)
            for t in range(3):
                variance(t, META if t == 2 else P, t + 1)
            for t in range(3):
                rows = META if t == 2 else P
                dve.wait_ge(pow_done, t + 1)
                dve.scalar_tensor_tensor(out=xn[0:rows, t, :], in0=hm[0:META, :] if t == 2 else hx[:, t, :],
                                         scalar=stat[0:rows, 6 + t:7 + t], in1=wmb[0:rows, :], op0=ALU.mult,
                                         op1=ALU.mult).then_inc(xn_done, 1)

            dve.wait_ge(consts, 9)
            dve.wait_ge(a_free, 2)
            taps = par[:, 0:256].rearrange("p (w c) -> p w c", c=KC)
            step = Chain(dve, conv_step)
            with dve.Fori(0, 4) as i:
                step.enter(i, 62)
                dve.tensor_copy(wt[:, :, :], taps[:, :, bass.ds(2 * i, 2)]).then_inc(wt_done, 1)
                for j in range(2):
                    dve.wait_ge(a_full, 2 * i + (1 + j))
                    dve.wait_ge(b_free, 2 * i + (3 + j))
                    dve.tensor_tensor(upad[:, j, PADL:PADL + TALL], pb[:, j, 0:TALL], sigb[:, j, :],
                                      ALU.mult).then_inc(a_free, 1)
                dve.wait_ge(wt_done, i + 1)
                for w in range(TAPS):
                    for j in range(2):
                        u = upad[:, j, w:w + REAL]
                        if w == 0:
                            dve.wait_ge(a_free, 2 * i + (3 + j))
                            ins = dve.tensor_scalar(cacc[:, j, :], u, wt[:, 0, j:j + 1], wt[:, TAPS, j:j + 1],
                                                    ALU.mult, ALU.add)
                        else:
                            step.wait(1)
                            o = cacc[:, j:j + 1, :] if w < TAPS - 1 else cv[:, bass.ds(2 * i + j, 1), :]
                            ins = dve.scalar_tensor_tensor(out=o, in0=upad[:, j:j + 1, w:w + REAL],
                                                           scalar=wt[:, w, j:j + 1], in1=cacc[:, j:j + 1, :],
                                                           op0=ALU.mult, op1=ALU.add)
                        step.did(ins)
                step.wait()
            step.leave(4)

            dve.wait_ge(tab_in, 48)
            dve.wait_ge(b3_step, 6)
            gn = Chain(dve, gn_step)

            def gate_y(h, h1):
                dve.wait_ge(a_free, 6 * h1 + 4)
                dve.wait_ge(b_free, 6 * h1 + 4)
                for c in range(VC):
                    dve.wait_ge(yt_done, 4 * h1 - (2 if c < 2 else 0))
                    src = pb[:, 4 + 3 * (c // 2), (c % 2) * REAL:(c % 2 + 1) * REAL].rearrange("p (o n) -> p o n", o=1)
                    if isinstance(h, int):
                        o, w = rT[:, h * VC + c:h * VC + c + 1, :], par[:, GNW - VC + h * VC + c:GNW - VC + h * VC + c + 1]
                    else:
                        o, w = rT[:, bass.ds(h * VC + c, 1), :], par[:, bass.ds(h * VC + (GNW - VC + c), 1)]
                    dve.scalar_tensor_tensor(out=o, in0=src, scalar=w, in1=sg[:, c:c + 1, :], op0=ALU.mult,
                                             op1=ALU.mult).then_inc(rt_done, 1)

            with dve.Fori(0, HEADS) as h:
                gn.enter(h, 8)
                gate_y(h, h + 1)
                dve.wait_ge(sc_done, 3 * h + 2)
                dve.tensor_tensor(sA.rearrange("p (o n) -> p o n", o=1), pb[:, 7:8, 0:REAL],
                                  decay[:, bass.ds(h, 1), 0:REAL], ALU.mult).then_inc(s_done, 1)
                dve.tensor_tensor(sM[0:META, :].rearrange("p (o n) -> p o n", o=1), pb[0:META, 7:8, REAL:2 * REAL],
                                  decay[0:META, bass.ds(h, 1), META:TALL], ALU.mult).then_inc(s_done, 1)
                dve.wait_ge(sc_done, 3 * h + 3)
                dve.tensor_tensor(sB.rearrange("p (o n) -> p o n", o=1), pb[:, 4:5, 0:P],
                                  decay[:, bass.ds(h, 1), 0:P], ALU.mult).then_inc(s_done, 1)
                for t in range(TT):
                    dve.wait_ge(y_done, 2 * h + (1 + t))
                    gn.did(dve.bn_stats(bst[:, t, :], pb[:, 5 + t, :]))
                gn.wait()
                gn.did(dve.tensor_tensor(bmv[:, :, 1], bst[:, :, 1], bst[:, :, 4], ALU.add))
                gn.did(dve.tensor_tensor(bmv[:, :, 2], bst[:, :, 1], bst[:, :, 4], ALU.subtract))
                gn.did(dve.tensor_tensor(bmv[:, :, 3], bst[:, :, 2], bst[:, :, 5], ALU.add))
                gn.wait()
                gn.did(dve.tensor_scalar(bmv[:, :, 0], bmv[:, :, 1], 0.5, None, ALU.mult))
                gn.did(dve.scalar_tensor_tensor(out=bmv[:, :, 2], in0=bmv[:, :, 2], scalar=0.25, in1=bmv[:, :, 2],
                                                op0=ALU.mult, op1=ALU.mult))
                gn.did(dve.tensor_scalar(bmv[:, :, 3], bmv[:, :, 3], 1.0 / DV, EPS, ALU.mult, ALU.add))
                gn.wait()
                dve.tensor_tensor(stat[:, 16:18], bmv[:, :, 2], bmv[:, :, 3], ALU.add).then_inc(gv_done, 1)
                dve.wait_ge(gp_done, h + 1)
                for t in range(TT):
                    dve.tensor_scalar(yn[:, t, :], pb[:, 5 + t, :], bmv[:, t, 0:1], stat[:, 18 + t:19 + t],
                                      ALU.subtract, ALU.mult).then_inc(yn_done, 1)
            gn.leave(HEADS)
            gate_y(HEADS, HEADS + 1)

            dve.wait_ge(b_full, 34)
            for c in range(2):
                m = pb[:, 2:3, 0:REAL].to_broadcast([P, KC // 2, REAL])
                part = cv[:, c * KC // 2:(c + 1) * KC // 2, :]
                dve.scalar_tensor_tensor(out=part, in0=m, scalar=-1.0 / D, in1=part, op0=ALU.mult,
                                         op1=ALU.add).then_inc(xc_done, 1)
            dve.wait_ge(xc_done, 2)
            dve.tensor_copy(stat[:, 12:13], cv[:, 0, 0:1]).then_inc(b_free, 1)
            dve.tensor_copy(stat[:, 13:14], cv[:, 4, 0:1]).then_inc(b_free, 1)
            dve.wait_ge(b_full, 36)
            for c in range(2):
                s_ = slice(c * P, (c + 1) * P)
                dve.tensor_scalar(lnv[:, s_], pb[:, 2, s_], 1.0 / D, EPS, ALU.mult, ALU.add).then_inc(lnv_done, 1)
            dve.wait_ge(lnv_done, 2)
            dve.tensor_copy(stat[:, 12:13], lnv[:, 0:1]).then_inc(b_free, 1)
            dve.tensor_copy(stat[:, 13:14], lnv[:, 0:1]).then_inc(b_free, 1)
            dve.wait_ge(lnp_done, 1)
            dve.tensor_tensor(cv[:, :, :], cv[:, :, :],
                              sigma[:, :].rearrange("p (o n) -> p o n", o=1).to_broadcast([P, KC, REAL]),
                              ALU.mult).then_inc(lnx_done, 1)
            with dve.Fori(0, UC) as g:
                for j in range(2):
                    dve.wait_ge(b_free, 2 * g + (39 + j))
                    dve.wait_ge(a_free, 42)
                    o = yret[:, bass.ds(2 * g + j, 1), :]
                    dve.tensor_tensor(o, o, sgb[:, bass.ds(2 * g + j, 1), :], ALU.mult).then_inc(gb_done, 1)
            dve.wait_ge(a_free, 50)
            dve.wait_ge(gb_done, KC)
            with dve.Fori(0, 2) as i:
                for q in range(4):
                    full, free, base = ((a_full, a_free, 49), (b_full, b_free, 45))[q // 2]
                    c = bass.ds(4 * i + q, 1)
                    dve.wait_ge(full, 2 * i + (base + q % 2))
                    dve.scalar_tensor_tensor(out=sga[:, c, :], in0=pb[:, q:q + 1, 0:REAL],
                                             scalar=par[:, bass.ds(4 * i + (BCO + q), 1)], in1=sga[:, c, :],
                                             op0=ALU.add, op1=ALU.mult).then_inc(free, 1)
                    dve.wait_ge(free, 2 * i + (base + 2 + q % 2))
                    dve.tensor_tensor(yret[:, c, :], yret[:, c, :], sga[:, c, :], ALU.add).then_inc(merged, 1)
            for n in range(UC):
                dve.wait_ge((a_full, b_full)[n // 2], (53, 49)[n // 2] + n % 2)
                o = hx[:, :, n * UNIT:(n + 1) * UNIT]
                dve.tensor_tensor(o, o, pb[:, n, :].rearrange("p (t n) -> p t n", t=TT), ALU.add).then_inc(h2_done, 1)
            dve.wait_ge(nwb_in, 32)
            for t in range(TT):
                variance(t, P, 4 + t)
            for t in range(TT):
                dve.wait_ge(pow_done, 4 + t)
                dve.scalar_tensor_tensor(out=xn2[:, t, :], in0=hx[:, t, :], scalar=stat[:, 6 + t:7 + t],
                                         in1=nwb[:, 0, :], op0=ALU.mult, op1=ALU.mult).then_inc(xn_done, 1)

            rt = Chain(dve, route_step)

            def do(ins):
                rt.did(ins)
                rt.wait()

            hot4 = pick[:, 0:TT * TOPK * NE].rearrange("p (t k e) -> p t k e", t=TT, k=TOPK)
            dve.wait_ge(rout_in, 32)
            for t in range(TT):
                dve.wait_ge(lgt, t + 1)
                dve.tensor_tensor(lg[:, t, :], pb[:, 4 + t, 0:NE], brb[:, :], ALU.add).then_inc(lgt_read, 1)
                dve.wait_ge(lgt_read, t + 1)
                do(dve.max(top[:, t, :], lg[:, t, :]))
                dve.tensor_scalar(gate4[:, t, :], top[:, t, 0:TOPK], top[:, t, 0:1], None,
                                  ALU.subtract).then_inc(shift_done, 1)
                do(dve.max_index(topi[:, t, :], top[:, t, :], lg[:, t, :]))
                do(dve.tensor_copy(topf[:, t, :], topi[:, t, 0:TOPK]))
                do(dve.tensor_tensor(hot4[:, t], iota_e[:, :].rearrange("p (o e) -> p o e", o=1).to_broadcast([P, TOPK, NE]),
                                     topf[:, t, :].rearrange("p (k o) -> p k o", o=1).to_broadcast([P, TOPK, NE]),
                                     ALU.is_equal))
                dve.tensor_reduce(mask[:, t, :], hot4[:, t].rearrange("p k e -> p e k"), AX_X, ALU.add).then_inc(route, 1)
            dve.wait_ge(x3_rdy, 1)
            dve.tensor_tensor(xres[:, :, :], xn2[:, :, :], x3[:, 0, :, :], ALU.subtract).then_inc(xr_rdy, 1)
            dve.wait_ge(rank_done, 1)
            cnt = pb[:, 6, 2 * NE:3 * NE]
            do(dve.tensor_scalar(nblk[:, :], cnt, float(SLOTS), 1.0, ALU.is_gt, ALU.add))
            for q in (2, 3):
                do(dve.scalar_tensor_tensor(out=nblk[:, :], in0=cnt, scalar=float(q * SLOTS), in1=nblk[:, :],
                                            op0=ALU.is_gt, op1=ALU.add))
            do(dve.tensor_tensor_scan(pend[:, :], ones[:, 0:NE], nblk[:, :], 0.0, ALU.mult, ALU.add))
            do(dve.tensor_tensor(nblk[:, :], pend[:, :], nblk[:, :], ALU.subtract))
            do(dve.tensor_scalar(nblk[:, :], nblk[:, :], float(SLOTS), 1.0, ALU.mult, ALU.add))
            starts = nblk[:, :].rearrange("p (o e) -> p o e", o=1).to_broadcast([P, TT, NE])
            do(dve.tensor_tensor(slot[:, :, :], pb[:, 6, 0:TT * NE].rearrange("p (t e) -> p t e", t=TT), starts, ALU.add))
            do(dve.tensor_tensor(slot[:, :, :], slot[:, :, :], mask[:, :, :], ALU.mult))
            do(dve.tensor_scalar(slot[:, :, :], slot[:, :, :], -1.0, None, ALU.add))
            for t in range(TT):
                dve.tensor_scalar(onehot[:, t, :], iota_s[:, :], slot[:, t, 0:1], None, ALU.is_equal).then_inc(hot_rdy, 1)
            dve.wait_ge(x3_rdy, 2)
            dve.wait_ge(xr_rdy, 1)
            dve.tensor_tensor(xres[:, :, :], xres[:, :, :], x3[:, 1, :, :], ALU.subtract).then_inc(xr_rdy, 1)
            for t in range(TT):
                dve.wait_ge(exp_done, t + 1)
                do(dve.reciprocal(stat[:, 12 + t:13 + t], stat[:, 10 + t:11 + t]))
                do(dve.tensor_scalar(gate4[:, t, :], gate4[:, t, :], stat[:, 12 + t:13 + t], None, ALU.mult))
                do(dve.tensor_tensor(hot4[:, t], hot4[:, t], gate4[:, t, :].rearrange("p (k o) -> p k o", o=1)
                                     .to_broadcast([P, TOPK, NE]), ALU.mult))
                do(dve.tensor_reduce(gdense[:, t, :], hot4[:, t].rearrange("p k e -> p e k"), AX_X, ALU.add))
            half = MAXB // 2
            c3 = pick[:, 0:half * NE].rearrange("p (b e) -> p b e", e=NE)
            for q in range(2):
                do(dve.tensor_tensor(c3, pend[:, :].rearrange("p (o e) -> p o e", o=1).to_broadcast([P, half, NE]),
                                     iota_b[:, q * half:(q + 1) * half].rearrange("p (b o) -> p b o", o=1)
                                     .to_broadcast([P, half, NE]), ALU.is_le))
                do(dve.tensor_reduce(tabf[:, q * half:(q + 1) * half], c3, AX_X, ALU.add))
            do(dve.tensor_scalar(tabf[:, :], tabf[:, :], float(NE - 1), None, ALU.min))
            dve.memset(table[0:1, 0:1], 0).then_inc(table_done, 1)
            dve.tensor_copy(table[0:1, 1:MAXB + 1], tabf[0:1, :]).then_inc(table_done, 1)
            dve.tensor_scalar(nblocks[:, 1:2], pend[0:1, NE - 1:NE], -1.0, None, ALU.add).then_inc(table_done, 1)
            dve.tensor_copy(nblocks[:, 0:1], pend[0:1, NE - 1:NE]).then_inc(table_done, 1)

            def pick_rows(b):
                col = tabf[:, b:b + 1] if isinstance(b, int) else tabf[:, bass.ds(b, 1)]
                dve.tensor_scalar(pick_e[:, :], eid[:, :], col, None, ALU.is_equal).then_inc(sel_rdy, 1)

            def tokens_low(n):
                dve.wait_ge(xhi_rdy, n)
                dve.tensor_tensor(xlo[:, :, :], pb[:, 7, :].rearrange("p (k n) -> p k n", n=SLOTS),
                                  xhi[:, :, :].bitcast(F32), ALU.subtract).then_inc(xlo_rdy, 1)

            dve.memset(gatehot[:, :, :], 0.0).then_inc(gh_rdy, 1)
            dve.memset(act, 0.0).then_inc(act_rdy, 1)
            dve.wait_ge(eid_in, 16)
            pick_rows(0)
            tokens_low(1)
            dve.wait_ge(table_done, 4)
            nb = dve.value_load(nblocks[0:1, 0:1], min_val=NE, max_val=MAXB - 1)

            def low(b, k):
                dve.wait_ge(hi_done, 24 * b + (k + 1))
                dve.tensor_tensor(wlo[:, k % HS, :], raw_half(k), whi[:, k % HS, :].bitcast(F32),
                                  ALU.subtract).then_inc(lo_v, 1)

            def activate(n, used, half=None):
                dve.wait_ge(w_used, used)
                dve.wait_ge(act_rdy, n)
                dve.tensor_scalar(hg, pb[0:SLOTS, 4, 0:UNIT], LIMIT, None, ALU.min).then_inc(min_rdy, 1)
                dve.tensor_scalar(hu, pb[0:SLOTS, 4, UNIT:2 * UNIT], -LIMIT, LIMIT, ALU.max, ALU.min).then_inc(clip_rdy, 1)
                if half:
                    low(*half)
                dve.wait_ge(sig_rdy, n)
                dve.tensor_tensor(sig, sig, hg, ALU.mult).then_inc(prod_rdy, 1)
                dve.wait_ge(clip_rdy, n)
                dve.wait_ge(prod_rdy, n)
                dve.scalar_tensor_tensor(out=act, in0=hu, scalar=1.0, in1=sig, op0=ALU.add,
                                         op1=ALU.mult).then_inc(act_rdy, 1)

            def gates_low(n):
                dve.wait_ge(ghi_rdy, n)
                dve.tensor_tensor(glo[:, :], pb[0:SLOTS, 7, 0:REAL], ghi[:, :].bitcast(F32), ALU.subtract).then_inc(glo_rdy, 1)

            def act_low(n):
                dve.wait_ge(ahi_rdy, n)
                dve.tensor_tensor(alo[:, :, :], pb[:, 7, 0:2 * SLOTS].rearrange("p (k n) -> p k n", n=SLOTS),
                                  ahi[:, :, :].bitcast(F32), ALU.subtract).then_inc(alo_rdy, 1)

            def out_low(n):
                dve.wait_ge(yhi_rdy, n)
                dve.tensor_tensor(ylo[:, :], pb[0:SLOTS, 5:7, :].rearrange("p a b -> p (a b)"),
                                  yhi[:, :].bitcast(F32), ALU.subtract).then_inc(ylo_rdy, 1)

            with dve.Fori(0, nb) as b:
                e = dve.value_load(table[0:1, bass.ds(b + 1, 1)], min_val=0, max_val=NE - 1)
                e1 = dve.value_load(table[0:1, bass.ds(b + 2, 1)], min_val=0, max_val=NE - 1)
                for q in range(STEPS):
                    k = q * HALVES
                    activate(4 * b + (q + 1), 24 * b + (HS + k - 2), (b, k))
                    low(b, k + 1)
                    if q == 0:
                        gates_low(b + 1)
                    low(b, k + 2)
                    if q == 1:
                        out_low(b + 1)
                    low(b, k + 3)
                    act_low(4 * b + (q + 1))
                    if q == 1:
                        dve.wait_ge(ght_done, b + 1)
                        dve.wait_ge(gh_rdy, 2 * b + 1)
                        for t in range(TT):
                            dve.tensor_scalar(gatehot[:, t, :], iota_s[:, :], slot[:, t, bass.ds(e, 1)],
                                              gdense[:, t, bass.ds(e, 1)], ALU.is_equal, ALU.mult).then_inc(gh_rdy, 1)
                        dve.wait_ge(gh_rdy, 2 * b + 3)
                        dve.wait_ge(hot_rdy, 2 * b + 2)
                        dve.tensor_scalar(iota_s[:, :], iota_s[:, :], float(SLOTS), None, ALU.add).then_inc(slot_step, 1)
                        dve.wait_ge(slot_step, b + 1)
                        dve.wait_ge(gathered, b + 1)
                        for t in range(TT):
                            dve.tensor_scalar(onehot[:, t, :], iota_s[:, :], slot[:, t, bass.ds(e1, 1)], None,
                                              ALU.is_equal).then_inc(hot_rdy, 1)
                    if q == 3:
                        dve.wait_ge(w_used, 24 * b + (HS + 19))
                        pick_rows(b + 1)
                        tokens_low(b + 2)
            activate(4 * nb + 1, 24 * nb + (HS - 2))
            gates_low(nb + 1)
            act_low(4 * nb + 1)
            out_low(nb + 1)
            for t in range(TT):
                variance(t, P, 6 + t)
            for t in range(TT):
                dve.wait_ge(pow_done, 6 + t)
                dve.scalar_tensor_tensor(out=osb[:, t, :], in0=pb[:, 2 * t:2 * t + 2, :].rearrange("p a b -> p (a b)"),
                                         scalar=stat[:, 6 + t:7 + t], in1=nwb[:, 1, :], op0=ALU.mult,
                                         op1=ALU.mult).then_inc(out_rdy, 1)


NAMES = ["x", "meta_tokens", "norm_mix_w", "w_in", "conv_dw_w", "conv_dw_b", "conv_ln_w", "conv_ln_b", "w_conv_out",
         "b_conv_out", "ret_gn_w", "w_ret_out", "w_mix_out", "norm_ffn_w", "w_router", "b_router", "w_gate_up",
         "b_gate_up", "w_down", "b_down", "norm_final_w"]


def shape_tables():
    import numpy as np
    f = np.float32
    inv = (f(10000.0) ** (-np.arange(0, DK, 2, dtype=f) / f(DK))).astype(f)
    ang = (inv[:, None] * np.arange(TALL, dtype=f)[None, :]).astype(f)
    lg = np.log1p(-np.exp2(-5.0 - np.arange(HEADS)))
    n = np.arange(TALL)[None, :] - np.arange(P)[:, None]
    dec = np.where(n[:, None, :] >= 0, np.exp(lg[None, :, None] * np.maximum(n, 0)[:, None, :]), 0.0) * DK ** -0.5
    rows = np.arange(P)
    eid = np.where(rows < 3 * NE, rows % NE, -1).astype(f)[:, None].repeat(SLOTS, 1)
    return {"eid": np.ascontiguousarray(eid), "cos": np.cos(ang).astype(f), "sin": np.sin(ang).astype(f), "decay": np.ascontiguousarray(dec.astype(f))}


def kernel(**inputs):
    import numpy as np
    import concourse.bacc as bacc
    from concourse.bass_utils import run_bass_kernel_spmd as run

    nc = bacc.Bacc("TRN2", target_bir_lowering=False, num_devices=1)
    arrays, aps = {}, {}
    tables = shape_tables()
    for name in NAMES + list(tables):
        arr = np.ascontiguousarray(tables[name] if name in tables else inputs[name])
        arrays[f"in_{name}"] = arr
        aps[name] = nc.dram_tensor(f"in_{name}", arr.shape, mybir.dt.from_np(arr.dtype), kind="ExternalInput").ap()
    out = nc.dram_tensor("out_0", (1, REAL, D), F32, kind="ExternalOutput").ap()
    build_block(nc, aps, out)
    return run(nc, [arrays], core_ids=[0]).results[0]["out_0"]
```

```python
from contextlib import ExitStack

import concourse.bass as bass
from concourse import mybir

F32 = mybir.dt.float32
I32 = mybir.dt.int32
U32 = mybir.dt.uint32
R32 = mybir.dt.float32r
BF16 = mybir.dt.bfloat16
ALU = mybir.AluOpType
ACT = mybir.ActivationFunctionType
AX_X = mybir.AxisListType.X

P = 128
D = 1024
KC = D // P
META = 16
REAL = 256
TT = REAL // P
TALL = META + REAL
TAPS = 31
PADL = TAPS - 1 - META
HEADS = 4
DK = 256
DV = 512
VC = DV // P
UNIT = 256
NE = 32
TOPK = 4
SLOTS = 64
MAXB = 48
STEPS = D // UNIT
HALVES = 6
HW = KC * UNIT // 2
HS = 4
PARTS = 3
EPS = 1e-5
LIMIT = 7.0
ALPHA = 1.702

TAP0, LNW, LNB, BCO, GNW = 0, 256, 264, 272, 280
NPAR = 296


class Chain:

    def __init__(self, eng, sem):
        self.eng, self.sem, self.base, self.n = eng, sem, 0, 0

    def did(self, ins):
        ins.then_inc(self.sem, 1)
        self.n += 1

    def wait(self, back=0):
        self.eng.wait_ge(self.sem, self.base + (self.n - back))

    def enter(self, i, per):
        self.start, self.per = self.base + self.n, per
        self.base, self.n = i * per + self.start, 0

    def leave(self, trips):
        assert self.n == self.per, (self.n, self.per)
        self.base, self.n = self.start + trips * self.per, 0


def build_block(nc, a, out):
    with ExitStack() as ctx:
        def sb(name, shape, dt=F32):
            return ctx.enter_context(nc.sbuf_tensor(name, shape, dt))

        def sem(name):
            return ctx.enter_context(nc.semaphore(name))

        pb = ctx.enter_context(nc.psum_tensor("pb", [P, 8, 512], F32))

        ring = sb("ring", [P, 6, KC, UNIT])
        xnT = sb("xnT", [P, KC, TALL])
        hx = sb("hx", [P, TT, D])
        cv = sb("cv", [P, KC, REAL])
        rT = sb("rT", [P, 4 * VC + VC, REAL])
        ubuf = sb("ubuf", [P, KC * (PADL + TALL)])
        scratch = sb("scratch", [P, 11268])
        whi = sb("whi", [P, HS, HW], R32)
        wlo = sb("wlo", [P, HS, HW], R32)
        xhi, xlo = (sb(n, [P, KC, SLOTS], R32) for n in ("xhi", "xlo"))
        ahi, alo = (sb(n, [P, 2, SLOTS], R32) for n in ("ahi", "alo"))
        yhi, ylo = (sb(n, [SLOTS, D], R32) for n in ("yhi", "ylo"))
        ghi, glo = (sb(n, [SLOTS, REAL], R32) for n in ("ghi", "glo"))
        bias3 = sb("bias3", [P, 3 * D], BF16)
        pick_e = sb("pick_e", [P, SLOTS], BF16)
        eid = sb("eid", [P, SLOTS])
        par = sb("par", [P, NPAR])
        ident = sb("ident", [P, P])
        ones = sb("ones", [P, P])
        before = sb("before", [P, P])
        iota_s = sb("iota_s", [P, SLOTS])
        iota_e = sb("iota_e", [P, NE])
        iota_b = sb("iota_b", [P, MAXB])
        mhalf = sb("mhalf", [P, 1])
        epsc = sb("epsc", [P, 1])
        stat = sb("stat", [P, 24])
        wt = sb("wt", [P, 32, 2])
        topi = sb("topi", [P, TT, 8], U32)
        onehot = sb("onehot", [P, TT, SLOTS], BF16)
        table = sb("table", [1, MAXB + 1], I32)
        nblocks = sb("nblocks", [1, 2], I32)
        tabf = sb("tabf", [P, MAXB])
        bst = sb("bst", [P, TT, 6])
        bmv = sb("bmv", [P, TT, 4])

        upad = ubuf[:, :].rearrange("p (a b) -> p a b", a=KC)
        yret = ubuf[:, 0:KC * REAL].rearrange("p (a b) -> p a b", a=KC)

        flat = scratch[:, :]
        at = [0]

        def tmp(*shape):
            n = 1
            for s in shape:
                n *= s
            v = flat[:, at[0]:at[0] + n]
            at[0] += n
            assert at[0] <= 11268
            if len(shape) == 2:
                v = v.rearrange("p (a b) -> p a b", a=shape[0])
            return v

        decay = tmp(HEADS, TALL)
        cos = tmp(TALL)
        sin = tmp(TALL)
        early = at[0]
        qraw, kraw = tmp(2, REAL), tmp(2, TALL)
        qrot, krot = tmp(2, REAL), tmp(2, TALL)
        rc, rs = tmp(2, TALL), tmp(2, TALL)
        vT = tmp(VC, TALL)
        vsb = tmp(2, DV)
        vM = tmp(DV)
        sA, sB, sM = tmp(REAL), tmp(P), tmp(REAL)
        at[0] = max(at[0], early + 6 * D + 384)
        yn = tmp(TT, DV)
        sg = tmp(VC, REAL)
        cacc = tmp(2, REAL)
        sigb = tmp(2, TALL)
        dflat = flat[:, early:]
        hm = dflat[:, 0:D]
        xn = dflat[:, D:4 * D].rearrange("p (a b) -> p a b", a=3)
        wmb = dflat[:, 4 * D:5 * D]
        prow = dflat[:, 5 * D:5 * D + 384].rearrange("p (a b) -> p a b", a=3)
        junk1 = dflat[:, 5 * D + 384:6 * D + 384]
        sq = flat[:, 0:KC * REAL].rearrange("p (a b) -> p a b", a=KC)

        sga = rT[:, 0:KC, :]
        sgb = rT[:, KC:2 * KC, :]
        rflat = rT[:, :, :].rearrange("p a b -> p (a b)")
        lnd = flat[:, KC * REAL:(KC + 1) * REAL].rearrange("p (t n) -> p t n", t=TT)
        brows = rflat[0:3 * NE, 0:3 * D]
        gatehot = flat[:, 0:TT * SLOTS].rearrange("p (a b) -> p a b", a=TT)
        hg = flat[0:SLOTS, 256:256 + UNIT]
        hu = flat[0:SLOTS, 512:512 + UNIT]
        sig = flat[0:SLOTS, 768:768 + UNIT]
        act = flat[0:SLOTS, 1024:1024 + UNIT]
        pick = flat[:, 2048:3072]
        at[0] = 3072
        wr = tmp(KC, NE)
        brb, nblk, pend = tmp(NE), tmp(NE), tmp(NE)
        lg, mask, gdense, slot = (tmp(TT, NE) for _ in range(4))
        top, topf, gate4 = tmp(TT, 8), tmp(TT, TOPK), tmp(TT, TOPK)
        assert at[0] <= 4096
        xres = flat[:, 4096:4096 + TT * D].rearrange("p (a b) -> p a b", a=TT)
        x3 = flat[:, 8192:8192 + PARTS * TT * D // 2].bitcast(BF16).rearrange("p (q a b) -> p q a b", q=PARTS, a=TT)
        junk2 = rflat[:, 4096:5120]
        xn2 = yret[:, :, :].rearrange("p a b -> p (a b)").rearrange("p (a b) -> p a b", a=TT)
        xflat = xnT[:, :, :].rearrange("p a b -> p (a b)")[:, 0:KC * REAL]
        xn2T = xflat.rearrange("p (a b) -> p a b", a=KC)
        osb = xflat.rearrange("p (a b) -> p a b", a=TT)
        nwb = cv[:, :, :].rearrange("p a b -> p (a b)").rearrange("p (a b) -> p a b", a=2)

        x_in, meta_in, wmb_in = sem("x_in"), sem("meta_in"), sem("wmb_in")
        eid_in, par_in, bias_in, tab_in, rout_in, nwb_in = (sem(n) for n in ("eid_in", "par_in", "bias_in", "tab_in", "rout_in", "nwb_in"))
        landed = [sem(f"landed{s}") for s in range(6)]
        e_in = [sem(f"e_in{s}") for s in range(6)]
        consts = sem("consts")
        masked = sem("masked")
        cols = sem("cols")
        colse = sem("colse")
        a_full, b_full = sem("a_full"), sem("b_full")
        a_free, b_free = sem("a_free"), sem("b_free")
        sq_done, vr_done, pow_done, xn_done = (sem(n) for n in ("sq_done", "vr_done", "pow_done", "xn_done"))
        sig_done = sem("sig_done")
        conv_step = sem("conv_step")
        rope_done, pool_step = sem("rope_done"), sem("pool_step")
        vt_done, v_done = sem("vt_done"), sem("v_done")
        sc_done, s_done, y_done = sem("sc_done"), sem("s_done"), sem("y_done")
        gn_step, gv_done, gp_done, yn_done = sem("gn_step"), sem("gv_done"), sem("gp_done"), sem("yn_done")
        yt_done, rt_done = sem("yt_done"), sem("rt_done")
        xc_done, lsq_done, lnv_done, lnp_done, lnd_done, lnx_done, ln_done = (
            sem(n) for n in ("xc_done", "lsq_done", "lnv_done", "lnp_done", "lnd_done", "lnx_done", "ln_done"))
        yr_done, sga_done, sgb_done, gb_done, vm_done, merged = (
            sem(n) for n in ("yr_done", "sga_done", "sgb_done", "gb_done", "vm_done", "merged"))
        h2_done, x2t, x2e, lgt, route = sem("h2_done"), sem("x2t"), sem("x2e"), sem("lgt"), sem("route")
        shift_done, wt_done, route_step = sem("shift_done"), sem("wt_done"), sem("route_step")
        exp_done, rank_done, table_done = sem("exp_done"), sem("rank_done"), sem("table_done")
        w_used = sem("w_used")
        hi_done = sem("hi_done")
        lo_v, lo_p = sem("lo_v"), sem("lo_p")
        lgt_read = sem("lgt_read")
        min_rdy, clip_rdy, sig_rdy, prod_rdy, act_rdy = (
            sem(n) for n in ("min_rdy", "clip_rdy", "sig_rdy", "prod_rdy", "act_rdy"))
        turned, ahi_rdy, alo_rdy = sem("turned"), sem("ahi_rdy"), sem("alo_rdy")
        yhi_rdy, ylo_rdy, ght_done, ghi_rdy, glo_rdy = (
            sem(n) for n in ("yhi_rdy", "ylo_rdy", "ght_done", "ghi_rdy", "glo_rdy"))
        hot_rdy, gathered, xhi_rdy, xlo_rdy = sem("hot_rdy"), sem("gathered"), sem("xhi_rdy"), sem("xlo_rdy")
        gh_rdy, sel_rdy, slot_step = sem("gh_rdy"), sem("sel_rdy"), sem("slot_step")
        zeroed, x3_rdy, xr_rdy, b3_step = sem("zeroed"), sem("x3_rdy"), sem("xr_rdy"), sem("b3_step")
        acc_done, fin, out_rdy, out_in = sem("acc_done"), sem("fin"), sem("out_rdy"), sem("out_in")

        w_in = a["w_in"][0].rearrange("(k p) n -> p k n", p=P)
        w_co = a["w_conv_out"][0].rearrange("(k p) n -> p k n", p=P)
        w_ro = a["w_ret_out"][0].rearrange("(k p) n -> p k n", p=P)
        w_mo = a["w_mix_out"][0].rearrange("(k p) n -> p k n", p=P)
        w_gu = a["w_gate_up"][0]
        w_dn = a["w_down"][0]

        LAST = slice(0, HW // 2)

        def gate_src(e, q, up):
            c0 = (D if up else 0) + q * UNIT
            return w_gu[bass.ds(e, 1), :, c0:c0 + UNIT].rearrange("o (k p) n -> p (o k) n", p=P)

        def down_src(e, q):
            return w_dn[bass.ds(e, 1), q * UNIT:(q + 1) * UNIT, :].rearrange("o (k p) n -> p (o k) n", p=P)

        def lo_count(b, k):
            q, h = divmod(k, HALVES)
            return 20 * b + (5 * q + h + 1) if h < 4 else 8 * b + (2 * q + h - 3)

        UC = D // UNIT
        U_A, U_B = 0, UC
        U_Q, U_K, U_V, U_G, U_GA, U_GB = 2 * UC, 3 * UC, 4 * UC, 6 * UC, 8 * UC, 9 * UC

        RET = ((4, 5), (2, 5), (0, 9), (4, 6))
        GATES = ((2, 6), (0, 10), (4, 7), (2, 7))
        CONV = ((0, 11), (4, 8))
        MIX = ((2, 8), (4, 9))

        def raw_half(k):
            return ring[:, k // 2 % 6, :, :].rearrange("p a b -> p (a b)")[:, k % 2 * HW:(k % 2 + 1) * HW]

        block = ctx.enter_context(nc.Block())


        @block.sync
        def _(sp):
            def load(s, src, u):
                cols_ = slice(u * UNIT, u * UNIT + UNIT) if isinstance(u, int) else bass.ds(u * UNIT, UNIT)
                sp.dma_start(ring[:, s, :, :], src[:, :, cols_]).then_inc(landed[s], 16)

            xr = a["x"][0].rearrange("(t p) n -> p t n", p=P)
            sp.dma_start(hm[0:META, :], a["meta_tokens"]).then_inc(meta_in, 16)
            sp.dma_start(hx[:, 0, :], xr[:, 0, :]).then_inc(x_in, 16)
            sp.dma_start(wmb, a["norm_mix_w"][0:1, :].to_broadcast([P, D])).then_inc(wmb_in, 16)
            sp.dma_start(hx[:, 1, :], xr[:, 1, :]).then_inc(x_in, 16)
            load(0, w_in, U_A)
            load(1, w_in, U_B)
            load(2, w_in, U_Q)
            load(3, w_in, U_K)
            load(4, w_in, U_V)
            load(5, w_in, U_V + 1)
            with sp.Fori(1, 4) as i:
                sp.wait_ge(a_full, 2 * i)
                load(0, w_in, i + U_A)
                sp.wait_ge(b_full, 2 * i)
                load(1, w_in, i + U_B)
            sp.wait_ge(a_full, 8)
            load(0, w_in, U_G)
            sp.wait_ge(b_full, 8)
            load(1, w_in, U_G + 1)
            with sp.Fori(1, HEADS) as h:
                sp.wait_ge(a_full, 6 * h + 4)
                load(2, w_in, h + U_Q)
                sp.wait_ge(b_full, 6 * h + 4)
                load(3, w_in, h + U_K)
                sp.wait_ge(a_full, 6 * h + 6)
                load(4, w_in, 2 * h + U_V)
                sp.wait_ge(b_full, 6 * h + 6)
                load(5, w_in, 2 * h + (U_V + 1))
                sp.wait_ge(a_full, 6 * h + 8)
                load(0, w_in, 2 * h + U_G)
                sp.wait_ge(b_full, 6 * h + 8)
                load(1, w_in, 2 * h + (U_G + 1))
            def unit(e_prev, e, j):
                q, kind = divmod(j, 3)
                dst = ring[:, j % 6, :, :]
                if kind == 2:
                    dst = dst.rearrange("p a b -> p (a b)").rearrange("p (a b) -> p a b", a=2)
                src = gate_src(e, q, kind) if kind < 2 else down_src(e if q else e_prev, q - 1 if q else STEPS - 1)
                sp.dma_start(dst, src).then_inc(e_in[j % 6], 16)

            def pair(slots, srcs, units, full_a, full_b):
                for c in range(2):
                    sp.wait_ge(a_full if c == 0 or not full_b else b_full, full_b if c and full_b else full_a)
                    load(slots + c, srcs[c], units[c])

            ret = (w_ro[:, 0:KC, :], w_ro[:, KC:2 * KC, :])
            pair(RET[0][0], ret, (0, 0), 30, 30)
            pair(RET[1][0], ret, (1, 1), 28, 28)
            pair(RET[2][0], ret, (2, 2), 32, 32)
            pair(RET[3][0], ret, (3, 3), 34, None)
            pair(GATES[0][0], (w_in, w_in), (U_GA, U_GB), 36, None)
            pair(GATES[1][0], (w_in, w_in), (U_GA + 1, U_GB + 1), 38, None)
            pair(GATES[2][0], (w_in, w_in), (U_GA + 2, U_GB + 2), 40, None)
            pair(GATES[3][0], (w_in, w_in), (U_GA + 3, U_GB + 3), 42, 40)
            pair(CONV[0][0], (w_co, w_co), (0, 1), 44, 42)
            pair(CONV[1][0], (w_co, w_co), (2, 3), 46, 44)
            pair(MIX[0][0], (w_mo, w_mo), (0, 1), 48, 46)
            sp.wait_ge(a_full, 50)
            sp.wait_ge(b_full, 48)
            unit(0, 0, 0)
            unit(0, 0, 1)
            pair(MIX[1][0], (w_mo, w_mo), (2, 3), 52, 50)
            sp.dma_start(wr, a["w_router"][0].rearrange("(k p) n -> p k n", p=P)).then_inc(rout_in, 16)
            sp.dma_start(brb, a["b_router"][0:1, :].to_broadcast([P, NE])).then_inc(rout_in, 16)
            sp.dma_start(nwb[:, 0, :], a["norm_ffn_w"][0:1, :].to_broadcast([P, D])).then_inc(nwb_in, 16)
            sp.dma_start(nwb[:, 1, :], a["norm_final_w"].rearrange("(o n) -> o n", o=1)[0:1, :]
                         .to_broadcast([P, D])).then_inc(nwb_in, 16)

            def slot_free(b, j):
                k = 2 * (j - 6) + 1
                if j % 3 == 2:
                    sp.wait_ge(w_used, 24 * b + (HS + k + 1))
                else:
                    sp.wait_ge(lo_v, lo_count(b, k))

            sp.wait_ge(a_full, 54)
            unit(0, 0, 2)
            unit(0, 0, 3)
            sp.wait_ge(b_full, 52)
            unit(0, 0, 4)
            unit(0, 0, 5)
            sp.wait_ge(table_done, 4)
            nb = sp.value_load(nblocks[0:1, 0:1], min_val=NE, max_val=MAXB - 1)
            before_last = sp.value_load(nblocks[0:1, 1:2], min_val=NE - 1, max_val=MAXB - 2)
            with sp.Fori(0, before_last) as b:
                e0 = sp.value_load(table[0:1, bass.ds(b + 1, 1)], min_val=0, max_val=NE - 1)
                e1 = sp.value_load(table[0:1, bass.ds(b + 2, 1)], min_val=0, max_val=NE - 1)
                for j in range(6, 18):
                    slot_free(b, j)
                    unit(e0, e0 if j < 12 else e1, j % 12)
            el = sp.value_load(table[0:1, bass.ds(nb, 1)], min_val=0, max_val=NE - 1)
            for j in range(6, 12):
                slot_free(before_last, j)
                unit(el, el, j)
            slot_free(before_last, 14)
            unit(el, el, 2)
            outr = out[0].rearrange("(t p) n -> p t n", p=P)
            for t in range(TT):
                sp.wait_ge(out_rdy, t + 1)
                sp.dma_start(outr[:, t, :], osb[:, t, :]).then_inc(out_in, 16)
            sp.wait_ge(out_in, 16 * TT)

        @block.gpsimd
        def _(pool):
            pool.memset(ident[:, :], 0.0).then_inc(consts, 1)
            pool.memset(ones[:, :], 1.0).then_inc(consts, 1)
            pool.memset(before[:, :], 1.0).then_inc(consts, 1)
            pool.memset(mhalf[:, :], -0.5).then_inc(consts, 1)
            pool.wait_ge(consts, 3)
            pool.affine_select(out=ident[:, :], in_=ident[:, :], compare_op=ALU.not_equal, fill=1.0,
                               base=0, pattern=[[-1, P]], channel_multiplier=1).then_inc(masked, 1)
            pool.affine_select(out=before[:, :], in_=before[:, :], compare_op=ALU.is_gt, fill=0.0,
                               base=0, pattern=[[1, P]], channel_multiplier=-1).then_inc(masked, 1)
            pool.iota(iota_s[:, :], [[1, SLOTS]], base=0, channel_multiplier=0,
                      allow_small_or_imprecise_dtypes=True).then_inc(consts, 1)
            pool.iota(iota_e[:, :], [[1, NE]], base=0, channel_multiplier=0,
                      allow_small_or_imprecise_dtypes=True).then_inc(consts, 1)
            pool.iota(iota_b[:, :], [[1, MAXB]], base=0, channel_multiplier=0,
                      allow_small_or_imprecise_dtypes=True).then_inc(consts, 1)
            pool.memset(upad[:, :, 0:PADL], 0.0).then_inc(consts, 1)
            pool.memset(sg[:, :, :], 0.0).then_inc(consts, 1)
            pool.memset(yn[:, :, :], 0.0).then_inc(yn_done, 1)
            pool.memset(stat[:, 18:20], 0.0).then_inc(rope_done, 1)

            def rsqrt(o, v, n):
                return pool.tensor_tensor(o, v, mhalf[0:v.shape[0], 0:1].to_broadcast([v.shape[0], n]), ALU.pow)

            pool.wait_ge(consts, 4)
            for t in range(3):
                rows = META if t == 2 else P
                pool.wait_ge(vr_done, t + 1)
                rsqrt(stat[0:rows, 6 + t:7 + t], stat[0:rows, 3 + t:4 + t], 1).then_inc(pow_done, 1)

            pool.wait_ge(bias_in, 16 * 6)
            b3 = Chain(pool, b3_step)

            def do(ins):
                b3.did(ins)
                b3.wait()

            last = slice(2 * NE, 3 * NE)
            do(pool.tensor_copy(bias3[0:3 * NE, :], brows))
            do(pool.tensor_tensor(brows, brows, bias3[0:3 * NE, :], ALU.subtract))
            do(pool.tensor_copy(bias3[NE:2 * NE, :], brows[NE:2 * NE, :]))
            do(pool.tensor_copy(bias3[last, :], brows[last, :]))
            do(pool.tensor_tensor(brows[last, :], brows[last, :], bias3[last, :], ALU.subtract))
            do(pool.tensor_copy(bias3[last, :], brows[last, :]))

            pool.wait_ge(tab_in, 48)
            step = Chain(pool, pool_step)
            with pool.Fori(0, HEADS) as h:
                step.enter(h, 6)
                for which, (raw, rot, n) in enumerate(((qraw, qrot, REAL), (kraw, krot, TALL))):
                    t0 = TALL - n
                    c_ = cos[:, t0:TALL].rearrange("p (o n) -> p o n", o=1).to_broadcast([P, 2, n])
                    pool.wait_ge((a_free, b_free)[which], 6 * h + 12)
                    if which:
                        step.wait()
                        pool.wait_ge(rope_done, 2 * h + 2)
                    else:
                        pool.wait_ge(rope_done, 2 * h + 1)
                    step.did(pool.tensor_tensor(rc[:, :, 0:n], raw[:, :, :], c_, ALU.mult))
                    step.did(pool.tensor_tensor(rs[:, 0, 0:n], raw[:, 1, :], sin[:, t0:TALL], ALU.mult))
                    step.did(pool.tensor_tensor(rs[:, 1, 0:n], raw[:, 0, :], sin[:, t0:TALL], ALU.mult))
                    step.wait()
                    pool.tensor_tensor(rot[:, 0, :], rc[:, 0, 0:n], rs[:, 0, 0:n], ALU.subtract)
                    pool.tensor_tensor(rot[:, 1, :], rc[:, 1, 0:n], rs[:, 1, 0:n], ALU.add).then_inc(rope_done, 1)
                pool.wait_ge(gv_done, h + 1)
                rsqrt(stat[:, 18:20], stat[:, 16:18], 2).then_inc(gp_done, 1)
            step.leave(HEADS)
            pool.wait_ge(lnv_done, 2)
            rsqrt(stat[:, 18:20], stat[:, 16:18], TT).then_inc(lnp_done, 1)
            for t in range(TT):
                pool.wait_ge(vr_done, 4 + t)
                rsqrt(stat[:, 6 + t:7 + t], stat[:, 3 + t:4 + t], 1).then_inc(pow_done, 1)
            pool.wait_ge(x3_rdy, TT + 1)
            pool.tensor_tensor(xres[:, :, :], xres[:, :, :], x3[:, 1, :, :], ALU.subtract).then_inc(xr_rdy, 1)
            pool.wait_ge(table_done, 4)
            nb = pool.value_load(nblocks[0:1, 0:1], min_val=NE, max_val=MAXB - 1)

            def low(b, k):
                cols_ = slice(HW // 2, HW) if k % HALVES == 5 else slice(0, HW)
                pool.wait_ge(hi_done, 24 * b + (k + 1))
                pool.tensor_tensor(wlo[:, k % HS, cols_], raw_half(k)[:, cols_], whi[:, k % HS, cols_].bitcast(F32),
                                   ALU.subtract).then_inc(lo_p, 1)

            with pool.Fori(0, nb) as b:
                for k in range(STEPS * HALVES):
                    if k % HALVES > 3:
                        low(b, k)
            for c, cols_ in enumerate((slice(0, HW), slice(HW // 2, HW))):
                pool.wait_ge(hi_done, 24 * nb + (c + 1))
                pool.tensor_tensor(wlo[:, c, cols_], raw_half(4 + c)[:, cols_], whi[:, c, cols_].bitcast(F32),
                                   ALU.subtract).then_inc(lo_p, 1)
            for t in range(TT):
                pool.wait_ge(vr_done, 6 + t)
                rsqrt(stat[:, 6 + t:7 + t], stat[:, 3 + t:4 + t], 1).then_inc(pow_done, 1)

        @block.tensor
        def _(pe):
            def copyT(o, i, n):
                return pe.transpose(o, i, ident[0:n, 0:n])

            pe.wait_ge(masked, 2)
            pe.wait_ge(par_in, 16 * 7)
            for r, n in enumerate((P, P, NPAR - 2 * P)):
                copyT(pb[:, 0, r * P:r * P + n], prow[0:n, r, :], n).then_inc(cols, 1)
            for t in (0, 1, 2):
                pe.wait_ge(xn_done, t + 1)
                n = META if t == 2 else P
                for k in range(KC):
                    o = pb[:, 1, k * META:(k + 1) * META] if t == 2 else pb[:, 4 + 2 * t + k // 4, (k % 4) * P:(k % 4 + 1) * P]
                    ins = copyT(o, xn[0:n, t, k * P:(k + 1) * P], n)
                ins.then_inc(cols, 1)
            pe.wait_ge(colse, 3)

            def project(s, use, fill, bank, t0, free, full, rhs=None):
                pe.wait_ge(landed[s], 16 * use)
                pe.wait_ge(free, 2 * fill)
                for j in range(2):
                    for k in range(KC):
                        mv = xnT[:, k, t0:TALL] if rhs is None else rhs[:, k, :]
                        ins = pe.matmul(pb[:, bank + j, 0:TALL - t0], ring[:, s, k, j * P:(j + 1) * P], mv,
                                        start=(k == 0), stop=(k == KC - 1))
                    ins.then_inc(full, 1)

            with pe.Fori(0, 4) as i:
                project(0, i + 1, i + 1, 0, 0, a_free, a_full)
                project(1, i + 1, i + 1, 2, 0, b_free, b_full)

            def turn_y(h1):
                pe.wait_ge(yn_done, 2 * h1 - 1)
                for c in range(VC):
                    for t in range(TT):
                        ins = copyT(pb[:, 4 + 3 * (c // 2), (c % 2) * REAL + t * P:(c % 2) * REAL + (t + 1) * P],
                                    yn[:, t, c * P:(c + 1) * P], P)
                    ins.then_inc(yt_done, 1)

            with pe.Fori(0, HEADS) as h:
                project(2, h + 1, 3 * h + 5, 0, META, a_free, a_full)
                project(3, h + 1, 3 * h + 5, 2, 0, b_free, b_full)
                project(4, h + 1, 3 * h + 6, 0, 0, a_free, a_full)
                turn_y(h + 1)
                project(5, h + 1, 3 * h + 6, 2, 0, b_free, b_full)
                project(0, h + 5, 3 * h + 7, 0, META, a_free, a_full)
                pe.wait_ge(a_free, 6 * h + 14)
                pe.wait_ge(b_free, 6 * h + 14)
                pe.wait_ge(rt_done, 4 * h + 4)
                for bank, t0, n in ((4, META, P), (5, META + P, P), (6, 0, META)):
                    for c in range(VC):
                        ins = copyT(pb[0:n, bank, c * P:(c + 1) * P], vT[:, c, t0:t0 + n], P)
                    ins.then_inc(vt_done, 1)
                pe.wait_ge(rope_done, 2 * h + 3)
                for c in range(2):
                    ins = pe.matmul(pb[:, 7, 0:REAL], krot[:, c, META:META + P], qrot[:, c, :],
                                    start=(c == 0), stop=(c == 1))
                ins.then_inc(sc_done, 1)
                for c in range(2):
                    ins = pe.matmul(pb[0:META, 7, REAL:2 * REAL], krot[:, c, 0:META], qrot[:, c, :],
                                    start=(c == 0), stop=(c == 1))
                ins.then_inc(sc_done, 1)
                project(1, h + 5, 3 * h + 7, 2, META, b_free, b_full)
                pe.wait_ge(v_done, 3 * h + 3)
                for c in range(2):
                    ins = pe.matmul(pb[:, 4, 0:P], krot[:, c, META + P:TALL], qrot[:, c, P:REAL],
                                    start=(c == 0), stop=(c == 1))
                ins.then_inc(sc_done, 1)
                pe.wait_ge(s_done, 3 * h + 2)
                pe.matmul(pb[:, 5, :], sM[0:META, 0:P], vM[0:META, :], start=True, stop=False)
                pe.matmul(pb[:, 5, :], sA[:, 0:P], vsb[:, 0, :], start=False, stop=True).then_inc(y_done, 1)
                pe.matmul(pb[:, 6, :], sM[0:META, P:REAL], vM[0:META, :], start=True, stop=False)
                pe.matmul(pb[:, 6, :], sA[:, P:REAL], vsb[:, 0, :], start=False, stop=False)
                pe.wait_ge(s_done, 3 * h + 3)
                pe.matmul(pb[:, 6, :], sB[:, 0:P], vsb[:, 1, :], start=False, stop=True).then_inc(y_done, 1)

            def channel_sum(src, fill):
                pe.wait_ge(b_free, 2 * fill)
                for k in range(KC):
                    ins = pe.matmul(pb[:, 2, 0:REAL], ones[:, :], src[:, k, :], start=(k == 0), stop=(k == KC - 1))
                    if k in (0, KC - 1):
                        ins.then_inc(b_full, 1)

            pe.wait_ge(conv_step, 4 * 62)
            channel_sum(cv, 17)
            turn_y(HEADS + 1)
            pe.wait_ge(rt_done, 4 * (HEADS + 1))
            for r in range(UC):
                s0, use = RET[r]
                pe.wait_ge(landed[s0], 16 * use)
                pe.wait_ge(landed[s0 + 1], 16 * use)
                pe.wait_ge(a_free, 2 * (r + 17))
                for j in range(2):
                    for k in range(2 * KC):
                        ins = pe.matmul(pb[:, j, 0:REAL], ring[:, s0 + k // KC, k % KC, j * P:(j + 1) * P],
                                        rT[:, VC + k, :], start=(k == 0), stop=(k == 2 * KC - 1))
                    ins.then_inc(a_full, 1)
                if r == 0:
                    pe.wait_ge(lsq_done, 1)
                    channel_sum(sq, 18)
                if r == 1:
                    pe.wait_ge(lnd_done, 1)
                    pe.wait_ge(b_free, 2 * 19)
                    pe.matmul(pb[:, 2, 0:REAL], ones[:, :], lnd, start=True, stop=True).then_inc(b_full, 2)
            for g in range(UC):
                s0, use = GATES[g]
                project(s0, use, g + 21, 0, META, a_free, a_full)
                project(s0 + 1, use, g + 20, 2, META, b_free, b_full)
            pe.wait_ge(ln_done, KC)
            for i in range(2):
                s0, use = CONV[i]
                project(s0, use, i + 25, 0, META, a_free, a_full, cv)
                project(s0 + 1, use, i + 24, 2, META, b_free, b_full, cv)
            pe.wait_ge(merged, KC)
            pe.wait_ge(a_free, 2 * 27)
            pe.wait_ge(b_free, 2 * 26)
            for n in range(UC):
                s0, use = MIX[n // 2]
                pe.wait_ge(landed[s0 + n % 2], 16 * use)
                for t in range(TT):
                    for k in range(KC):
                        ins = pe.matmul(pb[:, n, t * UNIT:(t + 1) * UNIT], yret[:, k, t * P:(t + 1) * P],
                                        ring[:, s0 + n % 2, k, :], start=(k == 0), stop=(k == KC - 1))
                ins.then_inc((a_full, b_full)[n // 2], 1)
            for t in range(TT):
                pe.wait_ge(xn_done, 4 + t)
                for k in range(KC):
                    ins = copyT(pb[:, 4 + 2 * t + k // 4, (k % 4) * P:(k % 4 + 1) * P], xn2[:, t, k * P:(k + 1) * P], P)
                ins.then_inc(x2t, 1)
            pe.wait_ge(rout_in, 32)
            for t in range(TT):
                pe.wait_ge(x2e, t + 1)
                for k in range(KC):
                    ins = pe.matmul(pb[:, 4 + t, 0:NE], xn2T[:, k, t * P:(t + 1) * P], wr[:, k, :],
                                    start=(k == 0), stop=(k == KC - 1))
                ins.then_inc(lgt, 1)
            pe.wait_ge(route, 2)
            pe.wait_ge(lgt_read, 2)
            pe.matmul(pb[:, 6, 0:NE], before[:, :], mask[:, 0, :], start=True, stop=True).then_inc(w_used, 1)
            pe.matmul(pb[:, 6, NE:2 * NE], before[:, :], mask[:, 1, :], start=True, stop=False).then_inc(w_used, 1)
            pe.matmul(pb[:, 6, NE:2 * NE], ones[:, :], mask[:, 0, :], start=False, stop=True).then_inc(w_used, 1)
            pe.matmul(pb[:, 6, 2 * NE:3 * NE], ones[:, :], mask[:, 0, :], start=True, stop=False).then_inc(w_used, 1)
            pe.matmul(pb[:, 6, 2 * NE:3 * NE], ones[:, :], mask[:, 1, :], start=False, stop=True).then_inc(rank_done, 1)

            def gather():
                for k in range(KC):
                    for n in range(PARTS * TT):
                        ins = pe.matmul(pb[:, 7, k * SLOTS:(k + 1) * SLOTS], x3[:, n % PARTS, n // PARTS, k * P:(k + 1) * P],
                                        onehot[:, n // PARTS, :], start=(n == 0), stop=(n == PARTS * TT - 1))
                ins.then_inc(gathered, 1)

            def split_product(pairs, stop):
                ins = None
                for m, (x, y) in enumerate(((0, 0), (0, 1), (1, 0))):
                    for o, st, mv in pairs:
                        ins = pe.matmul(o, st[x], mv[y], start=False, stop=(stop and m == 2), skip_group_check=True)
                return ins

            def low_ready(b, k):
                pe.wait_ge(lo_v if k % HALVES < 4 else lo_p, lo_count(b, k))

            def hidden(b, k, stop):
                up = k % HALVES // 2
                low_ready(b, k)
                for r in range(KC // 2):
                    c = k % 2 * (KC // 2) + r
                    mv = [w[:, k % HS, r * UNIT:(r + 1) * UNIT] for w in (whi, wlo)]
                    ins = split_product([(pb[0:SLOTS, 4, up * UNIT:(up + 1) * UNIT], (xhi[:, c, :], xlo[:, c, :]), mv)],
                                        stop and r == KC // 2 - 1)
                ins.then_inc(w_used, 1)

            def down(k, stop):
                st = (ahi[:, k % 2, :], alo[:, k % 2, :])
                split_product([(pb[0:SLOTS, 5 + c, :], st, [w[:, k % HS, c * 512:(c + 1) * 512] for w in (whi, wlo)])
                               for c in range(2)], stop).then_inc(w_used, 1)

            def turn_act(n):
                pe.wait_ge(act_rdy, n + 1)
                for c in range(2):
                    ins = pe.matmul(pb[:, 7, c * SLOTS:(c + 1) * SLOTS], act[:, c * P:(c + 1) * P],
                                    ident[0:SLOTS, 0:SLOTS], start=True, stop=True)
                ins.then_inc(turned, 1)

            def turn_gates():
                for t in range(TT):
                    ins = pe.matmul(pb[0:SLOTS, 7, t * P:(t + 1) * P], gatehot[:, t, :], ident[:, :],
                                    start=True, stop=True)
                ins.then_inc(ght_done, 1)

            def scatter(stop):
                for t in range(TT):
                    st = (ghi[:, t * P:(t + 1) * P], glo[:, t * P:(t + 1) * P])
                    ins = split_product([(pb[:, 2 * t + c, :], st, (yhi[:, c * 512:(c + 1) * 512], ylo[:, c * 512:(c + 1) * 512]))
                                         for c in range(2)], stop)
                return ins

            pe.wait_ge(x3_rdy, TT + PARTS - 1)
            pe.wait_ge(hot_rdy, 2)
            gather()
            pe.wait_ge(h2_done, 4)
            for t in range(TT):
                for c in range(2):
                    pe.matmul(pb[:, 2 * t + c, :], ident[:, :], hx[:, t, c * 512:(c + 1) * 512],
                              start=True, stop=False, skip_group_check=True)
            pe.wait_ge(b3_step, 6)
            pe.wait_ge(zeroed, 1)
            pe.wait_ge(gh_rdy, 1)
            pe.wait_ge(xlo_rdy, 1)
            turn_gates()
            pe.wait_ge(table_done, 4)
            nb = pe.value_load(nblocks[0:1, 0:1], min_val=NE, max_val=MAXB - 1)
            with pe.Fori(0, nb) as b:
                for q in range(STEPS):
                    k = q * HALVES
                    if q == 0:
                        pe.wait_ge(xlo_rdy, b + 1)
                        pe.wait_ge(sel_rdy, b + 1)
                    pe.wait_ge(clip_rdy, 4 * b + (q + 1))
                    pe.matmul(pb[0:SLOTS, 4, :], pick_e[:, :],
                              bias3[:, 0:2 * D].rearrange("p (u n) -> p u n", u=2)[:, :, q * UNIT:(q + 1) * UNIT],
                              start=True, stop=False, skip_group_check=True)
                    hidden(b, k, False)
                    hidden(b, k + 1, True)
                    if q == 0:
                        pe.wait_ge(glo_rdy, b + 1)
                    turn_act(4 * b + (q + 1))
                    hidden(b, k + 2, False)
                    hidden(b, k + 3, True)
                    if q == 3:
                        pe.wait_ge(hot_rdy, 2 * b + 4)
                        pe.wait_ge(alo_rdy, 4 * b + (q + 1))
                        gather()
                        pe.wait_ge(glo_rdy, b + 1)
                        pe.wait_ge(ylo_rdy, b + 1)
                        scatter(False)
                    pe.wait_ge(alo_rdy, 4 * b + (q + 1))
                    if q == 1:
                        pe.wait_ge(ylo_rdy, b + 1)
                        for c in range(2):
                            pe.matmul(pb[0:SLOTS, 5 + c, :], pick_e[:, :], bias3[:, 2 * D + c * 512:2 * D + (c + 1) * 512],
                                      start=True, stop=False, skip_group_check=True)
                    low_ready(b, k + 4)
                    down(k + 4, False)
                    pe.wait_ge(lo_v, 20 * b + (5 * q + 5))
                    low_ready(b, k + 5)
                    down(k + 5, q == 0)
                    if q == 3:
                        pe.wait_ge(gh_rdy, 2 * b + 3)
                        pe.wait_ge(xlo_rdy, b + 2)
                        turn_gates()
            pe.wait_ge(glo_rdy, nb + 1)
            turn_act(4 * nb + 1)
            pe.wait_ge(alo_rdy, 4 * nb + 1)
            pe.wait_ge(lo_p, 8 * nb + 1)
            down(4, False)
            pe.wait_ge(lo_v, 20 * nb + 1)
            pe.wait_ge(lo_p, 8 * nb + 2)
            down(5, True)
            pe.wait_ge(ylo_rdy, nb + 1)
            scatter(True).then_inc(acc_done, 1)

        @block.scalar
        def _(sc):
            rows = {0: a["conv_dw_w"][0].rearrange("w (c p) -> (w c) p", p=P)}
            sc.dma_start(prow[:, 0, :], rows[0][0:P, :]).then_inc(par_in, 16)
            sc.dma_start(prow[0:TAPS * KC - P, 1, :], rows[0][P:TAPS * KC, :]).then_inc(par_in, 16)
            for name, r0, n in (("conv_dw_b", TAPS * KC, KC), ("conv_ln_w", LNW, KC), ("conv_ln_b", LNB, KC),
                                ("b_conv_out", BCO, KC), ("ret_gn_w", GNW, 4 * VC)):
                sc.dma_start(prow[r0 % P:r0 % P + n, r0 // P, :],
                             a[name][0].rearrange("(c p) -> c p", p=P)).then_inc(par_in, 16)
            for q in range(3):
                sc.dma_start(brows[q * NE:(q + 1) * NE, 0:2 * D], a["b_gate_up"][0]).then_inc(bias_in, 16)
                sc.dma_start(brows[q * NE:(q + 1) * NE, 2 * D:3 * D], a["b_down"][0]).then_inc(bias_in, 16)
            sc.dma_start(eid[:, :], a["eid"]).then_inc(eid_in, 16)
            sc.dma_start(decay[:, :, :], a["decay"]).then_inc(tab_in, 16)
            sc.dma_start(cos, a["cos"]).then_inc(tab_in, 16)
            sc.dma_start(sin, a["sin"]).then_inc(tab_in, 16)

            for t in range(3):
                rows_ = META if t == 2 else P
                if t == 2:
                    sc.wait_ge(meta_in, 16)
                else:
                    sc.wait_ge(x_in, 32)
                if t:
                    sc.wait_ge(sq_done, t)
                sc.activation(junk1[0:rows_, :], hm[0:META, :] if t == 2 else hx[:, t, :], ACT.Square,
                              accum_out=stat[0:rows_, t:t + 1]).then_inc(sq_done, 1)
            sc.wait_ge(cols, 3)
            sc.activation(par[:, 0:P], pb[:, 0, 0:P], ACT.Copy).then_inc(a_free, 1)
            sc.activation(par[:, P:NPAR], pb[:, 0, P:NPAR], ACT.Copy).then_inc(a_free, 1)
            for t in range(3):
                sc.wait_ge(cols, 4 + t)
                if t < 2:
                    src = pb[:, 4 + 2 * t:6 + 2 * t, :].rearrange("p b (k n) -> p (b k) n", n=P)
                    dst = xnT[:, :, META + t * P:META + (t + 1) * P]
                else:
                    src = pb[:, 1, 0:KC * META].rearrange("p (k n) -> p k n", n=META)
                    dst = xnT[:, :, 0:META]
                sc.activation(dst, src, ACT.Copy).then_inc(colse, 1)

            with sc.Fori(0, 4) as i:
                for j in range(2):
                    sc.wait_ge(b_full, 2 * i + (1 + j))
                    if j == 0:
                        sc.wait_ge(a_free, 2 * i + 2)
                    sc.activation(sigb[:, j, :], pb[:, 2 + j, 0:TALL], ACT.Sigmoid).then_inc(b_free, 1)

            with sc.Fori(0, HEADS) as h:
                sc.wait_ge(rope_done, 2 * h + 1)
                for j in range(2):
                    sc.wait_ge(a_full, 6 * h + (9 + j))
                    sc.activation(qraw[:, j, :], pb[:, j, 0:REAL], ACT.Copy).then_inc(a_free, 1)
                for j in range(2):
                    sc.wait_ge(b_full, 6 * h + (9 + j))
                    sc.activation(kraw[:, j, :], pb[:, 2 + j, 0:TALL], ACT.Copy).then_inc(b_free, 1)
                for j in range(VC):
                    sc.wait_ge((a_full, b_full)[j // 2], 6 * h + (11 + j % 2))
                    sc.activation(vT[:, j, :], pb[:, j, 0:TALL], ACT.Copy).then_inc((a_free, b_free)[j // 2], 1)
                sc.wait_ge(rt_done, 4 * h + 4)
                for j in range(2):
                    sc.wait_ge(a_full, 6 * h + (13 + j))
                    sc.activation(sg[:, j, :], pb[:, j, 0:REAL], ACT.Silu).then_inc(a_free, 1)
                sc.wait_ge(vt_done, 3 * h + 1)
                sc.activation(vsb[:, 0, :], pb[:, 4, :], ACT.Copy).then_inc(v_done, 1)
                sc.wait_ge(vt_done, 3 * h + 2)
                sc.activation(vsb[:, 1, :], pb[:, 5, :], ACT.Copy).then_inc(v_done, 1)
                sc.wait_ge(vt_done, 3 * h + 3)
                sc.activation(vM[0:META, :], pb[0:META, 6, :], ACT.Copy).then_inc(v_done, 1)
                for j in range(2):
                    sc.wait_ge(b_full, 6 * h + (13 + j))
                    sc.activation(sg[:, 2 + j, :], pb[:, 2 + j, 0:REAL], ACT.Silu).then_inc(b_free, 1)

            sc.wait_ge(xc_done, 2)
            sc.activation(sq, cv[:, :, :], ACT.Square).then_inc(lsq_done, 1)
            with sc.Fori(0, UC) as r:
                for j in range(2):
                    sc.wait_ge(a_full, 2 * r + (33 + j))
                    sc.activation(yret[:, bass.ds(2 * r + j, 1), :], pb[:, j:j + 1, 0:REAL], ACT.Copy).then_inc(a_free, 1)
            for k in range(KC):
                sc.wait_ge(lnx_done, 1 + k // (KC // 2))
                sc.activation(cv[:, k, :], cv[:, k, :], ACT.Silu, scale=par[:, LNW + k:LNW + k + 1],
                              bias=par[:, LNB + k:LNB + k + 1]).then_inc(ln_done, 1)
            with sc.Fori(0, UC) as g:
                for j in range(2):
                    sc.wait_ge(a_full, 2 * g + (41 + j))
                    sc.activation(sga[:, bass.ds(2 * g + j, 1), :], pb[:, j:j + 1, 0:REAL], ACT.Sigmoid).then_inc(a_free, 1)
                for j in range(2):
                    sc.wait_ge(b_full, 2 * g + (39 + j))
                    sc.activation(sgb[:, bass.ds(2 * g + j, 1), :], pb[:, 2 + j:3 + j, 0:REAL], ACT.Sigmoid).then_inc(b_free, 1)

            sc.wait_ge(h2_done, 4)
            for t in range(TT):
                if t:
                    sc.wait_ge(sq_done, 3 + t)
                sc.activation(junk2, hx[:, t, :], ACT.Square, accum_out=stat[:, t:t + 1]).then_inc(sq_done, 1)
            for t in range(TT):
                sc.wait_ge(xn_done, 4 + t)
                sc.activation(x3[:, 0, t, :], xn2[:, t, :], ACT.Copy).then_inc(x3_rdy, 1)
            for t in range(TT):
                sc.wait_ge(x2t, t + 1)
                sc.activation(xn2T[:, :, t * P:(t + 1) * P],
                              pb[:, 4 + 2 * t:6 + 2 * t, :].rearrange("p b (k n) -> p (b k) n", n=P),
                              ACT.Copy).then_inc(x2e, 1)
            sc.wait_ge(xr_rdy, 1)
            sc.activation(x3[:, 1, :, :], xres[:, :, :], ACT.Copy).then_inc(x3_rdy, 1)
            for t in range(TT):
                sc.wait_ge(shift_done, t + 1)
                sc.activation(gate4[:, t, :], gate4[:, t, :], ACT.Exp, accum_out=stat[:, 10 + t:11 + t]).then_inc(exp_done, 1)
            sc.wait_ge(xr_rdy, 2)
            sc.activation(x3[:, 2, :, :], xres[:, :, :], ACT.Copy).then_inc(x3_rdy, 1)

            def tokens(n):
                sc.wait_ge(gathered, n)
                sc.activation(xhi[:, :, :], pb[:, 7, :].rearrange("p (k n) -> p k n", n=SLOTS), ACT.Copy).then_inc(xhi_rdy, 1)

            tokens(1)
            sc.wait_ge(table_done, 4)
            nb = sc.value_load(nblocks[0:1, 0:1], min_val=NE, max_val=MAXB - 1)

            def high(b, k):
                if k % 2 == 0:
                    sc.wait_ge(e_in[k // 2 % 6], 32 * b + 16 * (1 + k // 12))
                sc.wait_ge(w_used, 24 * b + (k + 1))
                sc.activation(whi[:, k % HS, :], raw_half(k), ACT.Copy).then_inc(hi_done, 1)

            def sigmoid(n):
                sc.wait_ge(min_rdy, n)
                sc.activation(sig, hg, ACT.Sigmoid, scale=ALPHA).then_inc(sig_rdy, 1)

            def act_high(n):
                sc.wait_ge(turned, n)
                sc.activation(ahi[:, :, :], pb[:, 7, 0:2 * SLOTS].rearrange("p (k n) -> p k n", n=SLOTS),
                              ACT.Copy).then_inc(ahi_rdy, 1)

            def gates_high(n):
                sc.wait_ge(ght_done, n)
                sc.activation(ghi[:, :], pb[0:SLOTS, 7, 0:REAL], ACT.Copy).then_inc(ghi_rdy, 1)

            def out_high(b):
                sc.wait_ge(w_used, 24 * b + (HS + 6))
                sc.activation(yhi[:, :], pb[0:SLOTS, 5:7, :].rearrange("p a b -> p (a b)"), ACT.Copy).then_inc(yhi_rdy, 1)

            with sc.Fori(0, nb) as b:
                sc.activation(stat[:, 20:21], mhalf[:, :], ACT.Sigmoid)
                for q in range(STEPS):
                    k = q * HALVES
                    high(b, k)
                    sigmoid(4 * b + (q + 1))
                    high(b, k + 1)
                    if q == 0:
                        gates_high(b + 1)
                    high(b, k + 2)
                    if q == 1:
                        out_high(b)
                    high(b, k + 3)
                    high(b, k + 4)
                    act_high(4 * b + (q + 1))
                    high(b, k + 5)
                    if q == 3:
                        tokens(b + 2)
            sigmoid(4 * nb + 1)
            gates_high(nb + 1)
            act_high(4 * nb + 1)
            sc.wait_ge(e_in[2], 32 * nb + 16)
            for k in (4, 5):
                sc.wait_ge(w_used, 24 * nb + (k - 3))
                sc.activation(whi[:, k % HS, :], raw_half(k), ACT.Copy).then_inc(hi_done, 1)
            sc.wait_ge(w_used, 24 * nb + (HS + 2))
            sc.activation(yhi[:, :], pb[0:SLOTS, 5:7, :].rearrange("p a b -> p (a b)"), ACT.Copy).then_inc(yhi_rdy, 1)
            sc.wait_ge(acc_done, 1)
            for t in range(TT):
                if t:
                    sc.wait_ge(sq_done, 5 + t)
                sc.activation(junk2, pb[:, 2 * t:2 * t + 2, :].rearrange("p a b -> p (a b)"), ACT.Square,
                              accum_out=stat[:, t:t + 1]).then_inc(sq_done, 1)

        @block.vector
        def _(dve):
            def variance(t, rows, n):
                dve.wait_ge(sq_done, n)
                dve.tensor_scalar(stat[0:rows, 3 + t:4 + t], stat[0:rows, t:t + 1], 1.0 / D, EPS, ALU.mult,
                                  ALU.add).then_inc(vr_done, 1)

            dve.memset(bias3[3 * NE:P, :], 0.0).then_inc(zeroed, 1)
            for c in (22, 23):
                dve.memset(stat[:, c:c + 1], 0.0).then_inc(b_free, 1)
            dve.wait_ge(wmb_in, 16)
            for t in range(3):
                variance(t, META if t == 2 else P, t + 1)
            for t in range(3):
                rows = META if t == 2 else P
                dve.wait_ge(pow_done, t + 1)
                dve.scalar_tensor_tensor(out=xn[0:rows, t, :], in0=hm[0:META, :] if t == 2 else hx[:, t, :],
                                         scalar=stat[0:rows, 6 + t:7 + t], in1=wmb[0:rows, :], op0=ALU.mult,
                                         op1=ALU.mult).then_inc(xn_done, 1)

            dve.wait_ge(consts, 9)
            dve.wait_ge(a_free, 2)
            taps = par[:, 0:256].rearrange("p (w c) -> p w c", c=KC)
            step = Chain(dve, conv_step)

            def gated_input(i):
                for j in range(2):
                    dve.wait_ge(a_full, 2 * i + (1 + j))
                    dve.wait_ge(b_free, 2 * i + (3 + j))
                    dve.tensor_tensor(upad[:, bass.ds(2 * i + j, 1), PADL:PADL + TALL], pb[:, j:j + 1, 0:TALL],
                                      sigb[:, j:j + 1, :], ALU.mult).then_inc(a_free, 1)

            def convolve(i, second):
                if not second:
                    dve.tensor_copy(wt[:, :, :], taps[:, :, bass.ds(2 * i, 2)]).then_inc(wt_done, 1)
                    dve.wait_ge(wt_done, i + 1)
                    dve.wait_ge(a_free, 2 * i + 4)
                for w in range(TAPS // 2, TAPS) if second else range(TAPS // 2):
                    for j in range(2):
                        u = upad[:, bass.ds(2 * i + j, 1), w:w + REAL]
                        if w == 0:
                            ins = dve.tensor_scalar(cacc[:, j:j + 1, :], u, wt[:, 0, j:j + 1], wt[:, TAPS, j:j + 1],
                                                    ALU.mult, ALU.add)
                        else:
                            step.wait(1)
                            o = cacc[:, j:j + 1, :] if w < TAPS - 1 else cv[:, bass.ds(2 * i + j, 1), :]
                            ins = dve.scalar_tensor_tensor(out=o, in0=u, scalar=wt[:, w, j:j + 1],
                                                           in1=cacc[:, j:j + 1, :], op0=ALU.mult, op1=ALU.add)
                        step.did(ins)
                if second:
                    step.wait()

            with dve.Fori(0, 2) as i:
                step.enter(i, 62)
                for second in range(2):
                    gated_input(2 * i + second)
                    convolve(i, second)
            step.leave(2)

            dve.wait_ge(tab_in, 48)
            dve.wait_ge(b3_step, 6)
            gn = Chain(dve, gn_step)

            def gate_y(h, h1):
                dve.wait_ge(a_free, 6 * h1 + 4)
                dve.wait_ge(b_free, 6 * h1 + 4)
                for c in range(VC):
                    dve.wait_ge(yt_done, 4 * h1 - (2 if c < 2 else 0))
                    src = pb[:, 4 + 3 * (c // 2), (c % 2) * REAL:(c % 2 + 1) * REAL].rearrange("p (o n) -> p o n", o=1)
                    if isinstance(h, int):
                        o, w = rT[:, h * VC + c:h * VC + c + 1, :], par[:, GNW - VC + h * VC + c:GNW - VC + h * VC + c + 1]
                    else:
                        o, w = rT[:, bass.ds(h * VC + c, 1), :], par[:, bass.ds(h * VC + (GNW - VC + c), 1)]
                    dve.scalar_tensor_tensor(out=o, in0=src, scalar=w, in1=sg[:, c:c + 1, :], op0=ALU.mult,
                                             op1=ALU.mult).then_inc(rt_done, 1)

            def head(h):
                gate_y(h, h + 1)
                dve.wait_ge(sc_done, 3 * h + 2)
                dve.tensor_tensor(sA.rearrange("p (o n) -> p o n", o=1), pb[:, 7:8, 0:REAL],
                                  decay[:, bass.ds(h, 1), 0:REAL], ALU.mult).then_inc(s_done, 1)
                dve.tensor_tensor(sM[0:META, :].rearrange("p (o n) -> p o n", o=1), pb[0:META, 7:8, REAL:2 * REAL],
                                  decay[0:META, bass.ds(h, 1), META:TALL], ALU.mult).then_inc(s_done, 1)
                dve.wait_ge(sc_done, 3 * h + 3)
                dve.tensor_tensor(sB.rearrange("p (o n) -> p o n", o=1), pb[:, 4:5, 0:P],
                                  decay[:, bass.ds(h, 1), 0:P], ALU.mult).then_inc(s_done, 1)
                for t in range(TT):
                    dve.wait_ge(y_done, 2 * h + (1 + t))
                    gn.did(dve.bn_stats(bst[:, t, :], pb[:, 5 + t, :]))
                gn.wait()
                gn.did(dve.tensor_tensor(bmv[:, :, 1], bst[:, :, 1], bst[:, :, 4], ALU.add))
                gn.did(dve.tensor_tensor(bmv[:, :, 2], bst[:, :, 1], bst[:, :, 4], ALU.subtract))
                gn.did(dve.tensor_tensor(bmv[:, :, 3], bst[:, :, 2], bst[:, :, 5], ALU.add))
                gn.wait()
                gn.did(dve.tensor_scalar(bmv[:, :, 0], bmv[:, :, 1], 0.5, None, ALU.mult))
                gn.did(dve.scalar_tensor_tensor(out=bmv[:, :, 2], in0=bmv[:, :, 2], scalar=0.25, in1=bmv[:, :, 2],
                                                op0=ALU.mult, op1=ALU.mult))
                gn.did(dve.tensor_scalar(bmv[:, :, 3], bmv[:, :, 3], 1.0 / DV, EPS, ALU.mult, ALU.add))
                gn.wait()
                dve.tensor_tensor(stat[:, 16:18], bmv[:, :, 2], bmv[:, :, 3], ALU.add).then_inc(gv_done, 1)
                dve.wait_ge(gp_done, h + 1)
                for t in range(TT):
                    dve.tensor_scalar(yn[:, t, :], pb[:, 5 + t, :], bmv[:, t, 0:1], stat[:, 18 + t:19 + t],
                                      ALU.subtract, ALU.mult).then_inc(yn_done, 1)

            with dve.Fori(0, HEADS // 2) as i:
                step.enter(i, 62)
                gn.enter(i, 16)
                for second in range(2):
                    convolve(i + 2, second)
                    head(2 * i + second)
            step.leave(2)
            gn.leave(HEADS // 2)
            gate_y(HEADS, HEADS + 1)

            dve.wait_ge(b_full, 34)
            for c in range(2):
                m = pb[:, 2:3, 0:REAL].to_broadcast([P, KC // 2, REAL])
                part = cv[:, c * KC // 2:(c + 1) * KC // 2, :]
                dve.scalar_tensor_tensor(out=part, in0=m, scalar=-1.0 / D, in1=part, op0=ALU.mult,
                                         op1=ALU.add).then_inc(xc_done, 1)
            dve.wait_ge(xc_done, 2)
            dve.memset(stat[:, 22:24], 0.0).then_inc(b_free, 2)
            dve.wait_ge(b_full, 36)
            diag = ident[:, :].rearrange("p (o n) -> p o n", o=1).to_broadcast([P, TT, P])
            dve.tensor_tensor(lnd, pb[:, 2, 0:REAL].rearrange("p (t n) -> p t n", t=TT), diag, ALU.mult).then_inc(b_free, 2)
            dve.wait_ge(b_free, 38)
            dve.tensor_reduce(stat[:, 16:18], lnd, AX_X, ALU.add).then_inc(lnv_done, 1)
            dve.wait_ge(lnv_done, 1)
            dve.tensor_scalar(stat[:, 16:18], stat[:, 16:18], 1.0 / D, EPS, ALU.mult, ALU.add).then_inc(lnv_done, 1)
            dve.wait_ge(lnp_done, 1)
            dve.tensor_tensor(lnd, stat[:, 18:20].rearrange("p (t o) -> p t o", o=1).to_broadcast([P, TT, P]), diag,
                              ALU.mult).then_inc(lnd_done, 1)
            dve.wait_ge(b_full, 38)
            for c in range(2):
                part = cv[:, c * KC // 2:(c + 1) * KC // 2, :]
                dve.tensor_tensor(part, part, pb[:, 2:3, 0:REAL].to_broadcast([P, KC // 2, REAL]), ALU.mult).then_inc(lnx_done, 1)
            dve.wait_ge(lnx_done, 2)
            dve.memset(stat[:, 22:24], 0.0).then_inc(b_free, 2)
            with dve.Fori(0, UC) as g:
                for j in range(2):
                    dve.wait_ge(b_free, 2 * g + (41 + j))
                    dve.wait_ge(a_free, 42)
                    o = yret[:, bass.ds(2 * g + j, 1), :]
                    dve.tensor_tensor(o, o, sgb[:, bass.ds(2 * g + j, 1), :], ALU.mult).then_inc(gb_done, 1)
            dve.wait_ge(a_free, 50)
            dve.wait_ge(gb_done, KC)
            with dve.Fori(0, 2) as i:
                for q in range(4):
                    full, free, base = ((a_full, a_free, 49), (b_full, b_free, 47))[q // 2]
                    c = bass.ds(4 * i + q, 1)
                    dve.wait_ge(full, 2 * i + (base + q % 2))
                    dve.scalar_tensor_tensor(out=sga[:, c, :], in0=pb[:, q:q + 1, 0:REAL],
                                             scalar=par[:, bass.ds(4 * i + (BCO + q), 1)], in1=sga[:, c, :],
                                             op0=ALU.add, op1=ALU.mult).then_inc(free, 1)
                    dve.wait_ge(free, 2 * i + (base + 2 + q % 2))
                    dve.tensor_tensor(yret[:, c, :], yret[:, c, :], sga[:, c, :], ALU.add).then_inc(merged, 1)
            for n in range(UC):
                dve.wait_ge((a_full, b_full)[n // 2], (53, 51)[n // 2] + n % 2)
                o = hx[:, :, n * UNIT:(n + 1) * UNIT]
                dve.tensor_tensor(o, o, pb[:, n, :].rearrange("p (t n) -> p t n", t=TT), ALU.add).then_inc(h2_done, 1)
            dve.wait_ge(nwb_in, 32)
            for t in range(TT):
                variance(t, P, 4 + t)
            for t in range(TT):
                dve.wait_ge(pow_done, 4 + t)
                dve.scalar_tensor_tensor(out=xn2[:, t, :], in0=hx[:, t, :], scalar=stat[:, 6 + t:7 + t],
                                         in1=nwb[:, 0, :], op0=ALU.mult, op1=ALU.mult).then_inc(xn_done, 1)

            dve.wait_ge(x3_rdy, 2)
            dve.tensor_tensor(xres[:, :, :], xn2[:, :, :], x3[:, 0, :, :], ALU.subtract).then_inc(xr_rdy, 1)

            rt = Chain(dve, route_step)

            def do(ins):
                rt.did(ins)
                rt.wait()

            hot4 = pick[:, 0:TT * TOPK * NE].rearrange("p (t k e) -> p t k e", t=TT, k=TOPK)
            dve.wait_ge(rout_in, 32)
            for t in range(TT):
                dve.wait_ge(lgt, t + 1)
                dve.tensor_tensor(lg[:, t, :], pb[:, 4 + t, 0:NE], brb[:, :], ALU.add).then_inc(lgt_read, 1)
                dve.wait_ge(lgt_read, t + 1)
                do(dve.max(top[:, t, :], lg[:, t, :]))
                dve.tensor_scalar(gate4[:, t, :], top[:, t, 0:TOPK], top[:, t, 0:1], None,
                                  ALU.subtract).then_inc(shift_done, 1)
                do(dve.max_index(topi[:, t, :], top[:, t, :], lg[:, t, :]))
                do(dve.tensor_copy(topf[:, t, :], topi[:, t, 0:TOPK]))
                do(dve.tensor_tensor(hot4[:, t], iota_e[:, :].rearrange("p (o e) -> p o e", o=1).to_broadcast([P, TOPK, NE]),
                                     topf[:, t, :].rearrange("p (k o) -> p k o", o=1).to_broadcast([P, TOPK, NE]),
                                     ALU.is_equal))
                dve.tensor_reduce(mask[:, t, :], hot4[:, t].rearrange("p k e -> p e k"), AX_X, ALU.add).then_inc(route, 1)
            dve.wait_ge(rank_done, 1)
            cnt = pb[:, 6, 2 * NE:3 * NE]
            do(dve.tensor_scalar(nblk[:, :], cnt, float(SLOTS), 1.0, ALU.is_gt, ALU.add))
            for q in (2, 3):
                do(dve.scalar_tensor_tensor(out=nblk[:, :], in0=cnt, scalar=float(q * SLOTS), in1=nblk[:, :],
                                            op0=ALU.is_gt, op1=ALU.add))
            do(dve.tensor_tensor_scan(pend[:, :], ones[:, 0:NE], nblk[:, :], 0.0, ALU.mult, ALU.add))
            do(dve.tensor_tensor(nblk[:, :], pend[:, :], nblk[:, :], ALU.subtract))
            do(dve.tensor_scalar(nblk[:, :], nblk[:, :], float(SLOTS), 1.0, ALU.mult, ALU.add))
            starts = nblk[:, :].rearrange("p (o e) -> p o e", o=1).to_broadcast([P, TT, NE])
            do(dve.tensor_tensor(slot[:, :, :], pb[:, 6, 0:TT * NE].rearrange("p (t e) -> p t e", t=TT), starts, ALU.add))
            do(dve.tensor_tensor(slot[:, :, :], slot[:, :, :], mask[:, :, :], ALU.mult))
            do(dve.tensor_scalar(slot[:, :, :], slot[:, :, :], -1.0, None, ALU.add))
            for t in range(TT):
                dve.tensor_scalar(onehot[:, t, :], iota_s[:, :], slot[:, t, 0:1], None, ALU.is_equal).then_inc(hot_rdy, 1)
            half = MAXB // 2
            c3 = pick[:, TT * TOPK * NE:TT * TOPK * NE + half * NE].rearrange("p (b e) -> p b e", e=NE)
            for q in range(2):
                do(dve.tensor_tensor(c3, pend[:, :].rearrange("p (o e) -> p o e", o=1).to_broadcast([P, half, NE]),
                                     iota_b[:, q * half:(q + 1) * half].rearrange("p (b o) -> p b o", o=1)
                                     .to_broadcast([P, half, NE]), ALU.is_le))
                do(dve.tensor_reduce(tabf[:, q * half:(q + 1) * half], c3, AX_X, ALU.add))
            do(dve.tensor_scalar(tabf[:, :], tabf[:, :], float(NE - 1), None, ALU.min))
            dve.memset(table[0:1, 0:1], 0).then_inc(table_done, 1)
            dve.tensor_copy(table[0:1, 1:MAXB + 1], tabf[0:1, :]).then_inc(table_done, 1)
            dve.tensor_scalar(nblocks[:, 1:2], pend[0:1, NE - 1:NE], -1.0, None, ALU.add).then_inc(table_done, 1)
            dve.tensor_copy(nblocks[:, 0:1], pend[0:1, NE - 1:NE]).then_inc(table_done, 1)

            def pick_rows(b):
                col = tabf[:, b:b + 1] if isinstance(b, int) else tabf[:, bass.ds(b, 1)]
                dve.tensor_scalar(pick_e[:, :], eid[:, :], col, None, ALU.is_equal).then_inc(sel_rdy, 1)

            def tokens_low(n):
                dve.wait_ge(xhi_rdy, n)
                dve.tensor_tensor(xlo[:, :, :], pb[:, 7, :].rearrange("p (k n) -> p k n", n=SLOTS),
                                  xhi[:, :, :].bitcast(F32), ALU.subtract).then_inc(xlo_rdy, 1)

            dve.memset(gatehot[:, :, :], 0.0).then_inc(gh_rdy, 1)
            dve.memset(act, 0.0).then_inc(act_rdy, 1)
            dve.wait_ge(eid_in, 16)
            pick_rows(0)
            tokens_low(1)
            for t in range(TT):
                dve.wait_ge(exp_done, t + 1)
                do(dve.reciprocal(stat[:, 12 + t:13 + t], stat[:, 10 + t:11 + t]))
                do(dve.tensor_scalar(gate4[:, t, :], gate4[:, t, :], stat[:, 12 + t:13 + t], None, ALU.mult))
                do(dve.tensor_tensor(hot4[:, t], hot4[:, t], gate4[:, t, :].rearrange("p (k o) -> p k o", o=1)
                                     .to_broadcast([P, TOPK, NE]), ALU.mult))
                do(dve.tensor_reduce(gdense[:, t, :], hot4[:, t].rearrange("p k e -> p e k"), AX_X, ALU.add))
            dve.wait_ge(table_done, 4)
            nb = dve.value_load(nblocks[0:1, 0:1], min_val=NE, max_val=MAXB - 1)

            def low(b, k):
                dve.wait_ge(hi_done, 24 * b + (k + 1))
                dve.tensor_tensor(wlo[:, k % HS, :], raw_half(k), whi[:, k % HS, :].bitcast(F32),
                                  ALU.subtract).then_inc(lo_v, 1)

            def last_low(b, k):
                dve.wait_ge(hi_done, 24 * b + (k + 1))
                dve.tensor_tensor(wlo[:, k % HS, LAST], raw_half(k)[:, LAST], whi[:, k % HS, LAST].bitcast(F32),
                                  ALU.subtract).then_inc(lo_v, 1)

            def activate(n, used, half=None):
                dve.wait_ge(w_used, used)
                dve.wait_ge(act_rdy, n)
                dve.tensor_scalar(hg, pb[0:SLOTS, 4, 0:UNIT], LIMIT, None, ALU.min).then_inc(min_rdy, 1)
                dve.tensor_scalar(hu, pb[0:SLOTS, 4, UNIT:2 * UNIT], -LIMIT, LIMIT, ALU.max, ALU.min).then_inc(clip_rdy, 1)
                if half:
                    low(*half)
                dve.wait_ge(sig_rdy, n)
                dve.tensor_tensor(sig, sig, hg, ALU.mult).then_inc(prod_rdy, 1)
                dve.wait_ge(clip_rdy, n)
                dve.wait_ge(prod_rdy, n)
                dve.scalar_tensor_tensor(out=act, in0=hu, scalar=1.0, in1=sig, op0=ALU.add,
                                         op1=ALU.mult).then_inc(act_rdy, 1)

            def gates_low(n):
                dve.wait_ge(ghi_rdy, n)
                dve.tensor_tensor(glo[:, :], pb[0:SLOTS, 7, 0:REAL], ghi[:, :].bitcast(F32), ALU.subtract).then_inc(glo_rdy, 1)

            def act_low(n):
                dve.wait_ge(ahi_rdy, n)
                dve.tensor_tensor(alo[:, :, :], pb[:, 7, 0:2 * SLOTS].rearrange("p (k n) -> p k n", n=SLOTS),
                                  ahi[:, :, :].bitcast(F32), ALU.subtract).then_inc(alo_rdy, 1)

            def out_low(n):
                dve.wait_ge(yhi_rdy, n)
                dve.tensor_tensor(ylo[:, :], pb[0:SLOTS, 5:7, :].rearrange("p a b -> p (a b)"),
                                  yhi[:, :].bitcast(F32), ALU.subtract).then_inc(ylo_rdy, 1)

            with dve.Fori(0, nb) as b:
                e = dve.value_load(table[0:1, bass.ds(b + 1, 1)], min_val=0, max_val=NE - 1)
                e1 = dve.value_load(table[0:1, bass.ds(b + 2, 1)], min_val=0, max_val=NE - 1)
                for q in range(STEPS):
                    k = q * HALVES
                    activate(4 * b + (q + 1), 24 * b + (HS + k - 2), (b, k))
                    low(b, k + 1)
                    if q == 0:
                        gates_low(b + 1)
                    low(b, k + 2)
                    if q == 1:
                        out_low(b + 1)
                    low(b, k + 3)
                    act_low(4 * b + (q + 1))
                    last_low(b, k + 5)
                    if q == 1:
                        dve.wait_ge(ght_done, b + 1)
                        dve.wait_ge(gh_rdy, 2 * b + 1)
                        for t in range(TT):
                            dve.tensor_scalar(gatehot[:, t, :], iota_s[:, :], slot[:, t, bass.ds(e, 1)],
                                              gdense[:, t, bass.ds(e, 1)], ALU.is_equal, ALU.mult).then_inc(gh_rdy, 1)
                        dve.wait_ge(gh_rdy, 2 * b + 3)
                        dve.wait_ge(hot_rdy, 2 * b + 2)
                        dve.tensor_scalar(iota_s[:, :], iota_s[:, :], float(SLOTS), None, ALU.add).then_inc(slot_step, 1)
                        dve.wait_ge(slot_step, b + 1)
                        dve.wait_ge(gathered, b + 1)
                        for t in range(TT):
                            dve.tensor_scalar(onehot[:, t, :], iota_s[:, :], slot[:, t, bass.ds(e1, 1)], None,
                                              ALU.is_equal).then_inc(hot_rdy, 1)
                    if q == 3:
                        dve.wait_ge(w_used, 24 * b + (HS + 19))
                        pick_rows(b + 1)
                        tokens_low(b + 2)
            activate(4 * nb + 1, 24 * nb + (HS - 2))
            gates_low(nb + 1)
            act_low(4 * nb + 1)
            dve.wait_ge(hi_done, 24 * nb + 2)
            dve.tensor_tensor(wlo[:, 1, LAST], raw_half(5)[:, LAST], whi[:, 1, LAST].bitcast(F32),
                              ALU.subtract).then_inc(lo_v, 1)
            out_low(nb + 1)
            for t in range(TT):
                variance(t, P, 6 + t)
            for t in range(TT):
                dve.wait_ge(pow_done, 6 + t)
                dve.scalar_tensor_tensor(out=osb[:, t, :], in0=pb[:, 2 * t:2 * t + 2, :].rearrange("p a b -> p (a b)"),
                                         scalar=stat[:, 6 + t:7 + t], in1=nwb[:, 1, :], op0=ALU.mult,
                                         op1=ALU.mult).then_inc(out_rdy, 1)


NAMES = ["x", "meta_tokens", "norm_mix_w", "w_in", "conv_dw_w", "conv_dw_b", "conv_ln_w", "conv_ln_b", "w_conv_out",
         "b_conv_out", "ret_gn_w", "w_ret_out", "w_mix_out", "norm_ffn_w", "w_router", "b_router", "w_gate_up",
         "b_gate_up", "w_down", "b_down", "norm_final_w"]


def shape_tables():
    import numpy as np
    f = np.float32
    inv = (f(10000.0) ** (-np.arange(0, DK, 2, dtype=f) / f(DK))).astype(f)
    ang = (inv[:, None] * np.arange(TALL, dtype=f)[None, :]).astype(f)
    lg = np.log1p(-np.exp2(-5.0 - np.arange(HEADS)))
    n = np.arange(TALL)[None, :] - np.arange(P)[:, None]
    dec = np.where(n[:, None, :] >= 0, np.exp(lg[None, :, None] * np.maximum(n, 0)[:, None, :]), 0.0) * DK ** -0.5
    rows = np.arange(P)
    eid = np.where(rows < 3 * NE, rows % NE, -1).astype(f)[:, None].repeat(SLOTS, 1)
    return {"eid": np.ascontiguousarray(eid), "cos": np.cos(ang).astype(f), "sin": np.sin(ang).astype(f), "decay": np.ascontiguousarray(dec.astype(f))}


def kernel(**inputs):
    import numpy as np
    import concourse.bacc as bacc
    from concourse.bass_utils import run_bass_kernel_spmd as run

    nc = bacc.Bacc("TRN2", target_bir_lowering=False, num_devices=1)
    arrays, aps = {}, {}
    tables = shape_tables()
    for name in NAMES + list(tables):
        arr = np.ascontiguousarray(tables[name] if name in tables else inputs[name])
        arrays[f"in_{name}"] = arr
        aps[name] = nc.dram_tensor(f"in_{name}", arr.shape, mybir.dt.from_np(arr.dtype), kind="ExternalInput").ap()
    out = nc.dram_tensor("out_0", (1, REAL, D), F32, kind="ExternalOutput").ap()
    build_block(nc, aps, out)
    return run(nc, [arrays], core_ids=[0]).results[0]["out_0"]
```

```python
from contextlib import ExitStack

import concourse.bass as bass
from concourse import mybir

F32 = mybir.dt.float32
I32 = mybir.dt.int32
U32 = mybir.dt.uint32
R32 = mybir.dt.float32r
BF16 = mybir.dt.bfloat16
ALU = mybir.AluOpType
ACT = mybir.ActivationFunctionType
AX_X = mybir.AxisListType.X

P = 128
D = 1024
KC = D // P
META = 16
REAL = 256
TT = REAL // P
TALL = META + REAL
TAPS = 31
PADL = TAPS - 1 - META
HEADS = 4
DK = 256
DV = 512
VC = DV // P
UNIT = 256
NE = 32
TOPK = 4
SLOTS = 64
MAXB = 48
STEPS = D // UNIT
HALVES = 6
HW = KC * UNIT // 2
HS = 4
PARTS = 3
EPS = 1e-5
LIMIT = 7.0
ALPHA = 1.702

TAP0, LNW, LNB, BCO, GNW = 0, 256, 264, 272, 280
NPAR = 296


class Chain:

    def __init__(self, eng, sem):
        self.eng, self.sem, self.base, self.n = eng, sem, 0, 0

    def did(self, ins):
        ins.then_inc(self.sem, 1)
        self.n += 1

    def wait(self, back=0):
        self.eng.wait_ge(self.sem, self.base + (self.n - back))

    def enter(self, i, per):
        self.start, self.per = self.base + self.n, per
        self.base, self.n = i * per + self.start, 0

    def leave(self, trips):
        assert self.n == self.per, (self.n, self.per)
        self.base, self.n = self.start + trips * self.per, 0


def build_block(nc, a, out):
    with ExitStack() as ctx:
        def sb(name, shape, dt=F32):
            return ctx.enter_context(nc.sbuf_tensor(name, shape, dt))

        def sem(name):
            return ctx.enter_context(nc.semaphore(name))

        pb = ctx.enter_context(nc.psum_tensor("pb", [P, 8, 512], F32))

        ring = sb("ring", [P, 6, KC, UNIT])
        parts = sb("parts", [P, 2 * KC * TALL], R32)
        hx = sb("hx", [P, TT, D])
        cv = sb("cv", [P, KC, REAL])
        rT = sb("rT", [P, 4 * VC + VC, REAL])
        ubuf = sb("ubuf", [P, KC * (PADL + TALL)])
        scratch = sb("scratch", [P, 11268])
        whi = sb("whi", [P, HS, HW], R32)
        wlo = sb("wlo", [P, HS, HW], R32)
        bias3 = sb("bias3", [P, 3 * D], BF16)
        pick_e = sb("pick_e", [P, SLOTS], BF16)
        eid = sb("eid", [P, SLOTS])
        par = sb("par", [P, NPAR])
        ident = sb("ident", [P, P])
        ones = sb("ones", [P, P])
        before = sb("before", [P, P])
        iota_s = sb("iota_s", [P, SLOTS])
        iota_e = sb("iota_e", [P, NE])
        iota_b = sb("iota_b", [P, MAXB])
        mhalf = sb("mhalf", [P, 1])
        epsc = sb("epsc", [P, 1])
        stat = sb("stat", [P, 24])
        wt = sb("wt", [P, 32, 2])
        topi = sb("topi", [P, TT, 8], U32)
        onehot = sb("onehot", [P, TT, SLOTS], BF16)
        table = sb("table", [1, MAXB + 1], I32)
        nblocks = sb("nblocks", [1, 2], I32)
        tabf = sb("tabf", [P, MAXB])
        bst = sb("bst", [P, TT, 6])
        bmv = sb("bmv", [P, TT, 4])

        upad = ubuf[:, :].rearrange("p (a b) -> p a b", a=KC)
        yret = ubuf[:, 0:KC * REAL].rearrange("p (a b) -> p a b", a=KC)

        pair_at = [0]

        def pair_of(rows, n):
            views = [parts[0:rows, pair_at[0] + c * n:pair_at[0] + (c + 1) * n] for c in range(2)]
            pair_at[0] += 2 * n
            return views

        nhi, nlo = (v.rearrange("p (k n) -> p k n", k=KC) for v in pair_of(P, KC * TALL))
        pair_at[0] = 0
        xhi, xlo = (v.rearrange("p (k n) -> p k n", k=KC) for v in pair_of(P, KC * SLOTS))
        ahi, alo = (v.rearrange("p (k n) -> p k n", k=2) for v in pair_of(P, 2 * SLOTS))
        yhi, ylo = pair_of(SLOTS, D)
        gslot = stat[0:SLOTS, 21:22]
        hotT = pair_of(SLOTS, REAL)[0]

        flat = scratch[:, :]
        at = [0]

        def tmp(*shape):
            n = 1
            for s in shape:
                n *= s
            v = flat[:, at[0]:at[0] + n]
            at[0] += n
            assert at[0] <= 11268
            if len(shape) == 2:
                v = v.rearrange("p (a b) -> p a b", a=shape[0])
            return v

        decay = tmp(HEADS, TALL)
        cos = tmp(TALL)
        sin = tmp(TALL)
        early = at[0]
        qraw, kraw = tmp(2, REAL), tmp(2, TALL)
        qrot, krot = tmp(2, REAL), tmp(2, TALL)
        rc, rs = tmp(2, TALL), tmp(2, TALL)
        vT = tmp(VC, TALL)
        vsb = tmp(2, DV)
        vM = tmp(DV)
        sA, sB, sM = tmp(REAL), tmp(P), tmp(REAL)
        at[0] = max(at[0], early + 6 * D + 384)
        yn = tmp(TT, DV)
        sg = tmp(VC, REAL)
        cacc = tmp(2, REAL)
        sigb = tmp(2, TALL)
        dflat = flat[:, early:]
        hm = dflat[:, 0:D]
        xn = dflat[:, D:4 * D].rearrange("p (a b) -> p a b", a=3)
        wmb = dflat[:, 4 * D:5 * D]
        prow = dflat[:, 5 * D:5 * D + 384].rearrange("p (a b) -> p a b", a=3)
        junk1 = dflat[:, 5 * D + 384:6 * D + 384]
        sq = flat[:, 0:KC * REAL].rearrange("p (a b) -> p a b", a=KC)

        sga = rT[:, 0:KC, :]
        sgb = rT[:, KC:2 * KC, :]
        rflat = rT[:, :, :].rearrange("p a b -> p (a b)")
        lnd = flat[:, KC * REAL:(KC + 1) * REAL].rearrange("p (t n) -> p t n", t=TT)
        brows = rflat[0:3 * NE, 0:3 * D]
        gatehot = flat[:, 0:TT * SLOTS].rearrange("p (a b) -> p a b", a=TT)
        hg = flat[0:SLOTS, 256:256 + UNIT]
        hu = flat[0:SLOTS, 512:512 + UNIT]
        sig = flat[0:SLOTS, 768:768 + UNIT]
        act = flat[0:SLOTS, 1024:1024 + UNIT]
        gates = flat[0:SLOTS, 1280:1280 + REAL]
        pick = flat[:, 2048:3072]
        at[0] = 3072
        wr = tmp(KC, NE)
        brb, nblk, pend = tmp(NE), tmp(NE), tmp(NE)
        lg, mask, gdense, slot = (tmp(TT, NE) for _ in range(4))
        top, topf, gate4 = tmp(TT, 8), tmp(TT, TOPK), tmp(TT, TOPK)
        assert at[0] <= 4096
        xres = flat[:, 4096:4096 + TT * D].rearrange("p (a b) -> p a b", a=TT)
        x3 = flat[:, 8192:8192 + PARTS * TT * D // 2].bitcast(BF16).rearrange("p (q a b) -> p q a b", q=PARTS, a=TT)
        junk2 = rflat[:, 4096:5120]
        xn2 = yret[:, :, :].rearrange("p a b -> p (a b)").rearrange("p (a b) -> p a b", a=TT)
        xn2T = rflat[:, 0:KC * REAL].rearrange("p (a b) -> p a b", a=KC)
        osb = rflat[:, KC * REAL:2 * KC * REAL].rearrange("p (a b) -> p a b", a=TT)
        nwb = cv[:, :, :].rearrange("p a b -> p (a b)").rearrange("p (a b) -> p a b", a=2)

        x_in, meta_in, wmb_in = sem("x_in"), sem("meta_in"), sem("wmb_in")
        eid_in, par_in, bias_in, tab_in, rout_in, nwb_in = (sem(n) for n in ("eid_in", "par_in", "bias_in", "tab_in", "rout_in", "nwb_in"))
        landed = [sem(f"landed{s}") for s in range(6)]
        e_in = [sem(f"e_in{s}") for s in range(6)]
        consts = sem("consts")
        masked = sem("masked")
        cols = sem("cols")
        colse = sem("colse")
        a_full, b_full = sem("a_full"), sem("b_full")
        a_free, b_free = sem("a_free"), sem("b_free")
        sq_done, vr_done, pow_done, xn_done = (sem(n) for n in ("sq_done", "vr_done", "pow_done", "xn_done"))
        conv_step = sem("conv_step")
        nlo_done = sem("nlo_done")
        m_hi, m_lov, m_lop = sem("m_hi"), sem("m_lov"), sem("m_lop")
        m_used = sem("m_used")
        rope_done, pool_step = sem("rope_done"), sem("pool_step")
        vt_done, v_done = sem("vt_done"), sem("v_done")
        sc_done, s_done, y_done = sem("sc_done"), sem("s_done"), sem("y_done")
        gn_step, gv_done, gp_done, yn_done = sem("gn_step"), sem("gv_done"), sem("gp_done"), sem("yn_done")
        yt_done, rt_done = sem("yt_done"), sem("rt_done")
        xc_done, lsq_done, lnv_done, lnp_done, lnd_done, lnx_done, ln_done = (
            sem(n) for n in ("xc_done", "lsq_done", "lnv_done", "lnp_done", "lnd_done", "lnx_done", "ln_done"))
        gb_done, merged = sem("gb_done"), sem("merged")
        h2_done, x2t, x2e, lgt, route = sem("h2_done"), sem("x2t"), sem("x2e"), sem("lgt"), sem("route")
        shift_done, wt_done, route_step = sem("shift_done"), sem("wt_done"), sem("route_step")
        exp_done, rank_done, table_done = sem("exp_done"), sem("rank_done"), sem("table_done")
        w_used = sem("w_used")
        hi_done = sem("hi_done")
        lo_v, lo_p = sem("lo_v"), sem("lo_p")
        lgt_read = sem("lgt_read")
        min_rdy, clip_rdy, sig_rdy, prod_rdy, act_rdy = (
            sem(n) for n in ("min_rdy", "clip_rdy", "sig_rdy", "prod_rdy", "act_rdy"))
        turned, ahi_rdy, alo_rdy = sem("turned"), sem("ahi_rdy"), sem("alo_rdy")
        yhi_rdy, ylo_rdy, ght_done, gslot_rdy, hotT_rdy = (
            sem(n) for n in ("yhi_rdy", "ylo_rdy", "ght_done", "gslot_rdy", "hotT_rdy"))
        hot_rdy, gathered, xhi_rdy, xlo_rdy = sem("hot_rdy"), sem("gathered"), sem("xhi_rdy"), sem("xlo_rdy")
        gh_rdy, sel_rdy, slot_step = sem("gh_rdy"), sem("sel_rdy"), sem("slot_step")
        zeroed, x3_rdy, xr_rdy, b3_step = sem("zeroed"), sem("x3_rdy"), sem("xr_rdy"), sem("b3_step")
        acc_done, out_rdy, out_in = sem("acc_done"), sem("out_rdy"), sem("out_in")

        w_in = a["w_in"][0].rearrange("(k p) n -> p k n", p=P)
        w_co = a["w_conv_out"][0].rearrange("(k p) n -> p k n", p=P)
        w_ro = a["w_ret_out"][0].rearrange("(k p) n -> p k n", p=P)
        w_mo = a["w_mix_out"][0].rearrange("(k p) n -> p k n", p=P)
        w_gu = a["w_gate_up"][0]
        w_dn = a["w_down"][0]

        LAST = slice(0, HW // 2)

        def gate_src(e, q, up):
            c0 = (D if up else 0) + q * UNIT
            return w_gu[bass.ds(e, 1), :, c0:c0 + UNIT].rearrange("o (k p) n -> p (o k) n", p=P)

        def down_src(e, q):
            return w_dn[bass.ds(e, 1), q * UNIT:(q + 1) * UNIT, :].rearrange("o (k p) n -> p (o k) n", p=P)

        def lo_count(b, k):
            q, h = divmod(k, HALVES)
            return 20 * b + (5 * q + h + 1) if h < 4 else 8 * b + (2 * q + h - 3)

        UC = D // UNIT
        U_A, U_B = 0, UC
        U_Q, U_K, U_V, U_G, U_GA, U_GB = 2 * UC, 3 * UC, 4 * UC, 6 * UC, 8 * UC, 9 * UC

        RET = ((4, 5), (2, 5), (0, 9), (4, 6))
        GATES = ((2, 6), (0, 10), (4, 7), (2, 7))
        CONV = ((0, 11), (4, 8))
        MIX = ((2, 8), (4, 9))

        M_HEADS, M_GATES = 2 * UC, 2 * UC + 6 * HEADS

        def m_raw(s, c):
            return ring[:, s, :, :].rearrange("p a b -> p (a b)")[:, c * HW:(c + 1) * HW]

        def raw_half(k):
            return ring[:, k // 2 % 6, :, :].rearrange("p a b -> p (a b)")[:, k % 2 * HW:(k % 2 + 1) * HW]

        block = ctx.enter_context(nc.Block())


        @block.sync
        def _(sp):
            def load(s, src, u):
                cols_ = slice(u * UNIT, u * UNIT + UNIT) if isinstance(u, int) else bass.ds(u * UNIT, UNIT)
                sp.dma_start(ring[:, s, :, :], src[:, :, cols_]).then_inc(landed[s], 16)

            xr = a["x"][0].rearrange("(t p) n -> p t n", p=P)
            sp.dma_start(hm[0:META, :], a["meta_tokens"]).then_inc(meta_in, 16)
            sp.dma_start(hx[:, 0, :], xr[:, 0, :]).then_inc(x_in, 16)
            sp.dma_start(wmb, a["norm_mix_w"][0:1, :].to_broadcast([P, D])).then_inc(wmb_in, 16)
            sp.dma_start(hx[:, 1, :], xr[:, 1, :]).then_inc(x_in, 16)
            load(0, w_in, U_A)
            load(1, w_in, U_B)
            load(2, w_in, U_Q)
            load(3, w_in, U_K)
            load(4, w_in, U_V)
            load(5, w_in, U_V + 1)
            with sp.Fori(0, UC - 1) as i:
                sp.wait_ge(m_lop, 4 * i + 2)
                load(0, w_in, i + (U_A + 1))
                sp.wait_ge(m_lop, 4 * i + 4)
                load(1, w_in, i + (U_B + 1))
            sp.wait_ge(m_lop, 14)
            load(0, w_in, U_G)
            sp.wait_ge(m_lop, 16)
            load(1, w_in, U_G + 1)
            with sp.Fori(0, HEADS - 1) as h:
                sp.wait_ge(m_lop, 6 * h + 18)
                load(2, w_in, h + (U_Q + 1))
                sp.wait_ge(m_lop, 6 * h + 20)
                load(3, w_in, h + (U_K + 1))
                sp.wait_ge(m_lov, 6 * h + 2)
                load(4, w_in, 2 * h + (U_V + 2))
                sp.wait_ge(m_lov, 6 * h + 4)
                load(5, w_in, 2 * h + (U_V + 3))
                sp.wait_ge(m_lov, 6 * h + 6)
                load(0, w_in, 2 * h + (U_G + 2))
                sp.wait_ge(m_lop, 6 * h + 22)
                load(1, w_in, 2 * h + (U_G + 3))

            def unit(e_prev, e, j):
                q, kind = divmod(j, 3)
                dst = ring[:, j % 6, :, :]
                if kind == 2:
                    dst = dst.rearrange("p a b -> p (a b)").rearrange("p (a b) -> p a b", a=2)
                src = gate_src(e, q, kind) if kind < 2 else down_src(e if q else e_prev, q - 1 if q else STEPS - 1)
                sp.dma_start(dst, src).then_inc(e_in[j % 6], 16)

            def pair(slots, srcs, units, full_a, full_b):
                for c in range(2):
                    sp.wait_ge(a_full if c == 0 or not full_b else b_full, full_b if c and full_b else full_a)
                    load(slots + c, srcs[c], units[c])

            ret = (w_ro[:, 0:KC, :], w_ro[:, KC:2 * KC, :])
            pair(RET[0][0], ret, (0, 0), 30, 30)
            pair(RET[1][0], ret, (1, 1), 28, 28)
            pair(RET[2][0], ret, (2, 2), 32, 32)
            pair(RET[3][0], ret, (3, 3), 34, None)
            pair(GATES[0][0], (w_in, w_in), (U_GA, U_GB), 36, None)
            pair(GATES[1][0], (w_in, w_in), (U_GA + 1, U_GB + 1), 38, None)
            pair(GATES[2][0], (w_in, w_in), (U_GA + 2, U_GB + 2), 40, None)
            pair(GATES[3][0], (w_in, w_in), (U_GA + 3, U_GB + 3), 42, 40)
            pair(CONV[0][0], (w_co, w_co), (0, 1), 44, 42)
            pair(CONV[1][0], (w_co, w_co), (2, 3), 46, 44)
            pair(MIX[0][0], (w_mo, w_mo), (0, 1), 48, 46)
            sp.wait_ge(a_full, 50)
            sp.wait_ge(b_full, 48)
            unit(0, 0, 0)
            unit(0, 0, 1)
            pair(MIX[1][0], (w_mo, w_mo), (2, 3), 52, 50)
            sp.dma_start(wr, a["w_router"][0].rearrange("(k p) n -> p k n", p=P)).then_inc(rout_in, 16)
            sp.dma_start(brb, a["b_router"][0:1, :].to_broadcast([P, NE])).then_inc(rout_in, 16)
            sp.dma_start(nwb[:, 0, :], a["norm_ffn_w"][0:1, :].to_broadcast([P, D])).then_inc(nwb_in, 16)
            sp.dma_start(nwb[:, 1, :], a["norm_final_w"].rearrange("(o n) -> o n", o=1)[0:1, :]
                         .to_broadcast([P, D])).then_inc(nwb_in, 16)

            def slot_free(b, j):
                k = 2 * (j - 6) + 1
                if j % 3 == 2:
                    sp.wait_ge(w_used, 24 * b + (HS + k + 1))
                else:
                    sp.wait_ge(lo_v, lo_count(b, k))

            sp.wait_ge(a_full, 54)
            unit(0, 0, 2)
            unit(0, 0, 3)
            sp.wait_ge(b_full, 52)
            unit(0, 0, 4)
            unit(0, 0, 5)
            sp.wait_ge(table_done, 4)
            nb = sp.value_load(nblocks[0:1, 0:1], min_val=NE, max_val=MAXB - 1)
            before_last = sp.value_load(nblocks[0:1, 1:2], min_val=NE - 1, max_val=MAXB - 2)
            with sp.Fori(0, before_last) as b:
                e0 = sp.value_load(table[0:1, bass.ds(b + 1, 1)], min_val=0, max_val=NE - 1)
                e1 = sp.value_load(table[0:1, bass.ds(b + 2, 1)], min_val=0, max_val=NE - 1)
                for j in range(6, 18):
                    slot_free(b, j)
                    unit(e0, e0 if j < 12 else e1, j % 12)
            el = sp.value_load(table[0:1, bass.ds(nb, 1)], min_val=0, max_val=NE - 1)
            for j in range(6, 12):
                slot_free(before_last, j)
                unit(el, el, j)
            slot_free(before_last, 14)
            unit(el, el, 2)
            outr = out[0].rearrange("(t p) n -> p t n", p=P)
            for t in range(TT):
                sp.wait_ge(out_rdy, t + 1)
                sp.dma_start(outr[:, t, :], osb[:, t, :]).then_inc(out_in, 16)
            sp.wait_ge(out_in, 16 * TT)

        @block.gpsimd
        def _(pool):
            pool.memset(ident[:, :], 0.0).then_inc(consts, 1)
            pool.memset(ones[:, :], 1.0).then_inc(consts, 1)
            pool.memset(before[:, :], 1.0).then_inc(consts, 1)
            pool.memset(mhalf[:, :], -0.5).then_inc(consts, 1)
            pool.wait_ge(consts, 3)
            pool.affine_select(out=ident[:, :], in_=ident[:, :], compare_op=ALU.not_equal, fill=1.0,
                               base=0, pattern=[[-1, P]], channel_multiplier=1).then_inc(masked, 1)
            pool.affine_select(out=before[:, :], in_=before[:, :], compare_op=ALU.is_gt, fill=0.0,
                               base=0, pattern=[[1, P]], channel_multiplier=-1).then_inc(masked, 1)
            pool.iota(iota_s[:, :], [[1, SLOTS]], base=0, channel_multiplier=0,
                      allow_small_or_imprecise_dtypes=True).then_inc(consts, 1)
            pool.iota(iota_e[:, :], [[1, NE]], base=0, channel_multiplier=0,
                      allow_small_or_imprecise_dtypes=True).then_inc(consts, 1)
            pool.iota(iota_b[:, :], [[1, MAXB]], base=0, channel_multiplier=0,
                      allow_small_or_imprecise_dtypes=True).then_inc(consts, 1)
            pool.memset(upad[:, :, 0:PADL], 0.0).then_inc(consts, 1)
            pool.memset(sg[:, :, :], 0.0).then_inc(consts, 1)
            pool.memset(yn[:, :, :], 0.0).then_inc(yn_done, 1)
            pool.memset(stat[:, 18:20], 0.0).then_inc(rope_done, 1)

            def rsqrt(o, v, n):
                return pool.tensor_tensor(o, v, mhalf[0:v.shape[0], 0:1].to_broadcast([v.shape[0], n]), ALU.pow)

            pool.wait_ge(consts, 4)
            for t in range(3):
                rows = META if t == 2 else P
                pool.wait_ge(vr_done, t + 1)
                rsqrt(stat[0:rows, 6 + t:7 + t], stat[0:rows, 3 + t:4 + t], 1).then_inc(pow_done, 1)

            def m_low(s, odd, n):
                for c in range(2):
                    pool.wait_ge(m_hi, n + c)
                    pool.tensor_tensor(wlo[:, 2 * odd + c, :], m_raw(s, c), whi[:, 2 * odd + c, :].bitcast(F32),
                                       ALU.subtract).then_inc(m_lop, 1)

            m_low(0, 0, 1)
            m_low(1, 1, 3)
            pool.wait_ge(m_lop, 4)
            pool.wait_ge(b3_step, 1)
            pool.tensor_tensor(brows, brows, bias3[0:3 * NE, :], ALU.subtract).then_inc(b3_step, 1)
            pool.wait_ge(b3_step, 2)
            with pool.Fori(1, UC) as i:
                m_low(0, 0, 4 * i + 1)
                m_low(1, 1, 4 * i + 3)
            pool.wait_ge(m_lop, 4 * UC)
            pool.wait_ge(b3_step, 4)
            pool.tensor_tensor(brows[2 * NE:3 * NE, :], brows[2 * NE:3 * NE, :], bias3[2 * NE:3 * NE, :],
                               ALU.subtract).then_inc(b3_step, 1)

            pool.wait_ge(tab_in, 48)
            step = Chain(pool, pool_step)
            pool.wait_ge(b3_step, 5)
            m_low(2, 0, 4 * UC + 1)

            def head(h, last):
                m_low(3, 1, 12 * h + (4 * UC + 3))
                for which, (raw, rot, n) in enumerate(((qraw, qrot, REAL), (kraw, krot, TALL))):
                    t0 = TALL - n
                    c_ = cos[:, t0:TALL].rearrange("p (o n) -> p o n", o=1).to_broadcast([P, 2, n])
                    pool.wait_ge((a_free, b_free)[which], 6 * h + 12)
                    if which:
                        step.wait()
                        pool.wait_ge(rope_done, 2 * h + 2)
                    else:
                        pool.wait_ge(rope_done, 2 * h + 1)
                    step.did(pool.tensor_tensor(rc[:, :, 0:n], raw[:, :, :], c_, ALU.mult))
                    step.did(pool.tensor_tensor(rs[:, 0, 0:n], raw[:, 1, :], sin[:, t0:TALL], ALU.mult))
                    step.did(pool.tensor_tensor(rs[:, 1, 0:n], raw[:, 0, :], sin[:, t0:TALL], ALU.mult))
                    step.wait()
                    pool.tensor_tensor(rot[:, 0, :], rc[:, 0, 0:n], rs[:, 0, 0:n], ALU.subtract)
                    pool.tensor_tensor(rot[:, 1, :], rc[:, 1, 0:n], rs[:, 1, 0:n], ALU.add).then_inc(rope_done, 1)
                m_low(1, 1, 12 * h + (4 * UC + 11))
                if not last:
                    m_low(2, 0, 12 * h + (4 * UC + 13))
                pool.wait_ge(gv_done, h + 1)
                rsqrt(stat[:, 18:20], stat[:, 16:18], 2).then_inc(gp_done, 1)

            with pool.Fori(0, HEADS - 1) as h:
                step.enter(h, 6)
                head(h, False)
            step.leave(HEADS - 1)
            head(HEADS - 1, True)
            pool.wait_ge(lnv_done, 2)
            rsqrt(stat[:, 18:20], stat[:, 16:18], TT).then_inc(lnp_done, 1)
            for g in range(UC):
                m_low(GATES[g][0] + 1, 1, 2 * (M_GATES + 2 * g) + 3)
            for t in range(TT):
                pool.wait_ge(vr_done, 4 + t)
                rsqrt(stat[:, 6 + t:7 + t], stat[:, 3 + t:4 + t], 1).then_inc(pow_done, 1)
            pool.wait_ge(x3_rdy, TT + 1)
            pool.tensor_tensor(xres[:, :, :], xres[:, :, :], x3[:, 1, :, :], ALU.subtract).then_inc(xr_rdy, 1)
            pool.wait_ge(table_done, 4)
            nb = pool.value_load(nblocks[0:1, 0:1], min_val=NE, max_val=MAXB - 1)

            def low(b, k):
                cols_ = slice(HW // 2, HW) if k % HALVES == 5 else slice(0, HW)
                pool.wait_ge(hi_done, 24 * b + (k + 1))
                pool.tensor_tensor(wlo[:, k % HS, cols_], raw_half(k)[:, cols_], whi[:, k % HS, cols_].bitcast(F32),
                                   ALU.subtract).then_inc(lo_p, 1)

            with pool.Fori(0, nb) as b:
                for k in range(STEPS * HALVES):
                    if k % HALVES > 3:
                        low(b, k)
            for c, cols_ in enumerate((slice(0, HW), slice(HW // 2, HW))):
                pool.wait_ge(hi_done, 24 * nb + (c + 1))
                pool.tensor_tensor(wlo[:, c, cols_], raw_half(4 + c)[:, cols_], whi[:, c, cols_].bitcast(F32),
                                   ALU.subtract).then_inc(lo_p, 1)
            for t in range(TT):
                pool.wait_ge(vr_done, 6 + t)
                rsqrt(stat[:, 6 + t:7 + t], stat[:, 3 + t:4 + t], 1).then_inc(pow_done, 1)

        @block.tensor
        def _(pe):
            def copyT(o, i, n):
                return pe.transpose(o, i, ident[0:n, 0:n])

            pe.wait_ge(masked, 2)
            pe.wait_ge(par_in, 16 * 7)
            for r, n in enumerate((P, P, NPAR - 2 * P)):
                copyT(pb[:, 0, r * P:r * P + n], prow[0:n, r, :], n).then_inc(cols, 1)
            for t in (0, 1, 2):
                pe.wait_ge(xn_done, t + 1)
                n = META if t == 2 else P
                for k in range(KC):
                    o = pb[:, 1, k * META:(k + 1) * META] if t == 2 else pb[:, 4 + 2 * t + k // 4, (k % 4) * P:(k % 4 + 1) * P]
                    ins = copyT(o, xn[0:n, t, k * P:(k + 1) * P], n)
                ins.then_inc(cols, 1)
            pe.wait_ge(nlo_done, 3)

            def project(s, use, fill, bank, t0, free, full, rhs):
                pe.wait_ge(landed[s], 16 * use)
                pe.wait_ge(free, 2 * fill)
                for j in range(2):
                    for k in range(KC):
                        ins = pe.matmul(pb[:, bank + j, 0:TALL - t0], ring[:, s, k, j * P:(j + 1) * P], rhs[:, k, :],
                                        start=(k == 0), stop=(k == KC - 1))
                    ins.then_inc(full, 1)

            def split_project(low, n, odd, fill, bank, t0, free, full):
                pe.wait_ge(free, 2 * fill)
                for c in range(2):
                    pe.wait_ge(low, n + c)
                    x = 2 * odd + c
                    for j in range(2):
                        for k in range(KC // 2):
                            wh, wl = (w[:, x, k * UNIT + j * P:k * UNIT + (j + 1) * P] for w in (whi, wlo))
                            first, last = c == 0 and k == 0, c == 1 and k == KC // 2 - 1
                            kc = c * KC // 2 + k
                            o, xh, xl = pb[:, bank + j, 0:TALL - t0], nhi[:, kc, t0:TALL], nlo[:, kc, t0:TALL]
                            pe.matmul(o, wh, xh, start=first, stop=False)
                            pe.matmul(o, wh, xl, start=False, stop=False)
                            ins = pe.matmul(o, wl, xh, start=False, stop=last)
                        if c:
                            ins.then_inc(full, 1)
                    if c == 0:
                        ins.then_inc(m_used, 1)

            with pe.Fori(0, 4) as i:
                split_project(m_lop, 4 * i + 1, 0, i + 1, 0, 0, a_free, a_full)
                split_project(m_lop, 4 * i + 3, 1, i + 1, 2, 0, b_free, b_full)

            def turn_y(h1):
                pe.wait_ge(yn_done, 2 * h1 - 1)
                for c in range(VC):
                    for t in range(TT):
                        ins = copyT(pb[:, 4 + 3 * (c // 2), (c % 2) * REAL + t * P:(c % 2) * REAL + (t + 1) * P],
                                    yn[:, t, c * P:(c + 1) * P], P)
                    ins.then_inc(yt_done, 1)

            with pe.Fori(0, HEADS) as h:
                split_project(m_lop, 6 * h + 17, 0, 3 * h + 5, 0, META, a_free, a_full)
                split_project(m_lop, 6 * h + 19, 1, 3 * h + 5, 2, 0, b_free, b_full)
                split_project(m_lov, 6 * h + 1, 0, 3 * h + 6, 0, 0, a_free, a_full)
                turn_y(h + 1)
                split_project(m_lov, 6 * h + 3, 1, 3 * h + 6, 2, 0, b_free, b_full)
                split_project(m_lov, 6 * h + 5, 0, 3 * h + 7, 0, META, a_free, a_full)
                pe.wait_ge(a_free, 6 * h + 14)
                pe.wait_ge(b_free, 6 * h + 14)
                pe.wait_ge(rt_done, 4 * h + 4)
                for bank, t0, n in ((4, META, P), (5, META + P, P), (6, 0, META)):
                    for c in range(VC):
                        ins = copyT(pb[0:n, bank, c * P:(c + 1) * P], vT[:, c, t0:t0 + n], P)
                    ins.then_inc(vt_done, 1)
                pe.wait_ge(rope_done, 2 * h + 3)
                for c in range(2):
                    ins = pe.matmul(pb[:, 7, 0:REAL], krot[:, c, META:META + P], qrot[:, c, :],
                                    start=(c == 0), stop=(c == 1))
                ins.then_inc(sc_done, 1)
                for c in range(2):
                    ins = pe.matmul(pb[0:META, 7, REAL:2 * REAL], krot[:, c, 0:META], qrot[:, c, :],
                                    start=(c == 0), stop=(c == 1))
                ins.then_inc(sc_done, 1)
                split_project(m_lop, 6 * h + 21, 1, 3 * h + 7, 2, META, b_free, b_full)
                pe.wait_ge(v_done, 3 * h + 3)
                for c in range(2):
                    ins = pe.matmul(pb[:, 4, 0:P], krot[:, c, META + P:TALL], qrot[:, c, P:REAL],
                                    start=(c == 0), stop=(c == 1))
                ins.then_inc(sc_done, 1)
                pe.wait_ge(s_done, 3 * h + 2)
                pe.matmul(pb[:, 5, :], sM[0:META, 0:P], vM[0:META, :], start=True, stop=False)
                pe.matmul(pb[:, 5, :], sA[:, 0:P], vsb[:, 0, :], start=False, stop=True).then_inc(y_done, 1)
                pe.matmul(pb[:, 6, :], sM[0:META, P:REAL], vM[0:META, :], start=True, stop=False)
                pe.matmul(pb[:, 6, :], sA[:, P:REAL], vsb[:, 0, :], start=False, stop=False)
                pe.wait_ge(s_done, 3 * h + 3)
                pe.matmul(pb[:, 6, :], sB[:, 0:P], vsb[:, 1, :], start=False, stop=True).then_inc(y_done, 1)

            def channel_sum(src, fill):
                pe.wait_ge(b_free, 2 * fill)
                for k in range(KC):
                    ins = pe.matmul(pb[:, 2, 0:REAL], ones[:, :], src[:, k, :], start=(k == 0), stop=(k == KC - 1))
                    if k in (0, KC - 1):
                        ins.then_inc(b_full, 1)

            pe.wait_ge(conv_step, 4 * 62)
            channel_sum(cv, 17)
            turn_y(HEADS + 1)
            pe.wait_ge(rt_done, 4 * (HEADS + 1))
            for r in range(UC):
                s0, use = RET[r]
                pe.wait_ge(landed[s0], 16 * use)
                pe.wait_ge(landed[s0 + 1], 16 * use)
                pe.wait_ge(a_free, 2 * (r + 17))
                for j in range(2):
                    for k in range(2 * KC):
                        ins = pe.matmul(pb[:, j, 0:REAL], ring[:, s0 + k // KC, k % KC, j * P:(j + 1) * P],
                                        rT[:, VC + k, :], start=(k == 0), stop=(k == 2 * KC - 1))
                    ins.then_inc(a_full, 1)
                if r == 0:
                    pe.wait_ge(lsq_done, 1)
                    channel_sum(sq, 18)
                if r == 1:
                    pe.wait_ge(lnd_done, 1)
                    pe.wait_ge(b_free, 2 * 19)
                    pe.matmul(pb[:, 2, 0:REAL], ones[:, :], lnd, start=True, stop=True).then_inc(b_full, 2)
            for g in range(UC):
                split_project(m_lov, 6 * HEADS + 2 * g + 1, 0, g + 21, 0, META, a_free, a_full)
                split_project(m_lop, 16 + 6 * HEADS + 2 * g + 1, 1, g + 20, 2, META, b_free, b_full)
            pe.wait_ge(ln_done, KC)
            for i in range(2):
                s0, use = CONV[i]
                project(s0, use, i + 25, 0, META, a_free, a_full, cv)
                project(s0 + 1, use, i + 24, 2, META, b_free, b_full, cv)
            pe.wait_ge(merged, KC)
            pe.wait_ge(a_free, 2 * 27)
            pe.wait_ge(b_free, 2 * 26)
            for n in range(UC):
                s0, use = MIX[n // 2]
                pe.wait_ge(landed[s0 + n % 2], 16 * use)
                for t in range(TT):
                    for k in range(KC):
                        ins = pe.matmul(pb[:, n, t * UNIT:(t + 1) * UNIT], yret[:, k, t * P:(t + 1) * P],
                                        ring[:, s0 + n % 2, k, :], start=(k == 0), stop=(k == KC - 1))
                ins.then_inc((a_full, b_full)[n // 2], 1)
            for t in range(TT):
                pe.wait_ge(xn_done, 4 + t)
                for k in range(KC):
                    ins = copyT(pb[:, 4 + 2 * t + k // 4, (k % 4) * P:(k % 4 + 1) * P], xn2[:, t, k * P:(k + 1) * P], P)
                ins.then_inc(x2t, 1)
            pe.wait_ge(rout_in, 32)
            for t in range(TT):
                pe.wait_ge(x2e, t + 1)
                for k in range(KC):
                    ins = pe.matmul(pb[:, 4 + t, 0:NE], xn2T[:, k, t * P:(t + 1) * P], wr[:, k, :],
                                    start=(k == 0), stop=(k == KC - 1))
                ins.then_inc(lgt, 1)
            pe.wait_ge(route, 2)
            pe.wait_ge(lgt_read, 2)
            pe.matmul(pb[:, 6, 0:NE], before[:, :], mask[:, 0, :], start=True, stop=True).then_inc(w_used, 1)
            pe.matmul(pb[:, 6, NE:2 * NE], before[:, :], mask[:, 1, :], start=True, stop=False).then_inc(w_used, 1)
            pe.matmul(pb[:, 6, NE:2 * NE], ones[:, :], mask[:, 0, :], start=False, stop=True).then_inc(w_used, 1)
            pe.matmul(pb[:, 6, 2 * NE:3 * NE], ones[:, :], mask[:, 0, :], start=True, stop=False).then_inc(w_used, 1)
            pe.matmul(pb[:, 6, 2 * NE:3 * NE], ones[:, :], mask[:, 1, :], start=False, stop=True).then_inc(rank_done, 1)

            def gather():
                for k in range(KC):
                    for n in range(PARTS * TT):
                        ins = pe.matmul(pb[:, 7, k * SLOTS:(k + 1) * SLOTS], x3[:, n % PARTS, n // PARTS, k * P:(k + 1) * P],
                                        onehot[:, n // PARTS, :], start=(n == 0), stop=(n == PARTS * TT - 1))
                ins.then_inc(gathered, 1)

            def split_product(pairs, stop):
                ins = None
                for m, (x, y) in enumerate(((0, 0), (0, 1), (1, 0))):
                    for o, st, mv in pairs:
                        ins = pe.matmul(o, st[x], mv[y], start=False, stop=(stop and m == 2), skip_group_check=True)
                return ins

            def low_ready(b, k):
                pe.wait_ge(lo_v if k % HALVES < 4 else lo_p, lo_count(b, k))

            def hidden(b, k, stop):
                up = k % HALVES // 2
                low_ready(b, k)
                for r in range(KC // 2):
                    c = k % 2 * (KC // 2) + r
                    mv = [w[:, k % HS, r * UNIT:(r + 1) * UNIT] for w in (whi, wlo)]
                    ins = split_product([(pb[0:SLOTS, 4, up * UNIT:(up + 1) * UNIT], (xhi[:, c, :], xlo[:, c, :]), mv)],
                                        stop and r == KC // 2 - 1)
                ins.then_inc(w_used, 1)

            def down(k, stop):
                st = (ahi[:, k % 2, :], alo[:, k % 2, :])
                split_product([(pb[0:SLOTS, 5 + c, :], st, [w[:, k % HS, c * 512:(c + 1) * 512] for w in (whi, wlo)])
                               for c in range(2)], stop).then_inc(w_used, 1)

            def turn_act(n):
                pe.wait_ge(act_rdy, n + 1)
                for c in range(2):
                    ins = pe.matmul(pb[:, 7, c * SLOTS:(c + 1) * SLOTS], act[:, c * P:(c + 1) * P],
                                    ident[0:SLOTS, 0:SLOTS], start=True, stop=True)
                ins.then_inc(turned, 1)

            def turn_gates():
                for t in range(TT):
                    ins = pe.matmul(pb[0:SLOTS, 7, t * P:(t + 1) * P], gatehot[:, t, :], ident[:, :],
                                    start=True, stop=True)
                ins.then_inc(ght_done, 1)

            def scatter(stop):
                for t in range(TT):
                    for n in range(4):
                        c, part = n // 2, (yhi, ylo)[n % 2]
                        ins = pe.matmul(pb[:, 2 * t + c, :], hotT[:, t * P:(t + 1) * P], part[:, c * 512:(c + 1) * 512],
                                        start=False, stop=stop and n % 2 == 1, skip_group_check=True)
                return ins

            pe.wait_ge(x3_rdy, TT + PARTS - 1)
            pe.wait_ge(hot_rdy, 2)
            gather()
            pe.wait_ge(h2_done, 4)
            for t in range(TT):
                for c in range(2):
                    pe.matmul(pb[:, 2 * t + c, :], ident[:, :], hx[:, t, c * 512:(c + 1) * 512],
                              start=True, stop=False, skip_group_check=True)
            pe.wait_ge(b3_step, 6)
            pe.wait_ge(zeroed, 1)
            pe.wait_ge(gh_rdy, 1)
            pe.wait_ge(xlo_rdy, 1)
            turn_gates()
            pe.wait_ge(table_done, 4)
            nb = pe.value_load(nblocks[0:1, 0:1], min_val=NE, max_val=MAXB - 1)
            with pe.Fori(0, nb) as b:
                for q in range(STEPS):
                    k = q * HALVES
                    if q == 0:
                        pe.wait_ge(xlo_rdy, b + 1)
                        pe.wait_ge(sel_rdy, b + 1)
                    pe.wait_ge(clip_rdy, 4 * b + (q + 1))
                    pe.matmul(pb[0:SLOTS, 4, :], pick_e[:, :],
                              bias3[:, 0:2 * D].rearrange("p (u n) -> p u n", u=2)[:, :, q * UNIT:(q + 1) * UNIT],
                              start=True, stop=False, skip_group_check=True)
                    hidden(b, k, False)
                    hidden(b, k + 1, True)
                    if q == 0:
                        pe.wait_ge(hotT_rdy, b + 1)
                    turn_act(4 * b + (q + 1))
                    hidden(b, k + 2, False)
                    hidden(b, k + 3, True)
                    if q == 3:
                        pe.wait_ge(hot_rdy, 2 * b + 4)
                        pe.wait_ge(alo_rdy, 4 * b + (q + 1))
                        gather()
                        pe.wait_ge(hotT_rdy, b + 1)
                        pe.wait_ge(ylo_rdy, b + 1)
                        scatter(False)
                    pe.wait_ge(alo_rdy, 4 * b + (q + 1))
                    if q == 1:
                        pe.wait_ge(ylo_rdy, b + 1)
                        for c in range(2):
                            pe.matmul(pb[0:SLOTS, 5 + c, :], pick_e[:, :], bias3[:, 2 * D + c * 512:2 * D + (c + 1) * 512],
                                      start=True, stop=False, skip_group_check=True)
                    low_ready(b, k + 4)
                    down(k + 4, False)
                    pe.wait_ge(lo_v, 20 * b + (5 * q + 5))
                    low_ready(b, k + 5)
                    down(k + 5, q == 0)
                    if q == 3:
                        pe.wait_ge(gh_rdy, 2 * b + 3)
                        pe.wait_ge(xlo_rdy, b + 2)
                        turn_gates()
            pe.wait_ge(hotT_rdy, nb + 1)
            turn_act(4 * nb + 1)
            pe.wait_ge(alo_rdy, 4 * nb + 1)
            pe.wait_ge(lo_p, 8 * nb + 1)
            down(4, False)
            pe.wait_ge(lo_v, 20 * nb + 1)
            pe.wait_ge(lo_p, 8 * nb + 2)
            down(5, True)
            pe.wait_ge(ylo_rdy, nb + 1)
            scatter(True).then_inc(acc_done, 1)

        @block.scalar
        def _(sc):
            rows = {0: a["conv_dw_w"][0].rearrange("w (c p) -> (w c) p", p=P)}
            sc.dma_start(prow[:, 0, :], rows[0][0:P, :]).then_inc(par_in, 16)
            sc.dma_start(prow[0:TAPS * KC - P, 1, :], rows[0][P:TAPS * KC, :]).then_inc(par_in, 16)
            for name, r0, n in (("conv_dw_b", TAPS * KC, KC), ("conv_ln_w", LNW, KC), ("conv_ln_b", LNB, KC),
                                ("b_conv_out", BCO, KC), ("ret_gn_w", GNW, 4 * VC)):
                sc.dma_start(prow[r0 % P:r0 % P + n, r0 // P, :],
                             a[name][0].rearrange("(c p) -> c p", p=P)).then_inc(par_in, 16)

            for t in range(3):
                rows_ = META if t == 2 else P
                if t == 2:
                    sc.wait_ge(meta_in, 16)
                else:
                    sc.wait_ge(x_in, 32)
                if t:
                    sc.wait_ge(sq_done, t)
                sc.activation(junk1[0:rows_, :], hm[0:META, :] if t == 2 else hx[:, t, :], ACT.Square,
                              accum_out=stat[0:rows_, t:t + 1]).then_inc(sq_done, 1)
            for q in range(3):
                sc.dma_start(brows[q * NE:(q + 1) * NE, 0:2 * D], a["b_gate_up"][0]).then_inc(bias_in, 16)
                sc.dma_start(brows[q * NE:(q + 1) * NE, 2 * D:3 * D], a["b_down"][0]).then_inc(bias_in, 16)
            sc.dma_start(eid[:, :], a["eid"]).then_inc(eid_in, 16)
            sc.dma_start(decay[:, :, :], a["decay"]).then_inc(tab_in, 16)
            sc.dma_start(cos, a["cos"]).then_inc(tab_in, 16)
            sc.dma_start(sin, a["sin"]).then_inc(tab_in, 16)

            def bias_part(rows):
                sc.activation(bias3[rows, :], brows[rows, :], ACT.Copy).then_inc(b3_step, 1)

            def m_high(s, use, odd, used, full, n):
                sc.wait_ge(landed[s], 16 * use)
                for c in range(2):
                    if full:
                        sc.wait_ge((m_used, full)[c], (used, n)[c])
                    sc.activation(whi[:, 2 * odd + c, :], m_raw(s, c), ACT.Copy).then_inc(m_hi, 1)

            m_high(0, 1, 0, None, None, None)
            m_high(1, 1, 1, None, None, None)
            sc.wait_ge(cols, 3)
            sc.activation(par[:, 0:P], pb[:, 0, 0:P], ACT.Copy).then_inc(a_free, 1)
            sc.activation(par[:, P:NPAR], pb[:, 0, P:NPAR], ACT.Copy).then_inc(a_free, 1)
            for t in range(3):
                sc.wait_ge(cols, 4 + t)
                if t < 2:
                    src = pb[:, 4 + 2 * t:6 + 2 * t, :].rearrange("p b (k n) -> p (b k) n", n=P)
                    dst = nhi[:, :, META + t * P:META + (t + 1) * P]
                else:
                    src = pb[:, 1, 0:KC * META].rearrange("p (k n) -> p k n", n=META)
                    dst = nhi[:, :, 0:META]
                sc.activation(dst, src, ACT.Copy).then_inc(colse, 1)

            sc.wait_ge(bias_in, 16 * 6)
            bias_part(slice(0, 3 * NE))

            def round_(i, sa, sb_, use):
                m_high(sa, use, 0, 2 * i + 1, a_full, 2 * i + 2)
                for j in range(2):
                    sc.wait_ge(b_full, 2 * i + (1 + j))
                    if j == 0:
                        sc.wait_ge(a_free, 2 * i + 2)
                    sc.activation(sigb[:, j, :], pb[:, 2 + j, 0:TALL], ACT.Sigmoid).then_inc(b_free, 1)
                m_high(sb_, use, 1, 2 * i + 2, b_full, 2 * i + 2)

            with sc.Fori(0, UC - 1) as i:
                round_(i, 0, 1, i + 2)
            sc.wait_ge(b3_step, 2)
            bias_part(slice(NE, 2 * NE))
            bias_part(slice(2 * NE, 3 * NE))
            round_(UC - 1, 2, 3, 1)
            sc.wait_ge(b3_step, 5)
            bias_part(slice(2 * NE, 3 * NE))

            def head(h, last):
                sc.wait_ge(rope_done, 2 * h + 1)
                for j in range(2):
                    sc.wait_ge(a_full, 6 * h + (9 + j))
                    sc.activation(qraw[:, j, :], pb[:, j, 0:REAL], ACT.Copy).then_inc(a_free, 1)
                m_high(4, h + 1, 0, 6 * h + 9, a_full, 6 * h + 10)
                for j in range(2):
                    sc.wait_ge(b_full, 6 * h + (9 + j))
                    sc.activation(kraw[:, j, :], pb[:, 2 + j, 0:TALL], ACT.Copy).then_inc(b_free, 1)
                m_high(5, h + 1, 1, 6 * h + 10, b_full, 6 * h + 10)
                for c in range(2):
                    full, free = ((a_full, a_free), (b_full, b_free))[c]
                    for j in range(2):
                        sc.wait_ge(full, 6 * h + (11 + j))
                        sc.activation(vT[:, 2 * c + j, :], pb[:, 2 * c + j, 0:TALL], ACT.Copy).then_inc(free, 1)
                    m_high(c, h + 5, c, 6 * h + (11 + c), full, 6 * h + 12)
                sc.wait_ge(rt_done, 4 * h + 4)
                for j in range(2):
                    sc.wait_ge(a_full, 6 * h + (13 + j))
                    sc.activation(sg[:, j, :], pb[:, j, 0:REAL], ACT.Silu).then_inc(a_free, 1)
                sc.wait_ge(vt_done, 3 * h + 1)
                sc.activation(vsb[:, 0, :], pb[:, 4, :], ACT.Copy).then_inc(v_done, 1)
                sc.wait_ge(vt_done, 3 * h + 2)
                sc.activation(vsb[:, 1, :], pb[:, 5, :], ACT.Copy).then_inc(v_done, 1)
                sc.wait_ge(vt_done, 3 * h + 3)
                sc.activation(vM[0:META, :], pb[0:META, 6, :], ACT.Copy).then_inc(v_done, 1)
                if not last:
                    m_high(2, h + 2, 0, 6 * h + 13, a_full, 6 * h + 14)
                for j in range(2):
                    sc.wait_ge(b_full, 6 * h + (13 + j))
                    sc.activation(sg[:, 2 + j, :], pb[:, 2 + j, 0:REAL], ACT.Silu).then_inc(b_free, 1)
                if not last:
                    m_high(3, h + 2, 1, 6 * h + 14, b_full, 6 * h + 14)

            with sc.Fori(0, HEADS - 1) as h:
                head(h, False)
            head(HEADS - 1, True)

            sc.wait_ge(xc_done, 2)
            sc.activation(sq, cv[:, :, :], ACT.Square).then_inc(lsq_done, 1)

            def gate_high(g, b):
                s0, use = GATES[g]
                n = 2 * (19 + g + (not b)) if g else 32
                m_high(s0 + b, use, b, M_GATES + 2 * g + b - 1, (a_full, b_full)[b], n)

            for r in range(UC):
                if r == UC - 1:
                    gate_high(0, 0)
                    gate_high(0, 1)
                    for k in range(KC):
                        if k % (KC // 2) == 0:
                            sc.wait_ge(lnx_done, 1 + k // (KC // 2))
                        sc.activation(cv[:, k, :], cv[:, k, :], ACT.Silu, scale=par[:, LNW + k:LNW + k + 1],
                                      bias=par[:, LNB + k:LNB + k + 1]).then_inc(ln_done, 1)
                for j in range(2):
                    sc.wait_ge(a_full, 2 * r + (33 + j))
                    sc.activation(yret[:, 2 * r + j, :], pb[:, j, 0:REAL], ACT.Copy).then_inc(a_free, 1)
            for g in range(UC):
                if g < UC - 1:
                    gate_high(g + 1, 0)
                for j in range(2):
                    sc.wait_ge(a_full, 2 * g + (41 + j))
                    sc.activation(sga[:, 2 * g + j, :], pb[:, j, 0:REAL], ACT.Sigmoid).then_inc(a_free, 1)
                if g < UC - 1:
                    gate_high(g + 1, 1)
                for j in range(2):
                    sc.wait_ge(b_full, 2 * g + (39 + j))
                    sc.activation(sgb[:, 2 * g + j, :], pb[:, 2 + j, 0:REAL], ACT.Sigmoid).then_inc(b_free, 1)

            sc.wait_ge(h2_done, 4)
            for t in range(TT):
                if t:
                    sc.wait_ge(sq_done, 3 + t)
                sc.activation(junk2, hx[:, t, :], ACT.Square, accum_out=stat[:, t:t + 1]).then_inc(sq_done, 1)
            for t in range(TT):
                sc.wait_ge(xn_done, 4 + t)
                sc.activation(x3[:, 0, t, :], xn2[:, t, :], ACT.Copy).then_inc(x3_rdy, 1)
            for t in range(TT):
                sc.wait_ge(x2t, t + 1)
                sc.activation(xn2T[:, :, t * P:(t + 1) * P],
                              pb[:, 4 + 2 * t:6 + 2 * t, :].rearrange("p b (k n) -> p (b k) n", n=P),
                              ACT.Copy).then_inc(x2e, 1)
            sc.wait_ge(xr_rdy, 1)
            sc.activation(x3[:, 1, :, :], xres[:, :, :], ACT.Copy).then_inc(x3_rdy, 1)
            for t in range(TT):
                sc.wait_ge(shift_done, t + 1)
                sc.activation(gate4[:, t, :], gate4[:, t, :], ACT.Exp, accum_out=stat[:, 10 + t:11 + t]).then_inc(exp_done, 1)
            sc.wait_ge(xr_rdy, 2)
            sc.activation(x3[:, 2, :, :], xres[:, :, :], ACT.Copy).then_inc(x3_rdy, 1)

            def tokens(n):
                sc.wait_ge(gathered, n)
                sc.activation(xhi[:, :, :], pb[:, 7, :].rearrange("p (k n) -> p k n", n=SLOTS), ACT.Copy).then_inc(xhi_rdy, 1)

            tokens(1)
            sc.wait_ge(table_done, 4)
            nb = sc.value_load(nblocks[0:1, 0:1], min_val=NE, max_val=MAXB - 1)

            def high(b, k):
                if k % 2 == 0:
                    sc.wait_ge(e_in[k // 2 % 6], 32 * b + 16 * (1 + k // 12))
                sc.wait_ge(w_used, 24 * b + (k + 1))
                sc.activation(whi[:, k % HS, :], raw_half(k), ACT.Copy).then_inc(hi_done, 1)

            def sigmoid(n):
                sc.wait_ge(min_rdy, n)
                sc.activation(sig, hg, ACT.Sigmoid, scale=ALPHA).then_inc(sig_rdy, 1)

            def act_high(n):
                sc.wait_ge(turned, n)
                sc.activation(ahi[:, :, :], pb[:, 7, 0:2 * SLOTS].rearrange("p (k n) -> p k n", n=SLOTS),
                              ACT.Copy).then_inc(ahi_rdy, 1)

            def slot_gates(n):
                sc.wait_ge(ght_done, n)
                sc.activation(gates, pb[0:SLOTS, 7, 0:REAL], ACT.Copy, accum_out=gslot).then_inc(gslot_rdy, 1)

            def out_high(b):
                sc.wait_ge(w_used, 24 * b + (HS + 6))
                sc.activation(yhi[:, :], pb[0:SLOTS, 5:7, :].rearrange("p a b -> p (a b)"), ACT.Copy, scale=gslot).then_inc(yhi_rdy, 1)

            with sc.Fori(0, nb) as b:
                sc.activation(stat[:, 20:21], mhalf[:, :], ACT.Sigmoid)
                for q in range(STEPS):
                    k = q * HALVES
                    high(b, k)
                    sigmoid(4 * b + (q + 1))
                    high(b, k + 1)
                    if q == 0:
                        slot_gates(b + 1)
                    high(b, k + 2)
                    if q == 1:
                        out_high(b)
                    high(b, k + 3)
                    high(b, k + 4)
                    act_high(4 * b + (q + 1))
                    high(b, k + 5)
                    if q == 3:
                        tokens(b + 2)
            sigmoid(4 * nb + 1)
            slot_gates(nb + 1)
            act_high(4 * nb + 1)
            sc.wait_ge(e_in[2], 32 * nb + 16)
            for k in (4, 5):
                sc.wait_ge(w_used, 24 * nb + (k - 3))
                sc.activation(whi[:, k % HS, :], raw_half(k), ACT.Copy).then_inc(hi_done, 1)
            sc.wait_ge(w_used, 24 * nb + (HS + 2))
            sc.activation(yhi[:, :], pb[0:SLOTS, 5:7, :].rearrange("p a b -> p (a b)"), ACT.Copy, scale=gslot).then_inc(yhi_rdy, 1)
            sc.wait_ge(acc_done, 1)
            for t in range(TT):
                if t:
                    sc.wait_ge(sq_done, 5 + t)
                sc.activation(junk2, pb[:, 2 * t:2 * t + 2, :].rearrange("p a b -> p (a b)"), ACT.Square,
                              accum_out=stat[:, t:t + 1]).then_inc(sq_done, 1)

        @block.vector
        def _(dve):
            def variance(t, rows, n):
                dve.wait_ge(sq_done, n)
                dve.tensor_scalar(stat[0:rows, 3 + t:4 + t], stat[0:rows, t:t + 1], 1.0 / D, EPS, ALU.mult,
                                  ALU.add).then_inc(vr_done, 1)

            dve.memset(bias3[3 * NE:P, :], 0.0).then_inc(zeroed, 1)
            for c in (22, 23):
                dve.memset(stat[:, c:c + 1], 0.0).then_inc(b_free, 1)
            dve.wait_ge(wmb_in, 16)
            for t in range(3):
                variance(t, META if t == 2 else P, t + 1)
            for t in range(3):
                rows = META if t == 2 else P
                dve.wait_ge(pow_done, t + 1)
                dve.scalar_tensor_tensor(out=xn[0:rows, t, :], in0=hm[0:META, :] if t == 2 else hx[:, t, :],
                                         scalar=stat[0:rows, 6 + t:7 + t], in1=wmb[0:rows, :], op0=ALU.mult,
                                         op1=ALU.mult).then_inc(xn_done, 1)

            for t in range(3):
                dve.wait_ge(colse, t + 1)
                if t < 2:
                    src = pb[:, 4 + 2 * t:6 + 2 * t, :].rearrange("p b (k n) -> p (b k) n", n=P)
                    tok = slice(META + t * P, META + (t + 1) * P)
                else:
                    src = pb[:, 1, 0:KC * META].rearrange("p (k n) -> p k n", n=META)
                    tok = slice(0, META)
                dve.tensor_tensor(nlo[:, :, tok], src, nhi[:, :, tok].bitcast(F32), ALU.subtract).then_inc(nlo_done, 1)

            def m_low(s, odd, n):
                for c in range(2):
                    dve.wait_ge(m_hi, n + c)
                    dve.tensor_tensor(wlo[:, 2 * odd + c, :], m_raw(s, c), whi[:, 2 * odd + c, :].bitcast(F32),
                                      ALU.subtract).then_inc(m_lov, 1)

            dve.wait_ge(consts, 9)
            dve.wait_ge(a_free, 2)
            taps = par[:, 0:256].rearrange("p (w c) -> p w c", c=KC)
            step = Chain(dve, conv_step)

            def gated_input(i):
                for j in range(2):
                    dve.wait_ge(a_full, 2 * i + (1 + j))
                    dve.wait_ge(b_free, 2 * i + (3 + j))
                    dve.tensor_tensor(upad[:, bass.ds(2 * i + j, 1), PADL:PADL + TALL], pb[:, j:j + 1, 0:TALL],
                                      sigb[:, j:j + 1, :], ALU.mult).then_inc(a_free, 1)

            def convolve(i, second):
                if not second:
                    dve.tensor_copy(wt[:, :, :], taps[:, :, bass.ds(2 * i, 2)]).then_inc(wt_done, 1)
                    dve.wait_ge(wt_done, i + 1)
                    dve.wait_ge(a_free, 2 * i + 4)
                for w in range(TAPS // 2, TAPS) if second else range(TAPS // 2):
                    for j in range(2):
                        u = upad[:, bass.ds(2 * i + j, 1), w:w + REAL]
                        if w == 0:
                            ins = dve.tensor_scalar(cacc[:, j:j + 1, :], u, wt[:, 0, j:j + 1], wt[:, TAPS, j:j + 1],
                                                    ALU.mult, ALU.add)
                        else:
                            step.wait(1)
                            o = cacc[:, j:j + 1, :] if w < TAPS - 1 else cv[:, bass.ds(2 * i + j, 1), :]
                            ins = dve.scalar_tensor_tensor(out=o, in0=u, scalar=wt[:, w, j:j + 1],
                                                           in1=cacc[:, j:j + 1, :], op0=ALU.mult, op1=ALU.add)
                        step.did(ins)
                if second:
                    step.wait()

            with dve.Fori(0, 2) as i:
                step.enter(i, 62)
                for second in range(2):
                    gated_input(2 * i + second)
                    convolve(i, second)
            step.leave(2)

            dve.wait_ge(tab_in, 48)
            dve.wait_ge(b3_step, 6)
            gn = Chain(dve, gn_step)

            def gate_y(h, h1):
                dve.wait_ge(a_free, 6 * h1 + 4)
                dve.wait_ge(b_free, 6 * h1 + 4)
                for c in range(VC):
                    dve.wait_ge(yt_done, 4 * h1 - (2 if c < 2 else 0))
                    src = pb[:, 4 + 3 * (c // 2), (c % 2) * REAL:(c % 2 + 1) * REAL].rearrange("p (o n) -> p o n", o=1)
                    if isinstance(h, int):
                        o, w = rT[:, h * VC + c:h * VC + c + 1, :], par[:, GNW - VC + h * VC + c:GNW - VC + h * VC + c + 1]
                    else:
                        o, w = rT[:, bass.ds(h * VC + c, 1), :], par[:, bass.ds(h * VC + (GNW - VC + c), 1)]
                    dve.scalar_tensor_tensor(out=o, in0=src, scalar=w, in1=sg[:, c:c + 1, :], op0=ALU.mult,
                                             op1=ALU.mult).then_inc(rt_done, 1)

            def head(h, i, second):
                m_low(4, 0, 12 * h + (4 * UC + 5))
                m_low(5, 1, 12 * h + (4 * UC + 7))
                gate_y(h, h + 1)
                m_low(0, 0, 12 * h + (4 * UC + 9))
                convolve(i + 2, second)
                dve.wait_ge(sc_done, 3 * h + 2)
                dve.tensor_tensor(sA.rearrange("p (o n) -> p o n", o=1), pb[:, 7:8, 0:REAL],
                                  decay[:, bass.ds(h, 1), 0:REAL], ALU.mult).then_inc(s_done, 1)
                dve.tensor_tensor(sM[0:META, :].rearrange("p (o n) -> p o n", o=1), pb[0:META, 7:8, REAL:2 * REAL],
                                  decay[0:META, bass.ds(h, 1), META:TALL], ALU.mult).then_inc(s_done, 1)
                dve.wait_ge(sc_done, 3 * h + 3)
                dve.tensor_tensor(sB.rearrange("p (o n) -> p o n", o=1), pb[:, 4:5, 0:P],
                                  decay[:, bass.ds(h, 1), 0:P], ALU.mult).then_inc(s_done, 1)
                for t in range(TT):
                    dve.wait_ge(y_done, 2 * h + (1 + t))
                    gn.did(dve.bn_stats(bst[:, t, :], pb[:, 5 + t, :]))
                gn.wait()
                gn.did(dve.tensor_tensor(bmv[:, :, 1], bst[:, :, 1], bst[:, :, 4], ALU.add))
                gn.did(dve.tensor_tensor(bmv[:, :, 2], bst[:, :, 1], bst[:, :, 4], ALU.subtract))
                gn.did(dve.tensor_tensor(bmv[:, :, 3], bst[:, :, 2], bst[:, :, 5], ALU.add))
                gn.wait()
                gn.did(dve.tensor_scalar(bmv[:, :, 0], bmv[:, :, 1], 0.5, None, ALU.mult))
                gn.did(dve.scalar_tensor_tensor(out=bmv[:, :, 2], in0=bmv[:, :, 2], scalar=0.25, in1=bmv[:, :, 2],
                                                op0=ALU.mult, op1=ALU.mult))
                gn.did(dve.tensor_scalar(bmv[:, :, 3], bmv[:, :, 3], 1.0 / DV, EPS, ALU.mult, ALU.add))
                gn.wait()
                dve.tensor_tensor(stat[:, 16:18], bmv[:, :, 2], bmv[:, :, 3], ALU.add).then_inc(gv_done, 1)
                dve.wait_ge(gp_done, h + 1)
                for t in range(TT):
                    dve.tensor_scalar(yn[:, t, :], pb[:, 5 + t, :], bmv[:, t, 0:1], stat[:, 18 + t:19 + t],
                                      ALU.subtract, ALU.mult).then_inc(yn_done, 1)

            with dve.Fori(0, HEADS // 2) as i:
                step.enter(i, 62)
                gn.enter(i, 16)
                for second in range(2):
                    head(2 * i + second, i, second)
            step.leave(2)
            gn.leave(HEADS // 2)
            gate_y(HEADS, HEADS + 1)

            dve.wait_ge(b_full, 34)
            for c in range(2):
                m = pb[:, 2:3, 0:REAL].to_broadcast([P, KC // 2, REAL])
                part = cv[:, c * KC // 2:(c + 1) * KC // 2, :]
                dve.scalar_tensor_tensor(out=part, in0=m, scalar=-1.0 / D, in1=part, op0=ALU.mult,
                                         op1=ALU.add).then_inc(xc_done, 1)
            dve.wait_ge(xc_done, 2)
            dve.memset(stat[:, 22:24], 0.0).then_inc(b_free, 2)
            dve.wait_ge(b_full, 36)
            diag = ident[:, :].rearrange("p (o n) -> p o n", o=1).to_broadcast([P, TT, P])
            dve.tensor_tensor(lnd, pb[:, 2, 0:REAL].rearrange("p (t n) -> p t n", t=TT), diag, ALU.mult).then_inc(b_free, 2)
            dve.wait_ge(b_free, 38)
            dve.tensor_reduce(stat[:, 16:18], lnd, AX_X, ALU.add).then_inc(lnv_done, 1)
            dve.wait_ge(lnv_done, 1)
            dve.tensor_scalar(stat[:, 16:18], stat[:, 16:18], 1.0 / D, EPS, ALU.mult, ALU.add).then_inc(lnv_done, 1)
            dve.wait_ge(lnp_done, 1)
            dve.tensor_tensor(lnd, stat[:, 18:20].rearrange("p (t o) -> p t o", o=1).to_broadcast([P, TT, P]), diag,
                              ALU.mult).then_inc(lnd_done, 1)
            dve.wait_ge(b_full, 38)
            for c in range(2):
                part = cv[:, c * KC // 2:(c + 1) * KC // 2, :]
                dve.tensor_tensor(part, part, pb[:, 2:3, 0:REAL].to_broadcast([P, KC // 2, REAL]), ALU.mult).then_inc(lnx_done, 1)
            dve.wait_ge(lnx_done, 2)
            dve.memset(stat[:, 22:24], 0.0).then_inc(b_free, 2)
            m_low(GATES[0][0], 0, 2 * M_GATES + 1)
            dve.wait_ge(a_free, 42)
            for g in range(UC):
                if g < UC - 1:
                    m_low(GATES[g + 1][0], 0, 2 * (M_GATES + 2 * g + 2) + 1)
                for j in range(2):
                    dve.wait_ge(b_free, 2 * g + (41 + j))
                    o = yret[:, 2 * g + j, :]
                    dve.tensor_tensor(o, o, sgb[:, 2 * g + j, :], ALU.mult).then_inc(gb_done, 1)
            dve.wait_ge(a_free, 50)
            dve.wait_ge(gb_done, KC)
            with dve.Fori(0, 2) as i:
                for q in range(4):
                    full, free, base = ((a_full, a_free, 49), (b_full, b_free, 47))[q // 2]
                    c = bass.ds(4 * i + q, 1)
                    dve.wait_ge(full, 2 * i + (base + q % 2))
                    dve.scalar_tensor_tensor(out=sga[:, c, :], in0=pb[:, q:q + 1, 0:REAL],
                                             scalar=par[:, bass.ds(4 * i + (BCO + q), 1)], in1=sga[:, c, :],
                                             op0=ALU.add, op1=ALU.mult).then_inc(free, 1)
                    dve.wait_ge(free, 2 * i + (base + 2 + q % 2))
                    dve.tensor_tensor(yret[:, c, :], yret[:, c, :], sga[:, c, :], ALU.add).then_inc(merged, 1)
            for n in range(UC):
                dve.wait_ge((a_full, b_full)[n // 2], (53, 51)[n // 2] + n % 2)
                o = hx[:, :, n * UNIT:(n + 1) * UNIT]
                dve.tensor_tensor(o, o, pb[:, n, :].rearrange("p (t n) -> p t n", t=TT), ALU.add).then_inc(h2_done, 1)
            dve.wait_ge(nwb_in, 32)
            for t in range(TT):
                variance(t, P, 4 + t)
            for t in range(TT):
                dve.wait_ge(pow_done, 4 + t)
                dve.scalar_tensor_tensor(out=xn2[:, t, :], in0=hx[:, t, :], scalar=stat[:, 6 + t:7 + t],
                                         in1=nwb[:, 0, :], op0=ALU.mult, op1=ALU.mult).then_inc(xn_done, 1)

            dve.wait_ge(x3_rdy, 2)
            dve.tensor_tensor(xres[:, :, :], xn2[:, :, :], x3[:, 0, :, :], ALU.subtract).then_inc(xr_rdy, 1)

            rt = Chain(dve, route_step)

            def do(ins):
                rt.did(ins)
                rt.wait()

            hot4 = pick[:, 0:TT * TOPK * NE].rearrange("p (t k e) -> p t k e", t=TT, k=TOPK)
            dve.wait_ge(rout_in, 32)
            for t in range(TT):
                dve.wait_ge(lgt, t + 1)
                dve.tensor_tensor(lg[:, t, :], pb[:, 4 + t, 0:NE], brb[:, :], ALU.add).then_inc(lgt_read, 1)
                dve.wait_ge(lgt_read, t + 1)
                do(dve.max(top[:, t, :], lg[:, t, :]))
                dve.tensor_scalar(gate4[:, t, :], top[:, t, 0:TOPK], top[:, t, 0:1], None,
                                  ALU.subtract).then_inc(shift_done, 1)
                do(dve.max_index(topi[:, t, :], top[:, t, :], lg[:, t, :]))
                do(dve.tensor_copy(topf[:, t, :], topi[:, t, 0:TOPK]))
                do(dve.tensor_tensor(hot4[:, t], iota_e[:, :].rearrange("p (o e) -> p o e", o=1).to_broadcast([P, TOPK, NE]),
                                     topf[:, t, :].rearrange("p (k o) -> p k o", o=1).to_broadcast([P, TOPK, NE]),
                                     ALU.is_equal))
                dve.tensor_reduce(mask[:, t, :], hot4[:, t].rearrange("p k e -> p e k"), AX_X, ALU.add).then_inc(route, 1)
            dve.wait_ge(rank_done, 1)
            cnt = pb[:, 6, 2 * NE:3 * NE]
            do(dve.tensor_scalar(nblk[:, :], cnt, float(SLOTS), 1.0, ALU.is_gt, ALU.add))
            for q in (2, 3):
                do(dve.scalar_tensor_tensor(out=nblk[:, :], in0=cnt, scalar=float(q * SLOTS), in1=nblk[:, :],
                                            op0=ALU.is_gt, op1=ALU.add))
            do(dve.tensor_tensor_scan(pend[:, :], ones[:, 0:NE], nblk[:, :], 0.0, ALU.mult, ALU.add))
            do(dve.tensor_tensor(nblk[:, :], pend[:, :], nblk[:, :], ALU.subtract))
            do(dve.tensor_scalar(nblk[:, :], nblk[:, :], float(SLOTS), 1.0, ALU.mult, ALU.add))
            starts = nblk[:, :].rearrange("p (o e) -> p o e", o=1).to_broadcast([P, TT, NE])
            do(dve.tensor_tensor(slot[:, :, :], pb[:, 6, 0:TT * NE].rearrange("p (t e) -> p t e", t=TT), starts, ALU.add))
            do(dve.tensor_tensor(slot[:, :, :], slot[:, :, :], mask[:, :, :], ALU.mult))
            do(dve.tensor_scalar(slot[:, :, :], slot[:, :, :], -1.0, None, ALU.add))
            for t in range(TT):
                dve.tensor_scalar(onehot[:, t, :], iota_s[:, :], slot[:, t, 0:1], None, ALU.is_equal).then_inc(hot_rdy, 1)
            half = MAXB // 2
            c3 = pick[:, TT * TOPK * NE:TT * TOPK * NE + half * NE].rearrange("p (b e) -> p b e", e=NE)
            for q in range(2):
                do(dve.tensor_tensor(c3, pend[:, :].rearrange("p (o e) -> p o e", o=1).to_broadcast([P, half, NE]),
                                     iota_b[:, q * half:(q + 1) * half].rearrange("p (b o) -> p b o", o=1)
                                     .to_broadcast([P, half, NE]), ALU.is_le))
                do(dve.tensor_reduce(tabf[:, q * half:(q + 1) * half], c3, AX_X, ALU.add))
            do(dve.tensor_scalar(tabf[:, :], tabf[:, :], float(NE - 1), None, ALU.min))
            dve.memset(table[0:1, 0:1], 0).then_inc(table_done, 1)
            dve.tensor_copy(table[0:1, 1:MAXB + 1], tabf[0:1, :]).then_inc(table_done, 1)
            dve.tensor_scalar(nblocks[:, 1:2], pend[0:1, NE - 1:NE], -1.0, None, ALU.add).then_inc(table_done, 1)
            dve.tensor_copy(nblocks[:, 0:1], pend[0:1, NE - 1:NE]).then_inc(table_done, 1)

            def pick_rows(b):
                col = tabf[:, b:b + 1] if isinstance(b, int) else tabf[:, bass.ds(b, 1)]
                dve.tensor_scalar(pick_e[:, :], eid[:, :], col, None, ALU.is_equal).then_inc(sel_rdy, 1)

            def tokens_low(n):
                dve.wait_ge(xhi_rdy, n)
                dve.tensor_tensor(xlo[:, :, :], pb[:, 7, :].rearrange("p (k n) -> p k n", n=SLOTS),
                                  xhi[:, :, :].bitcast(F32), ALU.subtract).then_inc(xlo_rdy, 1)

            dve.memset(gatehot[:, :, :], 0.0).then_inc(gh_rdy, 1)
            dve.memset(act, 0.0).then_inc(act_rdy, 1)
            dve.wait_ge(eid_in, 16)
            pick_rows(0)
            tokens_low(1)
            for t in range(TT):
                dve.wait_ge(exp_done, t + 1)
                do(dve.reciprocal(stat[:, 12 + t:13 + t], stat[:, 10 + t:11 + t]))
                do(dve.tensor_scalar(gate4[:, t, :], gate4[:, t, :], stat[:, 12 + t:13 + t], None, ALU.mult))
                do(dve.tensor_tensor(hot4[:, t], hot4[:, t], gate4[:, t, :].rearrange("p (k o) -> p k o", o=1)
                                     .to_broadcast([P, TOPK, NE]), ALU.mult))
                do(dve.tensor_reduce(gdense[:, t, :], hot4[:, t].rearrange("p k e -> p e k"), AX_X, ALU.add))
            dve.wait_ge(table_done, 4)
            nb = dve.value_load(nblocks[0:1, 0:1], min_val=NE, max_val=MAXB - 1)

            def low(b, k):
                dve.wait_ge(hi_done, 24 * b + (k + 1))
                dve.tensor_tensor(wlo[:, k % HS, :], raw_half(k), whi[:, k % HS, :].bitcast(F32),
                                  ALU.subtract).then_inc(lo_v, 1)

            def last_low(b, k):
                dve.wait_ge(hi_done, 24 * b + (k + 1))
                dve.tensor_tensor(wlo[:, k % HS, LAST], raw_half(k)[:, LAST], whi[:, k % HS, LAST].bitcast(F32),
                                  ALU.subtract).then_inc(lo_v, 1)

            def activate(n, used, half=None):
                dve.wait_ge(w_used, used)
                dve.wait_ge(act_rdy, n)
                dve.tensor_scalar(hg, pb[0:SLOTS, 4, 0:UNIT], LIMIT, None, ALU.min).then_inc(min_rdy, 1)
                dve.tensor_scalar(hu, pb[0:SLOTS, 4, UNIT:2 * UNIT], -LIMIT, LIMIT, ALU.max, ALU.min).then_inc(clip_rdy, 1)
                if half:
                    low(*half)
                    low(half[0], half[1] + 1)
                dve.wait_ge(sig_rdy, n)
                dve.tensor_tensor(sig, sig, hg, ALU.mult).then_inc(prod_rdy, 1)
                dve.wait_ge(clip_rdy, n)
                dve.wait_ge(prod_rdy, n)
                dve.scalar_tensor_tensor(out=act, in0=hu, scalar=1.0, in1=sig, op0=ALU.add,
                                         op1=ALU.mult).then_inc(act_rdy, 1)

            def slots_hot(n):
                dve.wait_ge(gslot_rdy, n)
                dve.tensor_scalar(hotT[:, :], pb[0:SLOTS, 7, 0:REAL], 0.0, None, ALU.is_gt).then_inc(hotT_rdy, 1)

            def act_low(n):
                dve.wait_ge(ahi_rdy, n)
                dve.tensor_tensor(alo[:, :, :], pb[:, 7, 0:2 * SLOTS].rearrange("p (k n) -> p k n", n=SLOTS),
                                  ahi[:, :, :].bitcast(F32), ALU.subtract).then_inc(alo_rdy, 1)

            def out_low(n):
                dve.wait_ge(yhi_rdy, n)
                dve.scalar_tensor_tensor(out=ylo[:, :], in0=pb[0:SLOTS, 5:7, :].rearrange("p a b -> p (a b)"), scalar=gslot,
                                         in1=yhi[:, :].bitcast(F32), op0=ALU.mult, op1=ALU.subtract).then_inc(ylo_rdy, 1)

            with dve.Fori(0, nb) as b:
                e = dve.value_load(table[0:1, bass.ds(b + 1, 1)], min_val=0, max_val=NE - 1)
                e1 = dve.value_load(table[0:1, bass.ds(b + 2, 1)], min_val=0, max_val=NE - 1)
                for q in range(STEPS):
                    k = q * HALVES
                    activate(4 * b + (q + 1), 24 * b + (HS + k - 2), (b, k))
                    if q == 0:
                        slots_hot(b + 1)
                    low(b, k + 2)
                    low(b, k + 3)
                    if q == 1:
                        out_low(b + 1)
                    act_low(4 * b + (q + 1))
                    last_low(b, k + 5)
                    if q == 1:
                        dve.wait_ge(ght_done, b + 1)
                        dve.wait_ge(gh_rdy, 2 * b + 1)
                        for t in range(TT):
                            dve.tensor_scalar(gatehot[:, t, :], iota_s[:, :], slot[:, t, bass.ds(e, 1)],
                                              gdense[:, t, bass.ds(e, 1)], ALU.is_equal, ALU.mult).then_inc(gh_rdy, 1)
                        dve.wait_ge(gh_rdy, 2 * b + 3)
                        dve.wait_ge(hot_rdy, 2 * b + 2)
                        dve.tensor_scalar(iota_s[:, :], iota_s[:, :], float(SLOTS), None, ALU.add).then_inc(slot_step, 1)
                        dve.wait_ge(slot_step, b + 1)
                        dve.wait_ge(gathered, b + 1)
                        for t in range(TT):
                            dve.tensor_scalar(onehot[:, t, :], iota_s[:, :], slot[:, t, bass.ds(e1, 1)], None,
                                              ALU.is_equal).then_inc(hot_rdy, 1)
                    if q == 3:
                        dve.wait_ge(w_used, 24 * b + (HS + 19))
                        pick_rows(b + 1)
                        tokens_low(b + 2)
            activate(4 * nb + 1, 24 * nb + (HS - 2))
            slots_hot(nb + 1)
            act_low(4 * nb + 1)
            dve.wait_ge(hi_done, 24 * nb + 2)
            dve.tensor_tensor(wlo[:, 1, LAST], raw_half(5)[:, LAST], whi[:, 1, LAST].bitcast(F32),
                              ALU.subtract).then_inc(lo_v, 1)
            out_low(nb + 1)
            for t in range(TT):
                variance(t, P, 6 + t)
            for t in range(TT):
                dve.wait_ge(pow_done, 6 + t)
                dve.scalar_tensor_tensor(out=osb[:, t, :], in0=pb[:, 2 * t:2 * t + 2, :].rearrange("p a b -> p (a b)"),
                                         scalar=stat[:, 6 + t:7 + t], in1=nwb[:, 1, :], op0=ALU.mult,
                                         op1=ALU.mult).then_inc(out_rdy, 1)


NAMES = ["x", "meta_tokens", "norm_mix_w", "w_in", "conv_dw_w", "conv_dw_b", "conv_ln_w", "conv_ln_b", "w_conv_out",
         "b_conv_out", "ret_gn_w", "w_ret_out", "w_mix_out", "norm_ffn_w", "w_router", "b_router", "w_gate_up",
         "b_gate_up", "w_down", "b_down", "norm_final_w"]


def shape_tables():
    import numpy as np
    f = np.float32
    inv = (f(10000.0) ** (-np.arange(0, DK, 2, dtype=f) / f(DK))).astype(f)
    ang = (inv[:, None] * np.arange(TALL, dtype=f)[None, :]).astype(f)
    lg = np.log1p(-np.exp2(-5.0 - np.arange(HEADS)))
    n = np.arange(TALL)[None, :] - np.arange(P)[:, None]
    dec = np.where(n[:, None, :] >= 0, np.exp(lg[None, :, None] * np.maximum(n, 0)[:, None, :]), 0.0) * DK ** -0.5
    rows = np.arange(P)
    eid = np.where(rows < 3 * NE, rows % NE, -1).astype(f)[:, None].repeat(SLOTS, 1)
    return {"eid": np.ascontiguousarray(eid), "cos": np.cos(ang).astype(f), "sin": np.sin(ang).astype(f), "decay": np.ascontiguousarray(dec.astype(f))}


def kernel(**inputs):
    import numpy as np
    import concourse.bacc as bacc
    from concourse.bass_utils import run_bass_kernel_spmd as run

    nc = bacc.Bacc("TRN2", target_bir_lowering=False, num_devices=1)
    arrays, aps = {}, {}
    tables = shape_tables()
    for name in NAMES + list(tables):
        arr = np.ascontiguousarray(tables[name] if name in tables else inputs[name])
        arrays[f"in_{name}"] = arr
        aps[name] = nc.dram_tensor(f"in_{name}", arr.shape, mybir.dt.from_np(arr.dtype), kind="ExternalInput").ap()
    out = nc.dram_tensor("out_0", (1, REAL, D), F32, kind="ExternalOutput").ap()
    build_block(nc, aps, out)
    return run(nc, [arrays], core_ids=[0]).results[0]["out_0"]
```
